# Optimizing a Trainium2 kernel written in Bass

```python
import jax, jax.numpy as jnp
from jax import lax
import numpy as np

D_MODEL = 1024
BATCH = 1
SEQ = 512
DEPTH = 1
DEC_BATCH = 8
DEC_SEQ = 4
PAST_LEN = 1024
PAGE_SIZE = 128

HEAD_DIM = 64
FOX_HEADS = 8
DSW_HEADS = 8
FOX_W = FOX_HEADS * HEAD_DIM
DSW_W = DSW_HEADS * HEAD_DIM
DSW_WINDOWS = (128, 512, 2048)
DSW_DILATIONS = (1, 4, 16)
DSW_TAPS = DSW_WINDOWS[0] // DSW_DILATIONS[0] + 1
DSW_MAX_WINDOW = max(DSW_WINDOWS)
FFN_HIDDEN = ((8 * D_MODEL + 3 * 256 - 1) // (3 * 256)) * 256
Q_BLOCK = 128
ROPE_THETA = 10000.0
RMS_EPS = 1e-6
SCALE = HEAD_DIM ** -0.5
FORGET_BIAS_BASE = 2.0
IN_SIZES = (FOX_W, FOX_W, FOX_W, FOX_HEADS, DSW_W, DSW_W, DSW_W, D_MODEL, D_MODEL)
IN_COLS = sum(IN_SIZES)

kernel_name = "fox_dilated_window_hybrid_step"

def rmsnorm(x, g):
    xf = x.astype(jnp.float32)
    y = xf * lax.rsqrt(jnp.mean(xf * xf, axis=-1, keepdims=True) + RMS_EPS)
    return (y * g.astype(jnp.float32)).astype(x.dtype)

def rope(x, pos):
    half = HEAD_DIM // 2
    inv = ROPE_THETA ** (-jnp.arange(half, dtype=jnp.float32) / half)
    ang = pos.astype(jnp.float32)[:, None] * inv[None, :]
    cos = jnp.cos(ang)[None, :, None, :]
    sin = jnp.sin(ang)[None, :, None, :]
    xf = x.astype(jnp.float32)
    x1, x2 = xf[..., :half], xf[..., half:]
    return jnp.concatenate([x1 * cos - x2 * sin, x2 * cos + x1 * sin], axis=-1).astype(x.dtype)

def project(x, pos, norm1_g, w_in, b_f, qn_f, kn_f, qn_d, kn_d):
    B, T, _ = x.shape
    z = rmsnorm(x, norm1_g) @ w_in
    splits = [int(v) for v in np.cumsum(IN_SIZES)[:-1]]
    qf, kf, vf, ff, qd, kd, vd, ga, gb = jnp.split(z, splits, axis=-1)
    qf = rmsnorm(qf.reshape(B, T, FOX_HEADS, HEAD_DIM), qn_f)
    kf = rmsnorm(kf.reshape(B, T, FOX_HEADS, HEAD_DIM), kn_f)
    vf = vf.reshape(B, T, FOX_HEADS, HEAD_DIM)
    logf = jax.nn.log_sigmoid((ff + b_f).astype(jnp.float32))
    qd = rope(rmsnorm(qd.reshape(B, T, DSW_HEADS, HEAD_DIM), qn_d), pos)
    kd = rope(rmsnorm(kd.reshape(B, T, DSW_HEADS, HEAD_DIM), kn_d), pos)
    vd = vd.reshape(B, T, DSW_HEADS, HEAD_DIM)
    return qf, kf, vf, logf, qd, kd, vd, ga, gb

def fox_prompt(q, k, v, logf):
    B, S, H, hd = q.shape
    nb = S // Q_BLOCK
    c = jnp.cumsum(logf, axis=1)
    cT = c.swapaxes(1, 2)
    qb = q.reshape(B, nb, Q_BLOCK, H, hd).swapaxes(0, 1)
    cb = cT.reshape(B, H, nb, Q_BLOCK).transpose(2, 0, 1, 3)
    kpos = jnp.arange(S)

    def block(args):
        i, qi, ci = args
        s = jnp.einsum('bqhd,bkhd->bhqk', qi, k).astype(jnp.float32) * SCALE
        s = s + ci[..., None] - cT[:, :, None, :]
        qpos = i * Q_BLOCK + jnp.arange(Q_BLOCK)
        s = jnp.where(kpos[None, :] <= qpos[:, None], s, -jnp.inf)
        p = jax.nn.softmax(s, axis=-1)
        return jnp.einsum('bhqk,bkhd->bqhd', p.astype(v.dtype), v)

    out = lax.map(block, (jnp.arange(nb), qb, cb))
    return out.swapaxes(0, 1).reshape(B, S, H, hd)

def fox_sample(q, k_new, v_new, lf_new, pool_k, pool_v, pool_lf, page_table):
    DB, T, H, hd = q.shape
    kp = pool_k[page_table].reshape(DB, -1, H, hd)
    vp = pool_v[page_table].reshape(DB, -1, H, hd)
    lp = pool_lf[page_table].reshape(DB, -1, H).astype(jnp.float32)
    P = kp.shape[1]
    k_all = jnp.concatenate([kp, k_new.astype(kp.dtype)], axis=1)
    v_all = jnp.concatenate([vp, v_new.astype(vp.dtype)], axis=1)
    c = jnp.cumsum(jnp.concatenate([lp, lf_new], axis=1), axis=1).swapaxes(1, 2)
    s = jnp.einsum('bqhd,bkhd->bhqk', q, k_all).astype(jnp.float32) * SCALE
    s = s + c[:, :, P:, None] - c[:, :, None, :]
    mask = jnp.arange(P + T)[None, :] <= (P + jnp.arange(T))[:, None]
    s = jnp.where(mask, s, -jnp.inf)
    p = jax.nn.softmax(s, axis=-1)
    return jnp.einsum('bhqk,bkhd->bqhd', p.astype(v_all.dtype), v_all)

def dsw_distances():
    return np.arange(DSW_TAPS)[None, :] * np.array(DSW_DILATIONS)[:, None]

def dilated_attend(q, kb, vb, idx, valid):
    kg = kb[:, idx]
    vg = vb[:, idx]
    s = jnp.einsum('bqhd,bgqnhd->bhgqn', q, kg).astype(jnp.float32) * SCALE
    s = jnp.where(valid[None, None], s, -jnp.inf)
    lse = jax.nn.logsumexp(s, axis=-1, keepdims=True)
    p = jnp.exp(s - lse)
    o = jnp.einsum('bhgqn,bgqnhd->bhgqd', p.astype(vb.dtype), vg)
    w = jax.nn.softmax(lse, axis=2)[..., 0]
    return jnp.einsum('bhgq,bhgqd->bqhd', w.astype(o.dtype), o)

def dsw_prompt(q, k, v):
    B, S, H, hd = q.shape
    nb = S // Q_BLOCK
    dist = dsw_distances()
    r = np.arange(Q_BLOCK)
    idx = jnp.asarray(DSW_MAX_WINDOW + r[None, :, None] - dist[:, None, :], jnp.int32)
    rel = jnp.asarray(r[None, :, None] - dist[:, None, :], jnp.int32)
    pad = ((0, 0), (DSW_MAX_WINDOW, 0), (0, 0), (0, 0))
    kp = jnp.pad(k, pad)
    vp = jnp.pad(v, pad)
    qb = q.reshape(B, nb, Q_BLOCK, H, hd).swapaxes(0, 1)

    def block(args):
        i, qi = args
        start = i * Q_BLOCK
        kband = lax.dynamic_slice_in_dim(kp, start, DSW_MAX_WINDOW + Q_BLOCK, axis=1)
        vband = lax.dynamic_slice_in_dim(vp, start, DSW_MAX_WINDOW + Q_BLOCK, axis=1)
        valid = (start + rel) >= 0
        return dilated_attend(qi, kband, vband, idx, valid)

    out = lax.map(block, (jnp.arange(nb), qb))
    return out.swapaxes(0, 1).reshape(B, S, H, hd)

def dsw_sample(q, k_new, v_new, buf_k, buf_v):
    L = buf_k.shape[1]
    T = q.shape[1]
    kb = jnp.concatenate([buf_k, k_new.astype(buf_k.dtype)], axis=1)
    vb = jnp.concatenate([buf_v, v_new.astype(buf_v.dtype)], axis=1)
    raw = L + np.arange(T)[None, :, None] - dsw_distances()[:, None, :]
    valid = jnp.asarray(raw >= 0)
    idx = jnp.asarray(np.maximum(raw, 0), jnp.int32)
    out = dilated_attend(q, kb, vb, idx, valid)
    return out, kb[:, -L:], vb[:, -L:]

def merge_ffn(x, of, od, ga, gb, w_o_fox, w_o_dsw, w_out, norm2_g, w_gate, w_up, w_down):
    B, T, _ = x.shape
    m = (jax.nn.sigmoid(ga) * (of.reshape(B, T, FOX_W) @ w_o_fox)
         + jax.nn.sigmoid(gb) * (od.reshape(B, T, DSW_W) @ w_o_dsw))
    h = x + m @ w_out
    u = rmsnorm(h, norm2_g)
    return h + (jax.nn.silu(u @ w_gate) * (u @ w_up)) @ w_down

def setup_inputs(seed: int = 0) -> dict:
    key = jax.random.key(seed)
    ks = iter(jax.random.split(key, 32))
    f32 = jnp.float32

    def nrm(shape, scale=1.0):
        return scale * jax.random.normal(next(ks), shape, f32)

    n_pages = PAST_LEN // PAGE_SIZE
    n_phys = (5 * DEC_BATCH * n_pages + 3) // 4
    win = min(DSW_MAX_WINDOW, PAST_LEN)
    inp = {}
    inp["x_prompt"] = nrm((BATCH, SEQ, D_MODEL))
    inp["x_sample"] = nrm((DEC_BATCH, DEC_SEQ, D_MODEL))
    inp["cache_k_fox"] = nrm((DEPTH, n_phys, PAGE_SIZE, FOX_HEADS, HEAD_DIM))
    inp["cache_v_fox"] = nrm((DEPTH, n_phys, PAGE_SIZE, FOX_HEADS, HEAD_DIM))
    inp["cache_logf_fox"] = jax.nn.log_sigmoid(
        FORGET_BIAS_BASE + 2.0 * jax.random.uniform(next(ks), (DEPTH, n_phys, PAGE_SIZE, FOX_HEADS), f32)
        + nrm((DEPTH, n_phys, PAGE_SIZE, FOX_HEADS), 0.5))
    inp["state_k_dsw"] = nrm((DEPTH, DEC_BATCH, win, DSW_HEADS, HEAD_DIM))
    inp["state_v_dsw"] = nrm((DEPTH, DEC_BATCH, win, DSW_HEADS, HEAD_DIM))
    inp["page_table"] = jax.random.permutation(next(ks), n_phys)[:DEC_BATCH * n_pages].reshape(
        DEC_BATCH, n_pages).astype(jnp.int32)
    inp["norm1_g"] = 1.0 + nrm((DEPTH, D_MODEL), 0.02)
    inp["w_in"] = nrm((DEPTH, D_MODEL, IN_COLS), D_MODEL ** -0.5)
    inp["b_f"] = FORGET_BIAS_BASE + 2.0 * jax.random.uniform(next(ks), (DEPTH, FOX_HEADS), f32)
    inp["q_norm_fox"] = 1.0 + nrm((DEPTH, HEAD_DIM), 0.02)
    inp["k_norm_fox"] = 1.0 + nrm((DEPTH, HEAD_DIM), 0.02)
    inp["q_norm_dsw"] = 1.0 + nrm((DEPTH, HEAD_DIM), 0.02)
    inp["k_norm_dsw"] = 1.0 + nrm((DEPTH, HEAD_DIM), 0.02)
    inp["w_o_fox"] = nrm((DEPTH, FOX_W, D_MODEL), FOX_W ** -0.5)
    inp["w_o_dsw"] = nrm((DEPTH, DSW_W, D_MODEL), DSW_W ** -0.5)
    inp["w_out"] = nrm((DEPTH, D_MODEL, D_MODEL), D_MODEL ** -0.5)
    inp["norm2_g"] = 1.0 + nrm((DEPTH, D_MODEL), 0.02)
    inp["w_gate"] = nrm((DEPTH, D_MODEL, FFN_HIDDEN), D_MODEL ** -0.5)
    inp["w_up"] = nrm((DEPTH, D_MODEL, FFN_HIDDEN), D_MODEL ** -0.5)
    inp["w_down"] = nrm((DEPTH, FFN_HIDDEN, D_MODEL), FFN_HIDDEN ** -0.5)
    return inp

def reference(x_prompt, x_sample, cache_k_fox, cache_v_fox, cache_logf_fox, state_k_dsw, state_v_dsw,
              page_table, norm1_g, w_in, b_f, q_norm_fox, k_norm_fox, q_norm_dsw, k_norm_dsw,
              w_o_fox, w_o_dsw, w_out, norm2_g, w_gate, w_up, w_down):
    S = x_prompt.shape[1]
    T = x_sample.shape[1]
    P = page_table.shape[1] * cache_k_fox.shape[2]
    Lp = min(DSW_MAX_WINDOW, S)
    pos_p = jnp.arange(S)
    pos_s = P + jnp.arange(T)
    hp, hs = x_prompt, x_sample
    kfp, vfp, lfp, kdp, vdp = [], [], [], [], []
    kfs, vfs, lfs, kds, vds = [], [], [], [], []
    for l in range(DEPTH):
        pw = (norm1_g[l], w_in[l], b_f[l], q_norm_fox[l], k_norm_fox[l], q_norm_dsw[l], k_norm_dsw[l])
        ow = (w_o_fox[l], w_o_dsw[l], w_out[l], norm2_g[l], w_gate[l], w_up[l], w_down[l])
        qf, kf, vf, lf, qd, kd, vd, ga, gb = project(hp, pos_p, *pw)
        of = fox_prompt(qf, kf, vf, lf)
        od = dsw_prompt(qd, kd, vd)
        kfp.append(kf); vfp.append(vf); lfp.append(lf)
        kdp.append(kd[:, S - Lp:]); vdp.append(vd[:, S - Lp:])
        hp = merge_ffn(hp, of, od, ga, gb, *ow)
        qf, kf, vf, lf, qd, kd, vd, ga, gb = project(hs, pos_s, *pw)
        of = fox_sample(qf, kf, vf, lf, cache_k_fox[l], cache_v_fox[l], cache_logf_fox[l], page_table)
        od, nbk, nbv = dsw_sample(qd, kd, vd, state_k_dsw[l], state_v_dsw[l])
        kfs.append(kf); vfs.append(vf); lfs.append(lf)
        kds.append(nbk); vds.append(nbv)
        hs = merge_ffn(hs, of, od, ga, gb, *ow)
    return (hp, hs,
            jnp.stack(kfp), jnp.stack(vfp), jnp.stack(lfp), jnp.stack(kdp), jnp.stack(vdp),
            jnp.stack(kfs), jnp.stack(vfs), jnp.stack(lfs), jnp.stack(kds), jnp.stack(vds))


_drawn_inputs = setup_inputs


def setup_inputs(seed=0):
    import zlib

    import numpy as np

    out = dict(_drawn_inputs(seed))
    spreads = {}
    factors = {'cache_logf_fox': 3.939,
     'norm1_g': 2.825,
     'q_norm_fox': 8.0,
     'k_norm_fox': 2.821,
     'q_norm_dsw': 8.0,
     'k_norm_dsw': 3.01,
     'norm2_g': 3.91}
    for name, (base, spread) in spreads.items():
        noise = np.random.default_rng([zlib.crc32(name.encode()), seed]).standard_normal(out[name].shape)
        drawn = base * np.exp(spread * noise) if base else spread * noise
        out[name] = __import__('jax').numpy.asarray(drawn.astype(out[name].dtype))
    for name, factor in factors.items():
        out[name] = (out[name] * factor).astype(out[name].dtype)
    return out
```

```python
import concourse.bass as bass
from concourse import mybir
from contextlib import ExitStack

D, TP, DB, DS = 1024, 512, 8, 4
TS = DB * DS
T = TP + TS
HALF = T // 2
KT = D // 128
HD, H = 64, 8
W = H * HD
NPAIR = W // 128
FFN, KF = 2816, 22
PAST, PAGE = 1024, 128
NPG = PAST // PAGE
EPS = 1e-6
NEG = -1e30
PT_ = [128, 128, 128, 128, TS]
FOX, DSW = 0, 1
NCH = [NPG + 1, 6]
COL_F, COL_G = 3 * W, 3 * W + H + 3 * W
BLOCKS = [W, 0, 3 * W + H + W, 3 * W + H, 2 * W, 3 * W + H + 2 * W]

C_ID, C_MEAN, C_ONE, C_TRI, C_NTRI, C_LC, C_COS, C_SIN, C_DM, C_FM, C_EPS = 0, 128, 256, 384, 512, 1408, 1920, 2240, 2560, 2584, 2588
C_END = 2589


def program(nc, x_prompt, x_sample, cache_k, cache_v, cache_lf, state_k, state_v, page_table, norm1_g, w_in, b_f,
            qn_f, kn_f, qn_d, kn_d, w_o_fox, w_o_dsw, w_out, norm2_g, w_gate, w_up, w_down, cpack, selin,
            y_p, y_s, kf_p, vf_p, lf_p, kd_p, vd_p, kf_s, vf_s, lf_s, kd_s, vd_s):
    f32, i32 = mybir.dt.float32, mybir.dt.int32
    ALU, ACT, AX = mybir.AluOpType, mybir.ActivationFunctionType, mybir.AxisListType
    ds = bass.ds
    ctx = ExitStack()
    with ctx:
        ctx.enter_context(nc.allow_non_contiguous_dma(reason="small parameter vectors"))
        names = set()

        def sem(name):
            return ctx.enter_context(nc.semaphore(name))

        ARENA = 52600
        arena = ctx.enter_context(nc.sbuf_tensor("arena", [128, ARENA], f32))
        cur = [0]

        def put(shape, at=None, part=128):
            n = 1
            for s in shape:
                n *= s
            if at is None:
                at = cur[0]
                cur[0] += n
            assert at + n <= ARENA, (at, n)
            v = arena[0:part, at:at + n]
            if len(shape) == 1:
                return v
            nm = "abcdef"[:len(shape)]
            return v.rearrange(f"p ({' '.join(nm)}) -> p {' '.join(nm)}", **{a: s for a, s in zip(nm, shape)})

        cp = put([C_END + 3])
        ident = cp[:, C_ID:C_ID + 128]
        mean1 = cp[:, C_MEAN:C_MEAN + 128]
        ones = cp[:, C_ONE:C_ONE + 128]
        tri = cp[:, C_TRI:C_TRI + 128]
        ntri = cp[:, C_NTRI:C_NTRI + 896]
        logc = cp[:, C_LC:C_LC + 512]
        cosr = cp[:, C_COS:C_COS + 320].rearrange("p (t d) -> p t d", d=64)
        sinr = cp[:, C_SIN:C_SIN + 320].rearrange("p (t d) -> p t d", d=64)
        dmask = cp[:, C_DM:C_DM + 24].rearrange("p (c q) -> p c q", q=4)
        fmask = cp[:, C_FM:C_FM + 4]
        eps = cp[:, C_EPS:C_EPS + 1]
        sel = put([H, 128], part=8)
        gains = put([4, HD])
        g1 = put([KT])
        g2 = put([KT])
        bf = put([H])
        ptab = put([64]).bitcast(i32)
        rstd = put([T])
        ssum = put([4, 5, H])
        lfx = put([5, H])
        lfe = put([5, H])
        lfa = put([5, H])
        negcT = put([TP], part=8)
        Qs = put([2, DB, NPAIR, 2, DS])
        mx = put([4, 1])
        mx2 = put([4, 1])
        negm = put([4, 1])
        rs = put([4, 1])
        rinv = put([4, 1])
        xT = put([KT, T])
        xnT = put([KT, T])
        Z = cur[0]
        WQ = put([2, KT, W], Z)
        rows = put([4, 5, W], Z + 8192)
        vrows = put([5, 2 * W], Z + 18432)
        qkT = put([16, T], Z + 23552)
        q0 = Z + 32256
        sq = put([2, T], q0)
        rt = put([2, W], q0 + 1088)
        wf = put([KT, H], q0 + 2112)
        xrow = put([5, D], Z + 23552)
        AT = put([2, NPAIR, T], Z)
        negc = put([H, TP], Z + 8192)
        ndiag = put([H, 4, 128], Z + 12288)
        PP = put([2, TP], Z + 4352)
        PTs = put([2, TP], Z + 5376)
        Arow = put([2, 128], Z + 6400)
        WG = put([2, KT, 128], Z + 4352)
        zg = put([16, T], Z + 6400)
        Kf = put([NCH[0], W], Z + 15104)
        Vf = put([NCH[0], W], Z + 19712)
        Kd = put([NCH[1], W], Z + 24320)
        Vd = put([NCH[1], W], Z + 27392)
        lfp = put([NCH[0], H], Z + 30464)
        cneg = put([NCH[0], H], Z + 30536)
        KTs = put([2, W], Z + 30608)
        S1 = [put([NCH[0], 32], Z + 31632), put([NCH[1], 32], Z + 31920)]
        mp = [put([32], Z + 32112 + 32 * k) for k in range(2)]
        mcol = [put([1], Z + 32176 + k) for k in range(2)]
        dg = [put([32], Z + 32178 + 32 * k) for k in range(2)]
        ps_ = [put([32], Z + 32242 + 32 * k) for k in range(2)]
        ri = [put([32], Z + 32306 + 32 * k) for k in range(2)]
        WO = put([4, 2, NPAIR, 128], Z + 32400)
        tg = put([2, T], Z + 15104)
        WX = put([4, KT, 128], Z + 16192)
        mT = xnT
        sq2 = put([2, T], Z + 20288)
        std2 = put([T], Z + 21376)
        hid = put([KF, T], Z)
        WU = put([4, KT, 2, 128], Z + 21920)
        WD = put([2, KF, 128], Z + 30112)
        sg = put([2, T], Z + 11968)
        yT = put([2, T], Z + 13056)
        yst = put([2, 5, 128], Z + 14144)
        bank = [ctx.enter_context(nc.psum_tensor(f"bank{i}", [128, 512], f32)) for i in range(8)]

        xp_v = x_prompt[0].rearrange("(t p) n -> p t n", p=128)
        xs_v = x_sample.rearrange("b s n -> (b s) n")
        win_v = w_in[0].rearrange("(k p) n -> p k n", p=128)
        lay = lambda a: a.rearrange("l b s h d -> (l b) s (h d)")
        kfp_v, vfp_v, kdp_v, vdp_v = [lay(a)[0].rearrange("(t p) n -> p t n", p=128) for a in (kf_p, vf_p, kd_p, vd_p)]
        kfs_v, vfs_v, kds_v, vds_v = [lay(a) for a in (kf_s, vf_s, kd_s, vd_s)]
        sk_v, sv_v = lay(state_k), lay(state_v)
        ck_v, cv_v = [a.rearrange("l n g h d -> (l n) g (h d)") for a in (cache_k, cache_v)]
        cl_v = cache_lf[0]
        lfs_v = lf_s[0]
        wof_v = [w[0].rearrange("(k p) n -> p k n", p=128) for w in (w_o_fox, w_o_dsw)]
        wx_v = w_out[0].rearrange("(k p) n -> p k n", p=128)
        wg_v = [w[0].rearrange("(k p) n -> p k n", p=128) for w in (w_gate, w_up)]
        wd_v = w_down[0].rearrange("(k p) n -> p k n", p=128)
        yp_v = y_p[0].rearrange("(t p) n -> p t n", p=128)
        ys_v = y_s.rearrange("b s n -> (b s) n")
        n_phys = ck_v.shape[0]

        c_in, x_in, f_in = sem("consts_in"), sem("x_in"), sem("wf_in")
        xT_ps, xT_sb = sem("xT_in_psum"), sem("xT_ready")
        sq_ok, sq_used, std_ok, rstd_ok, xn_ok = [sem("n1_" + s) for s in ("squared", "summed", "std", "rstd", "xn_ready")]
        sq2_ok, sq2_used, std2_ok, rstd2_ok, u_ok = [sem("n2_" + s) for s in ("squared", "summed", "std", "rstd", "u_ready")]
        z_init = sem("zeroed")
        f_ps, lfx_ok, lfe_ok, lf_ok = sem("f_in_psum"), sem("f_biased"), sem("f_act"), sem("logf_ready")
        wq_in = [sem(f"wqkv_in{s}") for s in range(2)]
        wq_used = sem("wqkv_used")
        z_ps, z_used = sem("z_in_psum"), sem("z_copied")
        zs_ok, zs_sum, zs_std, zs_inv, row_s, row_ok = [sem("row_" + s) for s in ("squared", "summed", "std", "inverse", "step", "done")]
        tr_ps, tr_a, tr_v = sem("qkT_in_psum"), sem("qkT_copied_act"), sem("qkT_copied_dve")
        st_k = sem("rows_stored")
        st_lf = sem("logf_stored")
        sts = sem("sample_rows_stored")
        cT_ps, cT_sb, cb_ps, cb_sb, nd_ok = sem("cT_in_psum"), sem("cT_ready"), sem("c_in_psum"), sem("negc_ready"), sem("ndiag_ready")
        Qs_ok = sem("Qs_ready")
        s_ps, s_mx, s_nm, p_ok, pt_ps, pt_a, pt_v, o_ps, r_ok, a_ok, at_ps, at_ok = [sem("pa_" + s) for s in (
            "scores", "max_step", "negmax", "probs", "probsT_psum", "probsT_act", "probsT_dve", "out_psum", "recip",
            "out_rows", "outT_psum", "outT_ready")]
        kf_in, vf_in, l_in, kd_in, vd_in = [sem(s) for s in ("kfox_in", "vfox_in", "lfox_in", "kdsw_in", "vdsw_in")]
        wg_in = [sem(f"wg_in{s}") for s in range(2)]
        wg_used, g_ps, g_ok = sem("wg_used"), sem("gate_in_psum"), sem("gate_copied")
        cc_ps, cc_ok = sem("sc_in_psum"), sem("sc_ready")
        kt_ps, kt_a, kt_v, ktq = sem("skT_psum"), sem("skT_act"), sem("skT_dve"), sem("skT_used")
        ss = [{n: sem(f"s{k}_{n}") for n in ("sc", "s1", "mp", "mt", "m", "dg", "mb", "sub", "p", "sum", "out", "ri", "at")} for k in range(2)]
        cpy = sem("state_copied")
        wo_in = [sem(f"wo_in{s}") for s in range(4)]
        wo_used, sg_ok, o_done, tg_ok, m_ok = sem("wo_used"), sem("gates_sigmoid"), sem("wo_out"), sem("merge_step"), sem("m_ready")
        wx_in = [sem(f"wx_in{s}") for s in range(4)]
        wx_ps, h_ok = sem("wout_out"), sem("h_ready")
        wu_in = [sem(f"wu_in{s}") for s in range(4)]
        u_ps, sil_ok, gm_ok, hid_ok = sem("ffn_up_out"), sem("ffn_sigmoid"), sem("ffn_gate_mul"), sem("hidden_ready")
        wd_in = [sem(f"wd_in{s}") for s in range(2)]
        d_ps, y_ok, yt_ps, yst_ok = sem("down_out"), sem("yT_ready"), sem("y_in_psum"), sem("y_rows_ready")
        y_st = [sem(f"y_stored{s}") for s in range(2)]
        N_CONST = 10

        block = ctx.enter_context(nc.Block())

        @block.sync
        def _(sp):
            sp.dma_start(cp[:, 0:C_END], cpack).then_inc(c_in, 16)
            sp.dma_start(xrow[:, 0:4, :], xp_v).then_inc(x_in, 16)
            sp.dma_start(xrow[0:TS, 4, :], xs_v).then_inc(x_in, 16)
            sp.dma_start(sel[0:8], selin.rearrange("h (a c) -> h a c", c=128)).then_inc(c_in, 16)
            sp.dma_start(g1, norm1_g[0].rearrange("(k p) -> p k", p=128)).then_inc(c_in, 16)
            sp.dma_start(g2, norm2_g[0].rearrange("(k p) -> p k", p=128)).then_inc(c_in, 16)
            for n, g in enumerate((kn_f, qn_f, kn_d, qn_d)):
                sp.dma_start(gains[:, n, :], g[0:1, :].to_broadcast([128, HD])).then_inc(c_in, 16)
            sp.dma_start(bf, b_f[0:1, :].to_broadcast([128, H])).then_inc(c_in, 16)
            sp.dma_start(ptab[0:1, :], page_table.rearrange("b n -> (b n)").rearrange("(a n) -> a n", a=1)).then_inc(c_in, 16)
            sp.dma_start(wf, win_v[:, :, COL_F:COL_F + H]).then_inc(f_in, 16)
            def shift(b):
                sp.dma_start(kds_v[b, 0:PAST - DS], sk_v[b, DS:PAST]).then_inc(cpy, 16)
                sp.dma_start(vds_v[b, 0:PAST - DS], sv_v[b, DS:PAST]).then_inc(cpy, 16)
            for n, col in enumerate(BLOCKS):
                if n >= 2:
                    sp.wait_ge(wq_used, n - 1)
                sp.dma_start(WQ[:, n % 2], win_v[:, :, col:col + W]).then_inc(wq_in[n % 2], 16)
                if n >= 1:
                    shift(n - 1)
            sp.wait_ge(sts, 16 * 5)
            sp.wait_ge(at_ok, 32)
            sp.wait_ge(z_init, 8)

            def pages(b, first):
                page = [sp.value_load(ptab[0:1, ds(b * NPG + n, 1)], min_val=0, max_val=n_phys - 1) for n in range(NPG)]
                if not first:
                    sp.wait_ge(kt_ps, b * 15 - 6)
                for n in range(NPG):
                    sp.dma_start(Kf[:, n, :], ck_v[ds(page[n], 1)].rearrange("a g n -> (a g) n")).then_inc(kf_in, 16)
                sp.dma_start(Kf[0:DS, NPG, :], kfs_v[ds(b, 1)].rearrange("a g n -> (a g) n")).then_inc(kf_in, 16)
                if not first:
                    sp.wait_ge(wg_used, 2 * b - 1)
                sp.dma_start(WG[:, 0], win_v[:, :, ds(COL_G + b * 256, 128)]).then_inc(wg_in[0], 16)
                if not first:
                    sp.wait_ge(cc_ps, b)
                for n in range(NPG):
                    sp.dma_start(lfp[:, n, :], cl_v[ds(page[n], 1)].rearrange("a g n -> (a g) n")).then_inc(l_in, 16)
                sp.dma_start(lfp[0:DS, NPG, :], lfs_v[ds(b, 1)].rearrange("a g n -> (a g) n")).then_inc(l_in, 16)
                if not first:
                    sp.wait_ge(kt_ps, b * 15)
                for n in range(4):
                    sp.dma_start(Kd[:, n, :], sk_v[ds(b, 1), 512 + 128 * n:640 + 128 * n].rearrange("a g n -> (a g) n")).then_inc(kd_in, 16)
                sp.dma_start(Kd[:, 4, :], sk_v[ds(b, 1), 0:512].rearrange("a (g r) n -> (a g) r n", r=16)[:, 0:4, :]).then_inc(kd_in, 16)
                sp.dma_start(Kd[0:DS, 5, :], kds_v[ds(b, 1), PAST - DS:PAST].rearrange("a g n -> (a g) n")).then_inc(kd_in, 16)
                if not first:
                    sp.wait_ge(ss[0]["out"], b)
                for n in range(NPG):
                    sp.dma_start(Vf[:, n, :], cv_v[ds(page[n], 1)].rearrange("a g n -> (a g) n")).then_inc(vf_in, 16)
                sp.dma_start(Vf[0:DS, NPG, :], vfs_v[ds(b, 1)].rearrange("a g n -> (a g) n")).then_inc(vf_in, 16)
                if not first:
                    sp.wait_ge(wg_used, 2 * b)
                sp.dma_start(WG[:, 1], win_v[:, :, ds(COL_G + b * 256 + 128, 128)]).then_inc(wg_in[1], 16)
                if not first:
                    sp.wait_ge(ss[1]["out"], b)
                for n in range(4):
                    sp.dma_start(Vd[:, n, :], sv_v[ds(b, 1), 512 + 128 * n:640 + 128 * n].rearrange("a g n -> (a g) n")).then_inc(vd_in, 16)
                sp.dma_start(Vd[:, 4, :], sv_v[ds(b, 1), 0:512].rearrange("a (g r) n -> (a g) r n", r=16)[:, 0:4, :]).then_inc(vd_in, 16)
                sp.dma_start(Vd[0:DS, 5, :], vds_v[ds(b, 1), PAST - DS:PAST].rearrange("a g n -> (a g) n")).then_inc(vd_in, 16)

            pages(0, True)
            with sp.Fori(1, DB) as b:
                pages(b, False)

            def load_wo(m, s):
                for k in range(2):
                    sp.dma_start(WO[:, s, k], wof_v[k][:, :, ds(m * 128, 128)]).then_inc(wo_in[s], 16)
            for m in range(4):
                load_wo(m, m)
            sp.wait_ge(kt_ps, DB * 15)
            sp.wait_ge(ss[0]["at"], 2 * DB)
            sp.wait_ge(ss[1]["at"], 2 * DB)
            def load_wx(m, s):
                sp.dma_start(WX[:, s], wx_v[:, :, ds(m * 128, 128)]).then_inc(wx_in[s], 16)
            for m in range(4):
                load_wx(m, m)
            for m in range(4, 8):
                sp.wait_ge(wo_used, m - 3)
                load_wo(m, m - 4)
            def load_wu(m, s):
                for k in range(2):
                    sp.dma_start(WU[:, s, :, k, :], wg_v[k][:, :, ds(m * 128, 128)]).then_inc(wu_in[s], 16)
            for m in range(4):
                load_wu(m, m)
            for m in range(4, 8):
                sp.wait_ge(wx_ps, m - 3)
                load_wx(m, m - 4)
            sp.wait_ge(wo_used, 8)
            def load_wd(m, s):
                sp.dma_start(WD[:, s], wd_v[:, :, ds(m * 128, 128)]).then_inc(wd_in[s], 16)
            for m in range(2):
                load_wd(m, m)
            with sp.Fori(1, 5) as i:
                for s in range(4):
                    sp.wait_ge(u_ps, 4 * i + s - 3)
                    load_wu(4 * i + s, s)
            for s in range(2):
                sp.wait_ge(u_ps, 17 + s)
                load_wu(20 + s, s)
            for b in range(5, DB):
                shift(b)
            with sp.Fori(1, 4) as i:
                for s in range(2):
                    sp.wait_ge(d_ps, 2 * i + s - 1)
                    load_wd(2 * i + s, s)
            sp.wait_ge(cpy, 16 * 2 * DB)
            sp.wait_ge(st_k, 16 * 4)
            sp.wait_ge(st_lf, 16)
            sp.wait_ge(sts, 16 * 5)

        @block.gpsimd
        def _(pool):
            nc.gpsimd.memset(Qs, 0.0).then_inc(z_init, 1)
            nc.gpsimd.memset(lfx, 0.0).then_inc(z_init, 1)
            nc.gpsimd.memset(ssum, 1.0).then_inc(z_init, 1)
            pool.wait_ge(lf_ok, 3)
            pool.dma_start(lf_p[0, 0].rearrange("(t p) h -> p t h", p=128), lfx[:, 0:4, :]).then_inc(st_lf, 16)
            pool.dma_start(lfs_v.rearrange("b s h -> (b s) h"), lfx[0:TS, 4, :]).then_inc(sts, 16)
            for blk, out_p, out_s in ((0, kfp_v, kfs_v), (2, kdp_v, kds_v)):
                pool.wait_ge(row_ok, 5 * blk + 5)
                pool.dma_start(out_p, rows[:, blk, 0:4, :]).then_inc(st_k, 16)
                if blk == 0:
                    pool.dma_start(out_s.rearrange("b s n -> (b s) n"), rows[0:TS, blk, 4, :]).then_inc(sts, 16)
                else:
                    pool.dma_start(out_s[:, PAST - DS:PAST, :], rows[0:TS, blk, 4, :]).then_inc(sts, 16)
            for k, out_p, out_s in ((0, vfp_v, vfs_v), (1, vdp_v, vds_v)):
                pool.wait_ge(z_used, 5 * (4 + k) + 5)
                pool.dma_start(out_p, vrows[:, 0:4, k * W:(k + 1) * W]).then_inc(st_k, 16)
                if k == 0:
                    pool.dma_start(out_s.rearrange("b s n -> (b s) n"), vrows[0:TS, 4, k * W:(k + 1) * W]).then_inc(sts, 16)
                else:
                    pool.dma_start(out_s[:, PAST - DS:PAST, :], vrows[0:TS, 4, k * W:(k + 1) * W]).then_inc(sts, 16)
            pool.wait_ge(tr_a, 8)
            pool.wait_ge(tr_v, 8)
            pool.wait_ge(z_init, 3)
            for k in range(2):
                for j in range(2):
                    nc.gpsimd.tensor_copy(Qs[64 * j:64 * j + 64, k, :, :, j, :],
                                          qkT[64 * j:64 * j + 64, 8 + 4 * k:12 + 4 * k, TP:T].rearrange("p c (b q) -> p b c q", q=DS)).then_inc(Qs_ok, 1)
            pool.wait_ge(Qs_ok, 4)
            for h in range(H):
                pool.wait_ge(cb_sb, h + 1)
                nc.gpsimd.tensor_tensor(ndiag[:, h], negc[:, h].rearrange("p (c n) -> p c n", n=128),
                                        tri.rearrange("p (a n) -> p a n", a=1).to_broadcast([128, 4, 128]), ALU.add).then_inc(nd_ok, 1)
            pool.wait_ge(at_ok, 32)
            for t in (Kf, Vf, lfp):
                nc.gpsimd.memset(t[:, NPG, :], 0.0).then_inc(z_init, 1)
            for t in (Kd, Vd):
                nc.gpsimd.memset(t[:, 5, :], 0.0).then_inc(z_init, 1)

        @block.scalar
        def _(act):
            def squares(ok, used, inn, src, dst):
                for k in range(KT):
                    act.wait_ge(inn, k + 1)
                    if k >= 2:
                        act.wait_ge(used, k - 1)
                    nc.scalar.activation(dst[:, k % 2], src[:, k], ACT.Square).then_inc(ok, 1)

            def stds(used, ok, dst):
                act.wait_ge(used, KT)
                for hf in range(2):
                    nc.scalar.activation(dst[:, hf * HALF:(hf + 1) * HALF], bank[6 + hf][:, 0:HALF], ACT.Sqrt, bias=eps).then_inc(ok, 1)

            act.wait_ge(c_in, 16 * N_CONST)
            squares(sq_ok, sq_used, xT_sb, xT, sq)
            stds(sq_used, std_ok, rstd)
            act.wait_ge(lfx_ok, 3)
            nc.scalar.activation(lfe, lfe, ACT.Exp, scale=-1.0).then_inc(lfe_ok, 1)
            act.wait_ge(lfe_ok, 1)
            nc.scalar.activation(lfe, lfe, ACT.Ln, bias=1.0).then_inc(lfe_ok, 1)

            def rows_block(blk):
                for t in range(5):
                    P = PT_[t]
                    act.wait_ge(z_ps, 5 * blk + t + 1)
                    nc.scalar.copy(rows[0:P, blk, t, :], bank[t][0:P, :]).then_inc(z_used, 1)
                    act.wait_ge(z_used, 5 * blk + t + 1)
                    if 5 * blk + t >= 2:
                        act.wait_ge(zs_sum, 5 * blk + t - 1)
                    nc.scalar.activation(sq[0:P, t % 2, 0:W], rows[0:P, blk, t, :], ACT.Square).then_inc(zs_ok, 1)
                act.wait_ge(zs_sum, 5 * blk + 5)
                nc.scalar.activation(ssum[:, blk], ssum[:, blk], ACT.Sqrt, bias=eps, scale=1.0 / HD).then_inc(zs_std, 1)
            act.wait_ge(z_init, 3)
            for blk in range(4):
                rows_block(blk)
            for k in range(2):
                for t in range(5):
                    P = PT_[t]
                    act.wait_ge(z_ps, 5 * (4 + k) + t + 1)
                    nc.scalar.copy(vrows[0:P, t, k * W:(k + 1) * W], bank[t][0:P, :]).then_inc(z_used, 1)
            act.wait_ge(cT_ps, 1)
            nc.scalar.copy(negcT[0:8], bank[6][0:8, :]).then_inc(cT_sb, 1)
            for u in range(0, 16, 2):
                blk, c = u // 4, u % 4
                dst = qkT[:, 8 * (blk % 2) + 4 * (blk // 2) + c]
                sc = 1.0 if blk % 2 == 0 else HD ** -0.5
                act.wait_ge(tr_ps, u + 1)
                b0 = 2 * (u % 3)
                nc.scalar.activation(dst[:, 0:TP], bank[b0][:, :], ACT.Copy, scale=sc)
                nc.scalar.activation(dst[:, TP:T], bank[b0 + 1][:, 0:TS], ACT.Copy, scale=sc).then_inc(tr_a, 1)
            act.wait_ge(st_k, 16 * 4)
            act.wait_ge(sts, 16 * 5)
            for h in range(H):
                act.wait_ge(cb_ps, h + 1)
                nc.scalar.copy(negc[:, h], bank[6 + h % 2][:, :]).then_inc(cb_sb, 1)

            def outT(p, i):
                n = 4 * p + i
                act.wait_ge(at_ps, n + 1)
                nc.scalar.copy(AT[:, p // 4, p % 4, i * 128:(i + 1) * 128],
                               bank[6 + i % 2][:, 0:128]).then_inc(at_ok, 1)

            def step(p, u, first=False, last=False):
                if not last:
                    i = u // 2
                    N = 128 * (i + 1)
                    act.wait_ge(s_nm, 8 * p + u + 1)
                    nc.scalar.activation(PP[:, u % 2, 0:N], PP[:, u % 2, 0:N], ACT.Exp, bias=negm[:, u % 4],
                                         accum_out=rs[:, u % 4]).then_inc(p_ok, 1)
                if (u - 1) % 2 == 0 and not (first and u < 1):
                    N = 128 * ((u - 1) // 2 + 1)
                    act.wait_ge(pt_ps, 8 * p + u)
                    nc.scalar.copy(PTs[:, 0, 0:N], bank[2][:, 0:N]).then_inc(pt_a, 1)
                if (u - 4) % 2 == 1 and not (first and u < 5):
                    v = (u - 4) % 8
                    outT(p if u >= 4 else p - 1, v // 2)
            for p in range(8):
                for u in range(8):
                    step(p, u, first=p == 0)
            for u in (1, 3):
                outT(7, (u + 4) // 2)
            def kt_even(n0, b, nch):
                for ch in range(0, nch, 2):
                    n = b * 15 + n0 + ch
                    act.wait_ge(kt_ps, n + 1)
                    nc.scalar.copy(KTs[:, 0], bank[0][:, :]).then_inc(kt_a, 1)

            def gate(b, s, hf):
                n = 4 * b + 2 * s + hf
                act.wait_ge(g_ps, n + 1)
                act.wait_ge(c_in, 16)
                nc.scalar.copy(zg[:, ds(2 * b + s, 1), hf * HALF:(hf + 1) * HALF].rearrange("p a n -> p (a n)"),
                               bank[6 + hf][:, 0:HALF]).then_inc(g_ok, 1)

            def probs(b, k):
                act.wait_ge(ss[k]["sub"], b + 1)
                nc.scalar.activation(S1[k], S1[k], ACT.Exp).then_inc(ss[k]["p"], 1)

            def batch(b):
                kt_even(0, b, NCH[0])
                gate(b, 0, 0)
                gate(b, 0, 1)
                kt_even(9, b, NCH[1])
                probs(b, 0)
                gate(b, 1, 0)
                probs(b, 1)
                gate(b, 1, 1)
            batch(0)
            with act.Fori(1, DB) as b:
                batch(b)
            for m in range(8):
                if m == 0:
                    act.wait_ge(g_ok, 4 * DB)
                nc.scalar.activation(zg[:, m:m + 9:8, :], zg[:, m:m + 9:8, :], ACT.Sigmoid).then_inc(sg_ok, 1)
            squares(sq2_ok, sq2_used, h_ok, xT, sq2)
            stds(sq2_used, std2_ok, std2)

            def silu(m, s, warm):
                act.wait_ge(u_ps, m + 1)
                if warm:
                    act.wait_ge(hid_ok, m - 1)
                for hf in range(2):
                    nc.scalar.activation(sg[:, s % 2, hf * HALF:(hf + 1) * HALF], bank[4 * (s % 2) + hf][:, 0:HALF], ACT.Sigmoid).then_inc(sil_ok, 1)
            for s in range(2):
                silu(s, s, False)
            with act.Fori(1, 11) as i:
                for s in range(2):
                    silu(2 * i + s, s, True)

            def yrows(m, s, warm):
                act.wait_ge(yt_ps, m + 1)
                if warm:
                    act.wait_ge(y_st[s], 32 * (m // 2) if isinstance(m, int) else 0)
                nc.scalar.copy(yst[:, s, 0:4, :], bank[4 + 2 * s][:, :].rearrange("p (t n) -> p t n", n=128))
                nc.scalar.copy(yst[0:TS, s, 4, :], bank[5 + 2 * s][0:TS, 0:128]).then_inc(yst_ok, 1)
                act.wait_ge(yst_ok, m + 1)
                act.dma_start(yp_v[:, :, ds(m * 128, 128)], yst[:, s, 0:4, :]).then_inc(y_st[s], 16)
                act.dma_start(ys_v[:, ds(m * 128, 128)], yst[0:TS, s, 4, :]).then_inc(y_st[s], 16)
            for m in range(8):
                yrows(m, m % 2, m >= 2)
            for s in range(2):
                act.wait_ge(y_st[s], 32 * 4)

        @block.vector
        def _(dve):
            V = nc.vector
            for k in range(KT):
                dve.wait_ge(xT_ps, k + 1)
                V.tensor_copy(xT[:, k, 0:TP], bank[2 * (k % 2)][:, :])
                V.tensor_copy(xT[:, k, TP:T], bank[2 * (k % 2) + 1][:, 0:TS]).then_inc(xT_sb, 1)

            def scaled(std, rok, ok, g, src, dst, sdt):
                dve.wait_ge(std, 2)
                V.reciprocal(sdt, sdt).then_inc(rok, 1)
                dve.wait_ge(rok, 1)
                for k in range(KT):
                    V.scalar_tensor_tensor(dst[:, k], src[:, k], g[:, k:k + 1], sdt, ALU.mult, ALU.mult).then_inc(ok, 1)
            dve.wait_ge(xT_sb, KT)
            dve.wait_ge(c_in, 16 * N_CONST)
            scaled(std_ok, rstd_ok, xn_ok, g1, xT, xnT, rstd)
            dve.wait_ge(f_ps, 1)
            dve.wait_ge(z_init, 3)
            fp = bank[5][:, 0:40].rearrange("p (t h) -> p t h", h=H)
            bfb = bf.rearrange("p (a h) -> p a h", a=1)
            V.tensor_tensor(lfx[:, 0:4], fp[:, 0:4], bfb.to_broadcast([128, 4, H]), ALU.add).then_inc(lfx_ok, 1)
            V.tensor_tensor(lfx[0:TS, 4], fp[0:TS, 4], bf[0:TS], ALU.add).then_inc(lfx_ok, 1)
            dve.wait_ge(lfx_ok, 2)
            V.scalar_tensor_tensor(lfe, lfx, -1.0, lfx, ALU.mult, ALU.max).then_inc(lfx_ok, 1)
            V.tensor_scalar(lfa, lfx, 0.0, None, ALU.min).then_inc(lf_ok, 1)
            dve.wait_ge(lf_ok, 1)
            dve.wait_ge(lfe_ok, 2)
            V.tensor_tensor(lfx, lfa, lfe, ALU.subtract).then_inc(lf_ok, 2)

            def norm_block(blk, rope, i0):
                for t in range(5):
                    P = PT_[t]
                    dve.wait_ge(zs_ok, 5 * blk + t + 1)
                    V.reduce_sum(ssum[0:P, blk, t, :], sq[0:P, t % 2, 0:W].rearrange("p (h d) -> p h d", d=HD), AX.X).then_inc(zs_sum, 1)
                dve.wait_ge(zs_std, blk + 1)
                V.reciprocal(ssum[:, blk], ssum[:, blk]).then_inc(zs_inv, 1)
                dve.wait_ge(zs_inv, blk + 1)
                n = i0
                for t in range(5):
                    P = PT_[t]
                    r = rows[0:P, blk, t, :].rearrange("p (h d) -> p h d", d=HD)
                    inv = ssum[0:P, blk, t, :].rearrange("p (h e) -> p h e", e=1)
                    g = gains[0:P, blk:blk + 1, :]
                    V.tensor_tensor(r, r, inv.to_broadcast([P, H, HD]), ALU.mult).then_inc(row_s, 1)
                    n = n + 1
                    dve.wait_ge(row_s, n)
                    if not rope:
                        V.tensor_tensor(r, r, g.to_broadcast([P, H, HD]), ALU.mult).then_inc(row_ok, 1)
                        continue
                    V.tensor_tensor(r, r, g.to_broadcast([P, H, HD]), ALU.mult).then_inc(row_s, 1)
                    n = n + 1
                    dve.wait_ge(row_s, n)
                    a, bb = [rt[0:P, e].rearrange("p (h d) -> p h d", d=HD) for e in range(2)]
                    V.tensor_tensor(a, r, cosr[0:P, t:t + 1, :].to_broadcast([P, H, HD]), ALU.mult).then_inc(row_s, 1)
                    for e in range(2):
                        V.tensor_tensor(bb[:, :, 32 * e:32 * e + 32], r[:, :, 32 - 32 * e:64 - 32 * e],
                                        sinr[0:P, t:t + 1, 32 * e:32 * e + 32].to_broadcast([P, H, 32]), ALU.mult).then_inc(row_s, 1)
                    n = n + 3
                    dve.wait_ge(row_s, n)
                    V.tensor_tensor(r, a, bb, ALU.add).then_inc(row_ok, 1)
                return n
            n = 0
            for blk in range(4):
                n = norm_block(blk, blk >= 2, n)
            for u in range(1, 16, 2):
                blk, c = u // 4, u % 4
                dst = qkT[:, 8 * (blk % 2) + 4 * (blk // 2) + c]
                sc = 1.0 if blk % 2 == 0 else HD ** -0.5
                dve.wait_ge(tr_ps, u + 1)
                b0 = 2 * (u % 3)
                V.tensor_scalar(dst[:, 0:TP], bank[b0][:, :], sc, None, ALU.mult)
                V.tensor_scalar(dst[:, TP:T], bank[b0 + 1][:, 0:TS], sc, None, ALU.mult).then_inc(tr_v, 1)
            dve.wait_ge(nd_ok, H)
            dve.wait_ge(cb_sb, H)

            def step(p, u, kind, first=False, last=False):
                if not last:
                    i, j, e = u // 2, u % 2, u % 4
                    N = 128 * (i + 1)
                    n = 8 * p + u
                    dve.wait_ge(s_ps, n + 1)
                    if not (first and u < 2):
                        dve.wait_ge(pt_ps, n - 1)
                    mxs = (14 * p + sum(2 if v >= 2 else 1 for v in range(u))) if kind == FOX else (56 + 8 * (p - 4) + u)
                    if kind == FOX:
                        h = 2 * p + j
                        V.tensor_tensor_reduce(PP[:, u % 2, i * 128:N], bank[u % 2][:, i * 128:N],
                                               ndiag[:, h, i, :],
                                               1.0, NEG, ALU.add, ALU.max, mx[:, e]).then_inc(s_mx, 1)
                        mxs = mxs + 1
                        last_mx = mx
                        if i > 0:
                            dve.wait_ge(s_mx, mxs)
                            V.tensor_tensor_reduce(PP[:, u % 2, 0:i * 128], bank[u % 2][:, 0:i * 128],
                                                   negc[:, h, 0:i * 128],
                                                   1.0, mx[:, e], ALU.add, ALU.max, mx2[:, e]).then_inc(s_mx, 1)
                            mxs = mxs + 1
                            last_mx = mx2
                    else:
                        V.tensor_tensor_reduce(PP[:, u % 2, 0:N], bank[u % 2][:, 0:N], logc[:, (3 - i) * 128:512],
                                               1.0, NEG, ALU.add, ALU.max, mx[:, e]).then_inc(s_mx, 1)
                        mxs = mxs + 1
                        last_mx = mx
                    dve.wait_ge(s_mx, mxs)
                    V.tensor_scalar(negm[:, e], last_mx[:, e], -1.0, None, ALU.mult).then_inc(s_nm, 1)
                if (u - 1) % 2 == 1 and not (first and u < 1):
                    v = (u - 1) % 8
                    N = 128 * (v // 2 + 1)
                    dve.wait_ge(pt_ps, 8 * p + u)
                    V.tensor_copy(PTs[:, 1, 0:N], bank[3][:, 0:N]).then_inc(pt_v, 1)
                if not (first and u < 2):
                    v = (u - 2) % 8
                    n = 8 * p + u - 2
                    V.reciprocal(rinv[:, v % 4], rs[:, v % 4]).then_inc(r_ok, 1)
                    dve.wait_ge(r_ok, n + 1)
                    dve.wait_ge(o_ps, n + 1)
                    if not (first and u < 6):
                        dve.wait_ge(at_ps, (8 * p + u - 2 - v % 2) // 2 - 1)
                    V.tensor_scalar(Arow[:, (v // 2) % 2, 64 * (v % 2):64 * (v % 2) + 64], bank[4 + v % 2][:, 0:HD], rinv[:, v % 4], None, ALU.mult).then_inc(a_ok, 1)
            for p in range(8):
                for u in range(8):
                    step(p, u, FOX if p < 4 else DSW, first=p == 0)
            for u in range(2):
                step(8, u, DSW, last=True)

            def kt_odd(n0, b, nch):
                for ch in range(1, nch, 2):
                    dve.wait_ge(kt_ps, b * 15 + n0 + ch + 1)
                    V.tensor_copy(KTs[:, 1], bank[1][:, :]).then_inc(kt_v, 1)

            def chunks_max(b, k):
                s, nch = ss[k], NCH[k]
                view = S1[k].rearrange("p c (h q) -> p c h q", q=DS)
                sc = bank[2 + k][:, 0:nch * 32].rearrange("p (c h q) -> p c h q", h=H, q=DS)
                dve.wait_ge(s["sc"], b + 1)
                if k == 0:
                    V.tensor_tensor(view, sc, cneg.rearrange("p c (h e) -> p c h e", e=1).to_broadcast([128, nch, H, DS]), ALU.add).then_inc(s["s1"], 1)
                    dve.wait_ge(s["s1"], 2 * b + 1)
                    V.tensor_tensor(view[:, NPG], view[:, NPG], fmask.rearrange("p (a q) -> p a q", a=1).to_broadcast([128, H, DS]), ALU.add).then_inc(s["s1"], 1)
                    dve.wait_ge(s["s1"], 2 * b + 2)
                else:
                    V.tensor_tensor(view, sc, dmask.rearrange("p c (e q) -> p c e q", e=1).to_broadcast([128, nch, H, DS]), ALU.add).then_inc(s["s1"], 1)
                    dve.wait_ge(s["s1"], b + 1)
                V.reduce_max(mp[k], S1[k].rearrange("p c n -> p n c"), AX.X).then_inc(s["mp"], 1)

            def max_diag(b, k):
                s = ss[k]
                dve.wait_ge(s["mt"], b + 1)
                V.reduce_max(mcol[k][0:32], bank[5][0:32, 0:128], AX.X).then_inc(s["m"], 1)
                dve.wait_ge(s["m"], b + 1)
                V.tensor_scalar(dg[k][0:32], ident[0:32, 0:32], mcol[k][0:32], None, ALU.mult).then_inc(s["dg"], 1)

            def shifted(b, k):
                s = ss[k]
                dve.wait_ge(s["mb"], b + 1)
                V.tensor_tensor(S1[k], S1[k], bank[5][:, 0:32].rearrange("p (a n) -> p a n", a=1).to_broadcast([128, NCH[k], 32]), ALU.subtract).then_inc(s["sub"], 1)

            def sums(b, k):
                s = ss[k]
                dve.wait_ge(s["p"], b + 1)
                V.reduce_sum(ps_[k], S1[k].rearrange("p c n -> p n c"), AX.X).then_inc(s["sum"], 1)

            def outputs(b, k):
                s = ss[k]
                dve.wait_ge(s["out"], b + 1)
                V.reciprocal(ri[k], bank[4][:, 32:64]).then_inc(s["ri"], 1)
                dve.wait_ge(s["ri"], b + 1)
                for j in range(2):
                    o = bank[4][64 * j:64 * j + 64, 0:32].rearrange("p (c j q) -> p c j q", j=2, q=DS)[:, :, j, :]
                    r = ri[k][64 * j:64 * j + 64].rearrange("p (c j q) -> p c j q", j=2, q=DS)[:, :, j, :]
                    V.tensor_tensor(AT[64 * j:64 * j + 64, k, :, ds(TP + b * DS, DS)], o, r, ALU.mult).then_inc(s["at"], 1)

            def batch(b):
                dve.wait_ge(cc_ps, b + 1)
                V.tensor_copy(cneg, bank[5][:, 0:72].rearrange("p (c h) -> p c h", h=H)).then_inc(cc_ok, 1)
                kt_odd(0, b, NCH[0])
                dve.wait_ge(cc_ok, b + 1)
                chunks_max(b, 0)
                max_diag(b, 0)
                kt_odd(9, b, NCH[1])
                shifted(b, 0)
                chunks_max(b, 1)
                sums(b, 0)
                max_diag(b, 1)
                outputs(b, 0)
                shifted(b, 1)
                sums(b, 1)
                outputs(b, 1)
            batch(0)
            with dve.Fori(1, DB) as b:
                batch(b)

            for m in range(8):
                b0 = 4 * (m % 2)
                dve.wait_ge(o_done, m + 1)
                dve.wait_ge(sg_ok, m + 1)
                if m >= 1:
                    dve.wait_ge(m_ok, m)
                for k in range(2):
                    for hf in range(2):
                        c = slice(hf * HALF, (hf + 1) * HALF)
                        V.tensor_tensor(tg[:, k, c], zg[:, m + 8 * k, c], bank[b0 + 2 * k + hf][:, 0:HALF], ALU.mult).then_inc(tg_ok, 1)
                dve.wait_ge(tg_ok, 4 * m + 4)
                V.tensor_tensor(mT[:, m], tg[:, 0], tg[:, 1], ALU.add).then_inc(m_ok, 1)
            for m in range(8):
                b0 = 2 * (m % 3)
                dve.wait_ge(wx_ps, m + 1)
                for hf in range(2):
                    c = slice(hf * HALF, (hf + 1) * HALF)
                    i = V.tensor_tensor(xT[:, m, c], xT[:, m, c], bank[b0 + hf][:, 0:HALF], ALU.add)
                i.then_inc(h_ok, 1)
            dve.wait_ge(h_ok, KT)
            scaled(std2_ok, rstd2_ok, u_ok, g2, xT, mT, std2)

            def hidden(m, s):
                b0 = 4 * (s % 2)
                dve.wait_ge(sil_ok, 2 * m + 2)
                for hf in range(2):
                    c = slice(hf * HALF, (hf + 1) * HALF)
                    V.tensor_tensor(sg[:, s % 2, c], sg[:, s % 2, c], bank[b0 + hf][:, 0:HALF], ALU.mult).then_inc(gm_ok, 1)
                dve.wait_ge(gm_ok, 2 * m + 2)
                for hf in range(2):
                    c = slice(hf * HALF, (hf + 1) * HALF)
                    i = V.tensor_tensor(hid[:, ds(m, 1), c].rearrange("p a n -> p (a n)"), sg[:, s % 2, c], bank[b0 + 2 + hf][:, 0:HALF], ALU.mult)
                i.then_inc(hid_ok, 1)
            with dve.Fori(0, 11) as i:
                for s in range(2):
                    hidden(2 * i + s, s)
            for m in range(8):
                dve.wait_ge(d_ps, m + 1)
                if m >= 2:
                    dve.wait_ge(yt_ps, m - 1)
                for hf in range(2):
                    c = slice(hf * HALF, (hf + 1) * HALF)
                    i = V.tensor_tensor(yT[:, m % 2, c], xT[:, m, c], bank[2 * (m % 2) + hf][:, 0:HALF], ALU.add)
                i.then_inc(y_ok, 1)

        @block.tensor
        def _(pe):
            mm = nc.tensor.matmul

            def halves(banks, w, src, ks, inc=None):
                for n, k in enumerate(ks):
                    for hf in range(2):
                        i = mm(banks[hf][:, 0:HALF], w[n], src[:, k, hf * HALF:(hf + 1) * HALF], start=(n == 0), stop=(n == len(ks) - 1))
                return i

            pe.wait_ge(c_in, 16 * N_CONST)
            pe.wait_ge(x_in, 32)
            for k in range(KT):
                if k >= 2:
                    pe.wait_ge(xT_sb, k - 1)
                for t in range(4):
                    nc.tensor.transpose(bank[2 * (k % 2)][:, t * 128:(t + 1) * 128], xrow[:, t, k * 128:(k + 1) * 128], ident)
                nc.tensor.transpose(bank[2 * (k % 2) + 1][:, 0:TS], xrow[0:TS, 4, k * 128:(k + 1) * 128], ident[0:TS, 0:TS]).then_inc(xT_ps, 1)

            def mean_square(ok, used, src):
                for k in range(KT):
                    pe.wait_ge(ok, k + 1)
                    for hf in range(2):
                        i = mm(bank[6 + hf][:, 0:HALF], mean1, src[:, k % 2, hf * HALF:(hf + 1) * HALF], start=(k == 0), stop=(k == KT - 1))
                    i.then_inc(used, 1)
            mean_square(sq_ok, sq_used, sq)
            pe.wait_ge(xn_ok, KT)
            pe.wait_ge(f_in, 16)
            for t in range(5):
                for k in range(KT):
                    i = mm(bank[5][0:PT_[t], 8 * t:8 * t + 8], xnT[:, k, t * 128:t * 128 + PT_[t]], wf[:, k, :], start=(k == 0), stop=(k == KT - 1))
            i.then_inc(f_ps, 1)

            def qkv(i, first):
                for s in range(2):
                    blk = 2 * i + s
                    pe.wait_ge(wq_in[s], 16 * i + 16)
                    for t in range(5):
                        if not (first and s == 0):
                            pe.wait_ge(z_used, 5 * blk + t - 4)
                        for k in range(KT):
                            x = mm(bank[t][0:PT_[t], :], xnT[:, k, t * 128:t * 128 + PT_[t]], WQ[:, s, k, :], start=(k == 0), stop=(k == KT - 1))
                        x.then_inc(z_ps, 1)
                    pe.wait_ge(z_ps, 5 * blk + 5)
                    pe.sem_inc(wq_used, 1)
            qkv(0, True)
            with pe.Fori(1, 3) as i:
                qkv(i, False)
            pe.wait_ge(lf_ok, 3)
            for j in range(4):
                i = mm(bank[6][0:8, :], lfx[:, j, :], ntri[:, 384 - 128 * j:896 - 128 * j], start=(j == 0), stop=(j == 3))
            i.then_inc(cT_ps, 1)
            for u in range(16):
                blk, c = u // 4, u % 4
                b0 = 2 * (u % 3)
                if c == 0:
                    pe.wait_ge(row_ok, 5 * blk + 5)
                if u == 0:
                    pe.wait_ge(z_used, 30)
                if u >= 3:
                    pe.wait_ge(tr_v if u % 2 == 0 else tr_a, (u - 3) // 2 + 1)
                for t in range(4):
                    nc.tensor.transpose(bank[b0][:, t * 128:(t + 1) * 128], rows[:, blk, t, c * 128:(c + 1) * 128], ident)
                nc.tensor.transpose(bank[b0 + 1][:, 0:TS], rows[0:TS, blk, 4, c * 128:(c + 1) * 128], ident[0:TS, 0:TS]).then_inc(tr_ps, 1)
            pe.wait_ge(cT_sb, 1)
            for h in range(H):
                if h >= 2:
                    pe.wait_ge(cb_sb, h - 1)
                mm(bank[6 + h % 2][:, :], sel[0:8, h, :], negcT[0:8], start=True, stop=True).then_inc(cb_ps, 1)
            pe.wait_ge(tr_a, 8)
            pe.wait_ge(tr_v, 8)
            pe.wait_ge(cb_sb, 8)

            def step(p, u, first=False, last=False):
                if not last:
                    i, j = u // 2, u % 2
                    N = 128 * (i + 1)
                    n = 8 * p + u
                    if not (first and u < 2):
                        pe.wait_ge(s_nm, n - 1)
                    mm(bank[u % 2][:, 0:N], qkT[64 * j:64 * j + 64, 8 + p, i * 128:(i + 1) * 128], qkT[64 * j:64 * j + 64, p, 0:N],
                       start=True, stop=True).then_inc(s_ps, 1)
                if not (first and u < 1) and not (last and u > 0):
                    v = (u - 1) % 8
                    n = 8 * p + u - 1
                    pe.wait_ge(p_ok, n + 1)
                    if not (first and u < 3):
                        e = (8 * p + u - 1 - v % 2) // 2
                        pe.wait_ge(pt_v if v % 2 else pt_a, e)
                    for c in range(v // 2 + 1):
                        x = nc.tensor.transpose(bank[2 + v % 2][:, c * 128:(c + 1) * 128], PP[:, v % 2, c * 128:(c + 1) * 128], ident)
                    x.then_inc(pt_ps, 1)
                if not (first and u < 2):
                    v = (u - 2) % 8
                    n = 8 * p + u - 2
                    e = (8 * p + u - 2 - v % 2) // 2
                    pe.wait_ge(pt_v if v % 2 else pt_a, e + 1)
                    if not (first and u < 4):
                        pe.wait_ge(a_ok, n - 1)
                    hcol = (2 * p + (v % 2)) * HD if u >= 2 else (2 * (p - 1) + (v % 2)) * HD
                    for c in range(v // 2 + 1):
                        x = mm(bank[4 + v % 2][:, 0:HD], PTs[:, v % 2, c * 128:(c + 1) * 128], vrows[:, c, hcol:hcol + HD], start=(c == 0), stop=(c == v // 2))
                    x.then_inc(o_ps, 1)
                if (u - 3) % 2 == 1 and not (first and u < 4):
                    block_out(p if u >= 4 else p - 1, ((u - 3) % 8) // 2, first)

            def block_out(p, i, first=False):
                pe.wait_ge(a_ok, 8 * p + 2 * i + 2)
                if not (first and i < 2):
                    pe.wait_ge(at_ok, 4 * p + i - 1)
                nc.tensor.transpose(bank[6 + i % 2][:, 0:128], Arow[:, i % 2, :], ident).then_inc(at_ps, 1)
            for p in range(8):
                for u in range(8):
                    step(p, u, first=p == 0)
            for u in range(2):
                step(8, u, last=True)
            block_out(7, 3)

            pe.wait_ge(at_ok, 32)
            pe.wait_ge(z_init, 8)
            pe.wait_ge(Qs_ok, 4)

            def chunks(b, k, n0, first):
                K, nch = (Kf, Kd)[k], NCH[k]

                def tr(ch):
                    n = b * 15 + n0 + ch
                    par = ch % 2
                    before = (b * 8 + (0 if k == 0 else 5) + ch // 2) if par == 0 else (b * 7 + (0 if k == 0 else 4) + ch // 2)
                    if not (first and n0 + ch < 2):
                        pe.wait_ge(kt_a if par == 0 else kt_v, before)
                    for c in range(NPAIR):
                        x = nc.tensor.transpose(bank[par][:, c * 128:(c + 1) * 128], K[:, ch, c * 128:(c + 1) * 128], ident)
                    x.then_inc(kt_ps, 1)
                tr(0)
                for ch in range(nch):
                    if ch + 1 < nch:
                        tr(ch + 1)
                    par = ch % 2
                    before = (b * 8 + (0 if k == 0 else 5) + ch // 2) if par == 0 else (b * 7 + (0 if k == 0 else 4) + ch // 2)
                    pe.wait_ge(kt_a if par == 0 else kt_v, before + 1)
                    for c in range(NPAIR):
                        x = mm(bank[2 + k][:, ch * 32 + c * 8:ch * 32 + c * 8 + 8], KTs[:, par, c * 128:(c + 1) * 128],
                               Qs[:, k, ds(b, 1), c].rearrange("p a j q -> p (a j q)"), start=True, stop=True)
                    if ch == nch - 1:
                        x.then_inc(ss[k]["sc"], 1)
                    else:
                        x.then_inc(ktq, 1)

            def max_T(b, k):
                s = ss[k]
                pe.wait_ge(s["mp"], b + 1)
                nc.tensor.transpose(bank[5][0:32, 0:128], mp[k], ident).then_inc(s["mt"], 1)

            def max_bc(b, k):
                s = ss[k]
                pe.wait_ge(s["dg"], b + 1)
                mm(bank[5][:, 0:32], ones[0:32], dg[k][0:32], start=True, stop=True).then_inc(s["mb"], 1)

            def attend(b, k):
                s, V, nch = ss[k], (Vf, Vd)[k], NCH[k]
                pe.wait_ge(s["sum"], b + 1)
                mm(bank[4][:, 32:64], ones, ps_[k], start=True, stop=True)
                for c in range(NPAIR):
                    for ch in range(nch):
                        x = mm(bank[4][:, c * 8:c * 8 + 8], V[:, ch, c * 128:(c + 1) * 128], S1[k][:, ch, c * 8:c * 8 + 8], start=(ch == 0), stop=(ch == nch - 1))
                x.then_inc(s["out"], 1)

            def gate(b, s, hf, first):
                if hf == 0:
                    pe.wait_ge(wg_in[s], 16 * b + 16)
                n = 4 * b + 2 * s + hf
                if not (first and s == 0):
                    pe.wait_ge(g_ok, n - 1)
                for k in range(KT):
                    x = mm(bank[6 + hf][:, 0:HALF], WG[:, s, k, :], xnT[:, k, hf * HALF:(hf + 1) * HALF], start=(k == 0), stop=(k == KT - 1))
                x.then_inc(g_ps, 1)
                if hf == 1:
                    pe.wait_ge(g_ps, n + 1)
                    pe.sem_inc(wg_used, 1)

            def batch(b, first):
                pe.wait_ge(l_in, 16 * 9 * (b + 1))
                if not first:
                    pe.wait_ge(ss[1]["sub"], b)
                cps = bank[5][:, 0:72]
                mm(cps, ntri[:, 384:512], lfp.rearrange("p c h -> p (c h)"), start=True, stop=False)
                for c in range(NPG):
                    x = mm(bank[5][:, 8 * (c + 1):72].rearrange("p (c h) -> p c h", h=H), ntri[:, 768:896],
                           lfp[:, c:c + 1, :].to_broadcast([128, NPG - c, H]), start=False, stop=(c == NPG - 1))
                x.then_inc(cc_ps, 1)
                pe.wait_ge(kf_in, 16 * 9 * (b + 1))
                chunks(b, 0, 0, first)
                gate(b, 0, 0, first)
                gate(b, 0, 1, first)
                max_T(b, 0)
                pe.wait_ge(kd_in, 16 * 6 * (b + 1))
                chunks(b, 1, 9, first)
                max_bc(b, 0)
                gate(b, 1, 0, first)
                pe.wait_ge(ss[0]["sub"], b + 1)
                max_T(b, 1)
                pe.wait_ge(vf_in, 16 * 9 * (b + 1))
                if not first:
                    pe.wait_ge(ss[1]["at"], 2 * b)
                attend(b, 0)
                max_bc(b, 1)
                gate(b, 1, 1, first)
                pe.wait_ge(vd_in, 16 * 6 * (b + 1))
                pe.wait_ge(ss[0]["at"], 2 * b + 2)
                attend(b, 1)
            batch(0, True)
            with pe.Fori(1, DB) as b:
                batch(b, False)

            pe.wait_ge(ss[0]["at"], 2 * DB)
            pe.wait_ge(ss[1]["at"], 2 * DB)
            pe.wait_ge(g_ok, 4 * DB)
            def merged(m, s, first):
                pe.wait_ge(wo_in[s], 32 * (m // 4) + 32 if isinstance(m, int) else 64)
                if not (first and s < 2):
                    pe.wait_ge(tg_ok, 4 * m - 4)
                for k in range(2):
                    x = halves(bank[4 * (s % 2) + 2 * k:4 * (s % 2) + 2 * k + 2], [WO[:, s, k, c] for c in range(NPAIR)], AT[:, k], range(NPAIR))
                x.then_inc(o_done, 1)
                pe.wait_ge(o_done, m + 1)
                pe.sem_inc(wo_used, 1)
            for m in range(8):
                merged(m, m % 4, m < 4)
            pe.wait_ge(tg_ok, 32)
            pe.wait_ge(m_ok, 8)
            for m in range(8):
                pe.wait_ge(wx_in[m % 4], 16 * (m // 4) + 16)
                if m >= 3:
                    pe.wait_ge(h_ok, m - 2)
                halves(bank[2 * (m % 3):2 * (m % 3) + 2], [WX[:, m % 4, k] for k in range(KT)], mT, range(KT)).then_inc(wx_ps, 1)
            mean_square(sq2_ok, sq2_used, sq2)

            pe.wait_ge(u_ok, KT)
            def up(m, s, first):
                pe.wait_ge(wu_in[s], 32 * (m // 4) + 32) if isinstance(m, int) else None
                if not (first and s < 2):
                    pe.wait_ge(hid_ok, m - 1)
                for k in range(2):
                    x = halves(bank[4 * (s % 2) + 2 * k:4 * (s % 2) + 2 * k + 2], [WU[:, s, c, k, :] for c in range(KT)], mT, range(KT))
                x.then_inc(u_ps, 1)
            for s in range(4):
                up(s, s, True)
            with pe.Fori(1, 5) as i:
                for s in range(4):
                    pe.wait_ge(wu_in[s], 32 * i + 32)
                    up(4 * i + s, s, False)
            for s in range(2):
                up(20 + s, s, False)
            pe.wait_ge(hid_ok, KF)

            def y_out(m):
                pe.wait_ge(y_ok, m + 1)
                if m >= 2:
                    pe.wait_ge(yst_ok, m - 1)
                b0 = 4 + 2 * (m % 2)
                for t in range(4):
                    nc.tensor.transpose(bank[b0][:, t * 128:(t + 1) * 128], yT[:, m % 2, t * 128:(t + 1) * 128], ident)
                nc.tensor.transpose(bank[b0 + 1][0:TS, 0:128], yT[:, m % 2, TP:T], ident).then_inc(yt_ps, 1)
            for m in range(8):
                pe.wait_ge(wd_in[m % 2], 16 * (m // 2) + 16)
                if m >= 2:
                    pe.wait_ge(y_ok, m - 1)
                halves(bank[2 * (m % 2):2 * (m % 2) + 2], [WD[:, m % 2, k] for k in range(KF)], hid, range(KF)).then_inc(d_ps, 1)
                if m >= 1:
                    y_out(m - 1)
            y_out(7)


_INS = ["x_prompt", "x_sample", "cache_k_fox", "cache_v_fox", "cache_logf_fox", "state_k_dsw", "state_v_dsw", "page_table",
        "norm1_g", "w_in", "b_f", "q_norm_fox", "k_norm_fox", "q_norm_dsw", "k_norm_dsw", "w_o_fox", "w_o_dsw", "w_out",
        "norm2_g", "w_gate", "w_up", "w_down"]


def constants():
    import numpy as np
    p = np.arange(128)
    c = np.zeros((128, C_END), np.float32)
    c[:, C_ID:C_ID + 128] = np.eye(128)
    c[:, C_MEAN:C_MEAN + 128] = 1.0 / D
    c[:, C_ONE:C_ONE + 128] = 1.0
    c[:, C_TRI:C_TRI + 128] = np.where(p[None, :] <= p[:, None], 0.0, NEG)
    c[:, C_NTRI:C_NTRI + 896] = np.where(np.arange(896)[None, :] - 384 >= p[:, None], -1.0, 0.0)

    def log_count(dist):
        n = ((dist >= 0) & (dist <= 128)) * 1 + ((dist >= 0) & (dist <= 512) & (dist % 4 == 0)) + ((dist >= 0) & (dist <= 2048) & (dist % 16 == 0))
        return np.where(n > 0, np.log(np.maximum(n, 1)), NEG)
    for s in range(4):
        c[:, C_LC + 128 * s:C_LC + 128 * (s + 1)] = log_count(128 * (3 - s) + p[:, None] - p[None, :])
    half = HD // 2
    inv = np.float32(10000.0) ** (-np.arange(half, dtype=np.float32) / np.float32(half))
    for t in range(5):
        pos = (128 * t + p) if t < 4 else PAST + p % DS
        ang = pos.astype(np.float32)[:, None] * inv.astype(np.float32)[None, :]
        co, si = np.cos(ang), np.sin(ang)
        c[:, C_COS + 64 * t:C_COS + 64 * t + 64] = np.concatenate([co, co], 1)
        c[:, C_SIN + 64 * t:C_SIN + 64 * t + 64] = np.concatenate([-si, si], 1)
    for ch in range(6):
        key = 512 + 128 * ch + p if ch < 4 else 16 * (p // 4) + p % 4 if ch == 4 else PAST + p
        for q in range(DS):
            v = log_count(PAST + q - key)
            c[:, C_DM + 4 * ch + q] = np.where(p < DS, v, NEG) if ch == 5 else v
    for q in range(DS):
        c[:, C_FM + q] = np.where((p < DS) & (p <= q), 0.0, NEG)
    c[:, C_EPS] = EPS
    s = np.zeros((8, 8, 128), np.float32)
    for h in range(8):
        s[h, h, :] = 1.0
    return c, s.reshape(8, 1024)


def kernel(**inputs):
    import numpy as np
    import concourse.bacc as bacc
    from concourse.bass_utils import run_bass_kernel_spmd
    nc = bacc.Bacc("TRN2", target_bir_lowering=False, num_devices=1)
    arrays, args = {}, []
    cpack, selin = constants()
    for name, a in [(n, inputs[n]) for n in _INS] + [("cpack", cpack), ("selin", selin)]:
        a = np.ascontiguousarray(a)
        arrays["in_" + name] = a
        args.append(nc.dram_tensor("in_" + name, a.shape, mybir.dt.from_np(a.dtype), kind="ExternalInput").ap())
    L = 1
    outs = [(1, TP, D), (DB, DS, D), (L, 1, TP, H, HD), (L, 1, TP, H, HD), (L, 1, TP, H), (L, 1, TP, H, HD), (L, 1, TP, H, HD),
            (L, DB, DS, H, HD), (L, DB, DS, H, HD), (L, DB, DS, H), (L, DB, PAST, H, HD), (L, DB, PAST, H, HD)]
    for i, shape in enumerate(outs):
        args.append(nc.dram_tensor(f"out_{i}", shape, mybir.dt.float32, kind="ExternalOutput").ap())
    program(nc, *args)
    r = run_bass_kernel_spmd(nc, [arrays], core_ids=[0])
    return tuple(r.results[0][f"out_{i}"] for i in range(len(outs)))
```

```python
import concourse.bass as bass
from concourse import mybir
from contextlib import ExitStack

D, TP, DB, DS = 1024, 512, 8, 4
TS = DB * DS
T = TP + TS
HALF = T // 2
KT = D // 128
HD, H = 64, 8
W = H * HD
NPAIR = W // 128
FFN, KF = 2816, 22
PAST, PAGE = 1024, 128
NPG = PAST // PAGE
EPS = 1e-6
NEG = -1e30
PT_ = [128, 128, 128, 128, TS]
FOX, DSW = 0, 1
NCH = [NPG + 1, 6]
NALL = NCH[0] + NCH[1]
NKR = 5
KD = KF // 2
PASSES = ((0, 0), (0, 1), (1, 0))
COL_F, COL_G = 3 * W, 3 * W + H + 3 * W
BLOCKS = [W, 0, 3 * W + H + W, 3 * W + H, 2 * W, 3 * W + H + 2 * W]

C_ID, C_MEAN, C_ONE, C_TRI, C_NTRI, C_LC, C_COS, C_SIN, C_DM, C_FM = 0, 128, 256, 384, 512, 1408, 1920, 2240, 2560, 2584
C_END = 2588


def program(nc, x_prompt, x_sample, cache_k, cache_v, cache_lf, state_k, state_v, page_table, norm1_g, w_in, b_f,
            qn_f, kn_f, qn_d, kn_d, w_o_fox, w_o_dsw, w_out, norm2_g, w_gate, w_up, w_down, cpack, selin,
            y_p, y_s, kf_p, vf_p, lf_p, kd_p, vd_p, kf_s, vf_s, lf_s, kd_s, vd_s):
    f32, i32 = mybir.dt.float32, mybir.dt.int32
    ALU, ACT, AX = mybir.AluOpType, mybir.ActivationFunctionType, mybir.AxisListType
    ds = bass.ds
    ctx = ExitStack()
    with ctx:
        ctx.enter_context(nc.allow_non_contiguous_dma(reason="small parameter vectors"))
        names = set()

        def sem(name):
            return ctx.enter_context(nc.semaphore(name))

        ARENA = 53184
        arena_at = 16512
        count = [0]
        cur = [0]

        def shaped(v, shape):
            if len(shape) == 1:
                return v
            nm = "abcdef"[:len(shape)]
            return v.rearrange(f"p ({' '.join(nm)}) -> p {' '.join(nm)}", **{a: s for a, s in zip(nm, shape)})

        def put(shape, at=None, part=128):
            n = 1
            for s in shape:
                n *= s
            if at is None:
                at = cur[0]
                cur[0] += n + -n % 8
            assert at + n <= ARENA, (at, n)
            count[0] += 1
            return shaped(nc.alloc_sbuf_tensor_at(f"buffer{count[0]}", [part, n], f32, offset=arena_at + 4 * at)[:, :], shape)

        def put_r(name, shape, at):
            n = 1
            for s in shape:
                n *= s
            assert at + n <= ARENA, (at, n)
            t = nc.alloc_sbuf_tensor_at(name, [128, n], mybir.dt.float32r, offset=arena_at + 4 * at)
            return shaped(t[:, :], shape)

        cp = put([C_END + 4])
        ident = cp[:, C_ID:C_ID + 128]
        mean1 = cp[:, C_MEAN:C_MEAN + 128]
        ones = cp[:, C_ONE:C_ONE + 128]
        tri = cp[:, C_TRI:C_TRI + 128]
        ntri = cp[:, C_NTRI:C_NTRI + 896]
        logc = cp[:, C_LC:C_LC + 512]
        cosr = cp[:, C_COS:C_COS + 320].rearrange("p (t d) -> p t d", d=64)
        sinr = cp[:, C_SIN:C_SIN + 320].rearrange("p (t d) -> p t d", d=64)
        dmask = cp[:, C_DM:C_DM + 24].rearrange("p (c q) -> p c q", q=4)
        fmask = cp[:, C_FM:C_FM + 4]
        SEL = cur[0]
        sel = put([H, 128], part=8)
        onr = put([W], SEL)
        WDr = put([2, KD, 128], C_TRI)
        epsc = put([1])
        gains = put([4, HD])
        g1 = put([KT])
        g2 = put([KT])
        bf = put([H])
        ptab = put([64]).bitcast(i32)
        rstd = put([T])
        ssum = put([4, 5, H])
        lfx = put([5, H])
        lfe = put([5, H])
        lfa = put([5, H])
        negcT = put([TP], part=8)
        Qs = put([2, DB, NPAIR, 2, DS])
        mx = put([4, 1])
        mx2 = put([4, 1])
        negm = put([4, 1])
        rs = put([4, 1])
        rinv = put([4, 1])
        xT = put([KT, T])
        X2at = cur[0]
        put([2, KT, T])
        X2 = put_r("x_split", [2, KT, T], X2at)
        Z = cur[0]
        WQ = put([2, 4, W], Z)
        WQs = put_r("wqkv_split", [2, 2, 4, W], Z + 4096)
        rows = put([4, 5, W], Z + 12288)
        xrow = put([5, D], Z + 12288)
        vrows = put([5, 2 * W], Z + 22528)
        sq = put([2, T], Z + 27648)
        rt = put([2, W], Z + 28736)
        wf = put([KT, H], Z + 29760)
        wfs = put_r("wf_split", [2, KT, H], Z + 29824)
        tmpA = put([2, T], Z + 29952)
        qkT = put([16, T], Z)
        negc = put([H, TP], Z + 12288)
        ndiag = put([H, 4, 128], Z + 16384)
        PP = put([2, TP], Z + 20480)
        PTs = put([2, TP], Z + 21504)
        Arow = put([2, 128], Z + 27648)
        AT = put([2, NPAIR, T], Z + 27904)
        WR = put([4, 1024], Z)
        WS = put_r("w_split", [2, 2, 1024], Z + 4096)
        zg = put([16, T], Z + 8192)
        Vf = put([NCH[0], W], Z + 16896)
        Vd = put([NCH[1], W], Z + 21504)
        Kr = put([NKR, W], Z + 24576)
        lfp = put([NCH[0], H], Z + 27136)
        cneg = put([NCH[0], H], Z + 27208)
        mp = put([128], Z + 27280)
        mcol = put([1], Z + 27408)
        dg = put([64], Z + 27416)
        ps_ = put([64], Z + 27480)
        ri = put([1], Z + 27544)
        KTs = put([3, W], Z + 32256)
        S1 = put([NALL, 32], Z + 33792)
        Ahl = put_r("a_split", [2, 2 * NPAIR, T], Z + 16896)
        tg = put([2, T], Z + 25600)
        sq2 = put([2, T], Z + 26688)
        std2 = put([T], Z + 32256)
        tmpM = put([2, T], Z + 32800)
        Hhl = put_r("h_split", [2, KF, T], Z + 8192)
        sg = put([2, T], Z + 32128)
        tmpH = put([T], Z + 33216)
        WSD = put_r("wd_split", [2, 2, KD * 128], Z)
        yT = put([2, T], X2at)
        yst = put([2, 5, 128], X2at + 1088)
        bank = [ctx.enter_context(nc.psum_tensor(f"bank{i}", [128, 512], f32)) for i in range(8)]

        TB = (0, 1, 3)

        xp_v = x_prompt[0].rearrange("(t p) n -> p t n", p=128)
        xs_v = x_sample.rearrange("b s n -> (b s) n")
        win_v = w_in[0].rearrange("(k p) n -> p k n", p=128)
        lay = lambda a: a.rearrange("l b s h d -> (l b) s (h d)")
        kfp_v, vfp_v, kdp_v, vdp_v = [lay(a)[0].rearrange("(t p) n -> p t n", p=128) for a in (kf_p, vf_p, kd_p, vd_p)]
        kfs_v, vfs_v, kds_v, vds_v = [lay(a) for a in (kf_s, vf_s, kd_s, vd_s)]
        sk_v, sv_v = lay(state_k), lay(state_v)
        ck_v, cv_v = [a.rearrange("l n g h d -> (l n) g (h d)") for a in (cache_k, cache_v)]
        cl_v = cache_lf[0]
        lfs_v = lf_s[0]
        wof_v = [w[0].rearrange("(k p) n -> p k n", p=128) for w in (w_o_fox, w_o_dsw)]
        wx_v = w_out[0].rearrange("(k p) n -> p k n", p=128)
        wg_v = [w[0].rearrange("(k p) n -> p k n", p=128) for w in (w_gate, w_up)]
        wd_v = w_down[0].rearrange("(k p) n -> p k n", p=128)
        yp_v = y_p[0].rearrange("(t p) n -> p t n", p=128)
        ys_v = y_s.rearrange("b s n -> (b s) n")
        n_phys = ck_v.shape[0]

        c_in, x_in, f_in = sem("consts_in"), sem("x_in"), sem("wf_in")
        xT_ps, xT_sb = sem("xT_in_psum"), sem("xT_ready")
        sq_ok, sq_used, std_ok, rstd_ok, xn_ok = [sem("n1_" + s) for s in ("squared", "summed", "std", "rstd", "xn_ready")]
        sq2_ok, sq2_used, std2_ok, rstd2_ok, u_ok = [sem("n2_" + s) for s in ("squared", "summed", "std", "rstd", "u_ready")]
        z_init, eps_ok = sem("zeroed"), sem("eps_laid")
        f_ps, lfx_ok, lfe_ok, lf_ok = sem("f_in_psum"), sem("f_biased"), sem("f_act"), sem("logf_ready")
        wq_in = [sem(f"wqkv_in{s}") for s in range(2)]
        wqh_ok, wql_ok, wfh_ok, wfl_ok = sem("wqkv_hi"), sem("wqkv_lo"), sem("wf_hi"), sem("wf_lo")
        xt_ok, xh_ok, ut_ok, uh_ok, ah_ok, al_ok = [sem(n) for n in ("xn_whole", "xn_hi", "u_whole", "u_hi", "a_hi", "a_lo")]
        z_ps, z_used = sem("z_in_psum"), sem("z_copied")
        zs_ok, zs_sum, zs_std, zs_inv, row_s, row_ok = [sem("row_" + s) for s in ("squared", "summed", "std", "inverse", "step", "done")]
        tr_ps, tr_a, tr_v = sem("qkT_in_psum"), sem("qkT_copied_act"), sem("qkT_copied_dve")
        st_k = sem("rows_stored")
        st_lf = sem("logf_stored")
        sts = sem("sample_rows_stored")
        cT_ps, cT_sb, cb_ps, cb_sb, nd_ok = sem("cT_in_psum"), sem("cT_ready"), sem("c_in_psum"), sem("negc_ready"), sem("ndiag_ready")
        Qs_ok = sem("Qs_ready")
        s_ps, s_mx, s_nm, p_ok, pt_ps, pt_a, pt_v, o_ps, r_ok, a_ok, at_ps, at_ok = [sem("pa_" + s) for s in (
            "scores", "max_step", "negmax", "probs", "probsT_psum", "probsT_act", "probsT_dve", "out_psum", "recip",
            "out_rows", "outT_psum", "outT_ready")]
        vf_in, l_in, vd_in = [sem(s) for s in ("vfox_in", "lfox_in", "vdsw_in")]
        k_in = [sem(f"keys_in{s}") for s in range(NKR)]
        w_in_ = [sem(f"w_in{s}") for s in range(4)]
        wh_ok, wl_ok, prod_ps, g_ok = sem("w_hi"), sem("w_lo"), sem("product_halves"), sem("gate_copied")
        cc_ps, cc_ok = sem("sc_in_psum"), sem("sc_ready")
        kt_ps, kt_a, kt_v, ktq = sem("skT_psum"), sem("skT_act"), sem("skT_dve"), sem("skT_used")
        sc_ps, s1_ok, mp_ok, mt_ps, m_col, dg_ok, mb_ps, sub_ok, sp_ok, sum_ok, so_ps, ri_ok, on_ok, ot_ps, sat_ok = [sem("sa_" + n) for n in (
            "scores", "biased", "chunk_max", "max_T", "max", "max_diag", "max_bc", "shifted", "probs", "sums", "outputs", "recip", "rows", "rows_T", "outT")]
        cpy = sem("state_copied")
        sg_ok, tg_ok, mt_ok, mh_ok, m_ok = sem("gates_sigmoid"), sem("merge_step"), sem("m_whole"), sem("m_hi"), sem("m_ready")
        h_ok = sem("h_ready")
        sil_ok, gm_ok, ht_ok, hh_ok, hid_ok = sem("ffn_sigmoid"), sem("ffn_gate_mul"), sem("hidden_whole"), sem("hidden_hi"), sem("hidden_ready")
        wd_in = [sem(f"wd_in{s}") for s in range(2)]
        dh_ok, dl_ok = sem("wd_hi"), sem("wd_lo")
        d_ps, y_ok, yt_ps, yst_ok = sem("down_out"), sem("yT_ready"), sem("y_in_psum"), sem("y_rows_ready")
        y_st = [sem(f"y_stored{s}") for s in range(2)]
        N_CONST = 10

        block = ctx.enter_context(nc.Block())

        @block.sync
        def _(sp):
            sp.dma_start(cp[:, 0:C_END], cpack).then_inc(c_in, 16)
            sp.dma_start(xrow[:, 0:4, :], xp_v).then_inc(x_in, 16)
            sp.dma_start(xrow[0:TS, 4, :], xs_v).then_inc(x_in, 16)
            sp.dma_start(sel[0:8], selin.rearrange("h (a c) -> h a c", c=128)).then_inc(c_in, 16)
            sp.dma_start(g1, norm1_g[0].rearrange("(k p) -> p k", p=128)).then_inc(c_in, 16)
            sp.dma_start(g2, norm2_g[0].rearrange("(k p) -> p k", p=128)).then_inc(c_in, 16)
            for n, g in enumerate((kn_f, qn_f, kn_d, qn_d)):
                sp.dma_start(gains[:, n, :], g[0:1, :].to_broadcast([128, HD])).then_inc(c_in, 16)
            sp.dma_start(bf, b_f[0:1, :].to_broadcast([128, H])).then_inc(c_in, 16)
            sp.dma_start(ptab[0:1, :], page_table.rearrange("b n -> (b n)").rearrange("(a n) -> a n", a=1)).then_inc(c_in, 16)
            sp.dma_start(wf, win_v[:, :, COL_F:COL_F + H]).then_inc(f_in, 16)
            def shift(b):
                sp.dma_start(kds_v[b, 0:PAST - DS], sk_v[b, DS:PAST]).then_inc(cpy, 16)
                sp.dma_start(vds_v[b, 0:PAST - DS], sv_v[b, DS:PAST]).then_inc(cpy, 16)
            for n in range(12):
                blk, kh = n // 2, n % 2
                if n >= 2:
                    sp.wait_ge(wql_ok, n - 1)
                sp.dma_start(WQ[:, n % 2], win_v[:, 4 * kh:4 * kh + 4, BLOCKS[blk]:BLOCKS[blk] + W]).then_inc(wq_in[n % 2], 16)
                if n % 2 and n >= 3:
                    shift(blk - 1)
            sp.wait_ge(sts, 16 * 5)
            sp.wait_ge(at_ok, 32)
            sp.wait_ge(z_init, 8)

            def pages(b, e, first):
                page = [sp.value_load(ptab[0:1, ds(b * NPG + n, 1)], min_val=0, max_val=n_phys - 1) for n in range(NPG)]
                if not first:
                    sp.wait_ge(cc_ps, b)
                sp.dma_start(lfp[0:DS, NPG, :], lfs_v[ds(b, 1)].rearrange("a g n -> (a g) n")).then_inc(l_in, 16)
                for n in range(NPG):
                    sp.dma_start(lfp[:, n, :], cl_v[ds(page[n], 1)].rearrange("a g n -> (a g) n")).then_inc(l_in, 16)
                for s in range(2):
                    if not first or b:
                        if not (isinstance(b, int) and 2 * b + s < 4):
                            sp.wait_ge(wl_ok, 2 * b + s - 3)
                    sp.dma_start(WR[:, 2 * e + s].rearrange("p (k n) -> p k n", n=128), win_v[:, :, ds(COL_G + b * 256 + s * 128, 128)]).then_inc(w_in_[2 * e + s], 32)
                for ch in range(NALL):
                    if not (first and ch < NKR):
                        sp.wait_ge(kt_ps, b * NALL + ch - NKR + 1)
                    dst, inc = Kr[:, ch % NKR, :], k_in[ch % NKR]
                    if ch < NPG:
                        sp.dma_start(dst, ck_v[ds(page[ch], 1)].rearrange("a g n -> (a g) n")).then_inc(inc, 16)
                    elif ch == NPG:
                        sp.dma_start(dst[0:DS], kfs_v[ds(b, 1)].rearrange("a g n -> (a g) n")).then_inc(inc, 16)
                    elif ch < NALL - 2:
                        n = ch - NCH[0]
                        sp.dma_start(dst, sk_v[ds(b, 1), 512 + 128 * n:640 + 128 * n].rearrange("a g n -> (a g) n")).then_inc(inc, 16)
                    elif ch == NALL - 2:
                        sp.dma_start(Vd[:, 0, :], sv_v[ds(b, 1), 512:640].rearrange("a g n -> (a g) n")).then_inc(vd_in, 16)
                        sp.dma_start(dst, sk_v[ds(b, 1), 0:512].rearrange("a (g r) n -> (a g) r n", r=16)[:, 0:4, :]).then_inc(inc, 16)
                    else:
                        sp.dma_start(dst[0:DS], kds_v[ds(b, 1), PAST - DS:PAST].rearrange("a g n -> (a g) n")).then_inc(inc, 16)
                    if ch == NKR - 1:
                        if not first:
                            sp.wait_ge(so_ps, b)
                        for n in range(NPG):
                            sp.dma_start(Vf[:, n, :], cv_v[ds(page[n], 1)].rearrange("a g n -> (a g) n")).then_inc(vf_in, 16)
                        sp.dma_start(Vf[0:DS, NPG, :], vfs_v[ds(b, 1)].rearrange("a g n -> (a g) n")).then_inc(vf_in, 16)
                for n in range(1, 4):
                    sp.dma_start(Vd[:, n, :], sv_v[ds(b, 1), 512 + 128 * n:640 + 128 * n].rearrange("a g n -> (a g) n")).then_inc(vd_in, 16)
                sp.dma_start(Vd[:, 4, :], sv_v[ds(b, 1), 0:512].rearrange("a (g r) n -> (a g) r n", r=16)[:, 0:4, :]).then_inc(vd_in, 16)
                sp.dma_start(Vd[0:DS, 5, :], vds_v[ds(b, 1), PAST - DS:PAST].rearrange("a g n -> (a g) n")).then_inc(vd_in, 16)

            pages(0, 0, True)
            pages(1, 1, False)
            with sp.Fori(1, DB // 2) as i:
                for e in range(2):
                    pages(2 * i + e, e, False)
            ring = lambda s: WR[:, s].rearrange("p (k n) -> p k n", n=128)
            for m in range(8):
                sp.wait_ge(wl_ok, 16 + m - 3)
                for k in range(2):
                    sp.dma_start(ring(m % 4)[:, 4 * k:4 * k + 4], wof_v[k][:, :, m * 128:(m + 1) * 128]).then_inc(w_in_[m % 4], 16)
            for m in range(8):
                sp.wait_ge(wl_ok, 24 + m - 3)
                sp.dma_start(ring(m % 4), wx_v[:, :, m * 128:(m + 1) * 128]).then_inc(w_in_[m % 4], 32)
            with sp.Fori(0, KF // 2) as i:
                for s in range(4):
                    sp.wait_ge(wl_ok, 32 + 4 * i + s - 3)
                    sp.dma_start(ring(s), wg_v[s % 2][:, :, ds((2 * i + s // 2) * 128, 128)]).then_inc(w_in_[s], 32)
            sp.wait_ge(sat_ok, 4 * DB)
            for b in range(5, DB):
                shift(b)
            for n in range(16):
                m, kh = n // 2, n % 2
                if n >= 2:
                    sp.wait_ge(dl_ok, n - 1)
                sp.dma_start(WDr[:, kh], wd_v[:, KD * kh:KD * kh + KD, m * 128:(m + 1) * 128]).then_inc(wd_in[kh], 16)
            sp.wait_ge(cpy, 16 * 2 * DB)
            sp.wait_ge(st_k, 16 * 4)
            sp.wait_ge(st_lf, 16)
            sp.wait_ge(sts, 16 * 5)

        @block.gpsimd
        def _(pool):
            nc.gpsimd.memset(epsc, EPS).then_inc(eps_ok, 1)
            nc.gpsimd.memset(Qs, 0.0).then_inc(z_init, 1)
            nc.gpsimd.memset(lfx, 0.0).then_inc(z_init, 1)
            nc.gpsimd.memset(ssum, 1.0).then_inc(z_init, 1)
            pool.wait_ge(lf_ok, 3)
            pool.dma_start(lf_p[0, 0].rearrange("(t p) h -> p t h", p=128), lfx[:, 0:4, :]).then_inc(st_lf, 16)
            pool.dma_start(lfs_v.rearrange("b s h -> (b s) h"), lfx[0:TS, 4, :]).then_inc(sts, 16)
            for blk, out_p, out_s in ((0, kfp_v, kfs_v), (2, kdp_v, kds_v)):
                pool.wait_ge(row_ok, 5 * blk + 5)
                pool.dma_start(out_p, rows[:, blk, 0:4, :]).then_inc(st_k, 16)
                if blk == 0:
                    pool.dma_start(out_s.rearrange("b s n -> (b s) n"), rows[0:TS, blk, 4, :]).then_inc(sts, 16)
                else:
                    pool.dma_start(out_s[:, PAST - DS:PAST, :], rows[0:TS, blk, 4, :]).then_inc(sts, 16)
            for k, out_p, out_s in ((0, vfp_v, vfs_v), (1, vdp_v, vds_v)):
                pool.wait_ge(z_used, 5 * (4 + k) + 5)
                pool.dma_start(out_p, vrows[:, 0:4, k * W:(k + 1) * W]).then_inc(st_k, 16)
                if k == 0:
                    pool.dma_start(out_s.rearrange("b s n -> (b s) n"), vrows[0:TS, 4, k * W:(k + 1) * W]).then_inc(sts, 16)
                else:
                    pool.dma_start(out_s[:, PAST - DS:PAST, :], vrows[0:TS, 4, k * W:(k + 1) * W]).then_inc(sts, 16)
            pool.wait_ge(tr_a, 8)
            pool.wait_ge(tr_v, 8)
            pool.wait_ge(z_init, 3)
            for k in range(2):
                for j in range(2):
                    nc.gpsimd.tensor_copy(Qs[64 * j:64 * j + 64, k, :, :, j, :],
                                          qkT[64 * j:64 * j + 64, 8 + 4 * k:12 + 4 * k, TP:T].rearrange("p c (b q) -> p b c q", q=DS)).then_inc(Qs_ok, 1)
            pool.wait_ge(Qs_ok, 4)
            for h in range(H):
                pool.wait_ge(cb_sb, h + 1)
                nc.gpsimd.tensor_tensor(ndiag[:, h], negc[:, h].rearrange("p (c n) -> p c n", n=128),
                                        tri.rearrange("p (a n) -> p a n", a=1).to_broadcast([128, 4, 128]), ALU.add).then_inc(nd_ok, 1)
            pool.wait_ge(at_ok, 32)
            nc.gpsimd.memset(mp, 0.0).then_inc(z_init, 1)
            nc.gpsimd.memset(onr, 0.0).then_inc(z_init, 1)
            for t in (Vf, lfp):
                nc.gpsimd.memset(t[:, NPG, :], 0.0).then_inc(z_init, 1)
            nc.gpsimd.memset(Vd[:, 5, :], 0.0).then_inc(z_init, 1)

        @block.scalar
        def _(act):
            def squares(ok, used, inn, src, dst):
                for k in range(KT):
                    act.wait_ge(inn, k + 1)
                    if k >= 2:
                        act.wait_ge(used, k - 1)
                    nc.scalar.activation(dst[:, k % 2], src[:, k], ACT.Square).then_inc(ok, 1)

            def stds(used, ok, dst):
                act.wait_ge(used, KT)
                for hf in range(2):
                    nc.scalar.activation(dst[:, hf * HALF:(hf + 1) * HALF], bank[6 + hf][:, 0:HALF], ACT.Sqrt, bias=epsc).then_inc(ok, 1)

            def hi(dst, src, whole, n, done):
                act.wait_ge(whole, n)
                nc.scalar.copy(dst, src).then_inc(done, 1)

            def wq_hi(n):
                act.wait_ge(wq_in[n % 2], 16 * (n // 2) + 16)
                if n >= 2:
                    act.wait_ge(z_ps, 5 * (n - 1))
                nc.scalar.copy(WQs[:, n % 2, 0], WQ[:, n % 2]).then_inc(wqh_ok, 1)
            act.wait_ge(c_in, 16 * N_CONST)
            act.wait_ge(eps_ok, 1)
            squares(sq_ok, sq_used, xT_sb, xT, sq)
            stds(sq_used, std_ok, rstd)
            hi(wfs[:, 0], wf, f_in, 16, wfh_ok)
            for k in range(KT):
                hi(X2[:, 0, k], tmpA[:, k % 2], xt_ok, k + 1, xh_ok)
            wq_hi(0)
            wq_hi(1)
            act.wait_ge(lfx_ok, 3)
            nc.scalar.activation(lfe, lfe, ACT.Exp, scale=-1.0).then_inc(lfe_ok, 1)
            act.wait_ge(lfe_ok, 1)
            nc.scalar.activation(lfe, lfe, ACT.Ln, bias=1.0).then_inc(lfe_ok, 1)

            def rows_block(blk):
                wq_hi(2 * blk + 2)
                for t in range(5):
                    P = PT_[t]
                    act.wait_ge(z_ps, 10 * blk + 5 + t + 1)
                    nc.scalar.copy(rows[0:P, blk, t, :], bank[t][128 - P:128, :]).then_inc(z_used, 1)
                    act.wait_ge(z_used, 5 * blk + t + 1)
                    if 5 * blk + t >= 2:
                        act.wait_ge(zs_sum, 5 * blk + t - 1)
                    nc.scalar.activation(sq[0:P, t % 2, 0:W], rows[0:P, blk, t, :], ACT.Square).then_inc(zs_ok, 1)
                wq_hi(2 * blk + 3)
                act.wait_ge(zs_sum, 5 * blk + 5)
                nc.scalar.activation(ssum[:, blk], ssum[:, blk], ACT.Sqrt, bias=epsc, scale=1.0 / HD).then_inc(zs_std, 1)
            act.wait_ge(z_init, 3)
            for blk in range(4):
                rows_block(blk)
            for k in range(2):
                if k == 0:
                    wq_hi(10)
                for t in range(5):
                    P = PT_[t]
                    act.wait_ge(z_ps, 10 * (4 + k) + 5 + t + 1)
                    nc.scalar.copy(vrows[0:P, t, k * W:(k + 1) * W], bank[t][128 - P:128, :]).then_inc(z_used, 1)
                if k == 0:
                    wq_hi(11)
            act.wait_ge(cT_ps, 1)
            nc.scalar.copy(negcT[0:8], bank[6][0:8, :]).then_inc(cT_sb, 1)
            for u in range(0, 16, 2):
                blk, c = u // 4, u % 4
                dst = qkT[:, 8 * (blk % 2) + 4 * (blk // 2) + c]
                sc = 1.0 if blk % 2 == 0 else HD ** -0.5
                act.wait_ge(tr_ps, u + 1)
                b0 = 2 * (u % 3)
                nc.scalar.activation(dst[:, 0:TP], bank[b0][:, :], ACT.Copy, scale=sc)
                nc.scalar.activation(dst[:, TP:T], bank[b0 + 1][:, 0:TS], ACT.Copy, scale=sc).then_inc(tr_a, 1)
            act.wait_ge(st_k, 16 * 4)
            act.wait_ge(sts, 16 * 5)
            for h in range(H):
                act.wait_ge(cb_ps, h + 1)
                nc.scalar.copy(negc[:, h], bank[6 + h % 2][:, :]).then_inc(cb_sb, 1)

            def outT(p, i):
                n = 4 * p + i
                act.wait_ge(at_ps, n + 1)
                nc.scalar.copy(AT[:, p // 4, p % 4, i * 128:(i + 1) * 128],
                               bank[6 + i % 2][:, 0:128]).then_inc(at_ok, 1)

            def step(p, u, first=False, last=False):
                if not last:
                    i = u // 2
                    N = 128 * (i + 1)
                    act.wait_ge(s_nm, 8 * p + u + 1)
                    nc.scalar.activation(PP[:, u % 2, 0:N], PP[:, u % 2, 0:N], ACT.Exp, bias=negm[:, u % 4],
                                         accum_out=rs[:, u % 4]).then_inc(p_ok, 1)
                if (u - 1) % 2 == 0 and not (first and u < 1):
                    N = 128 * ((u - 1) // 2 + 1)
                    act.wait_ge(pt_ps, 8 * p + u)
                    nc.scalar.copy(PTs[:, 0, 0:N], bank[2][:, 0:N]).then_inc(pt_a, 1)
                if (u - 4) % 2 == 1 and not (first and u < 5):
                    v = (u - 4) % 8
                    outT(p if u >= 4 else p - 1, v // 2)
            for p in range(8):
                for u in range(8):
                    step(p, u, first=p == 0)
            for u in (1, 3):
                outT(7, (u + 4) // 2)
            def w_hi(c, s, first=False):
                act.wait_ge(w_in_[s], 32 * (c // 4) + 32 if isinstance(c, int) else 8 * (c - s) + 32)
                if not first:
                    act.wait_ge(prod_ps, 2 * c - 2)
                nc.scalar.copy(WS[:, s % 2, 0], WR[:, s]).then_inc(wh_ok, 1)

            def gate(b, s, hf):
                act.wait_ge(prod_ps, 4 * b + 2 * s + hf + 1)
                act.wait_ge(c_in, 16)
                nc.scalar.copy(zg[:, ds(2 * b + s, 1), hf * HALF:(hf + 1) * HALF].rearrange("p a n -> p (a n)"),
                               bank[6 + hf][:, 0:HALF]).then_inc(g_ok, 1)

            act.wait_ge(z_init, 8)
            w_hi(0, 0, True)
            w_hi(1, 1, True)
            with act.Fori(0, DB // 2) as i:
                for e in range(2):
                    b = 2 * i + e
                    for ch in range(0, NALL, 2):
                        act.wait_ge(kt_ps, b * NALL + ch + 1)
                        nc.scalar.copy(KTs[:, ch % 3], bank[TB[ch % 3]][:, :]).then_inc(kt_a, 1)
                    gate(b, 0, 0)
                    gate(b, 0, 1)
                    w_hi(4 * i + 2 * e + 2, (2 * e + 2) % 4)
                    gate(b, 1, 0)
                    act.wait_ge(sub_ok, 2 * b + 2)
                    nc.scalar.activation(S1, S1, ACT.Exp).then_inc(sp_ok, 1)
                    gate(b, 1, 1)
                    w_hi(4 * i + 2 * e + 3, (2 * e + 3) % 4)
            for k in range(2 * NPAIR):
                hi(Ahl[:, 0, k], AT[:, k // NPAIR, k % NPAIR], sat_ok, 4 * DB, ah_ok)
            for m in range(8):
                if m == 0:
                    act.wait_ge(g_ok, 4 * DB)
                nc.scalar.activation(zg[:, m:m + 9:8, :], zg[:, m:m + 9:8, :], ACT.Sigmoid).then_inc(sg_ok, 1)
            for m in range(8):
                w_hi(18 + m, (18 + m) % 4)
                hi(X2[:, 0, m], tmpM[:, m % 2], mt_ok, m + 1, mh_ok)
            for c in range(26, 34):
                w_hi(c, c % 4)
            for m in range(8):
                act.wait_ge(h_ok, m + 1)
                if m >= 2:
                    act.wait_ge(sq2_used, m - 1)
                nc.scalar.activation(sq2[:, m % 2], xT[:, m], ACT.Square).then_inc(sq2_ok, 1)
            stds(sq2_used, std2_ok, std2)
            for k in range(KT):
                hi(X2[:, 0, k], tmpM[:, k % 2], ut_ok, k + 1, uh_ok)

            def d_hi(n):
                s = n % 2
                act.wait_ge(wd_in[s], 16 * (n // 2) + 16)
                if n >= 2:
                    act.wait_ge(d_ps, n - 1)
                else:
                    act.wait_ge(prod_ps, 2 * 76)
                nc.scalar.copy(WSD[:, s, 0], WDr[:, s].rearrange("p k n -> p (k n)")).then_inc(dh_ok, 1)

            def silu(m, s, last=False):
                c = 32 + 2 * m
                act.wait_ge(prod_ps, 2 * c + 2)
                for hf in range(2):
                    nc.scalar.activation(sg[:, s, hf * HALF:(hf + 1) * HALF], bank[4 * s + hf][:, 0:HALF], ACT.Sigmoid).then_inc(sil_ok, 1)
                if not last:
                    w_hi(c + 2, (2 * s + 2) % 4)
                act.wait_ge(ht_ok, m + 1)
                act.wait_ge(c_in, 16)
                nc.scalar.copy(Hhl[:, 0, ds(m, 1)].rearrange("p a n -> p (a n)"), tmpH).then_inc(hh_ok, 1)
                if not last:
                    w_hi(c + 3, (2 * s + 3) % 4)
            with act.Fori(0, KF // 2 - 1) as i:
                for s in range(2):
                    silu(2 * i + s, s)
            silu(KF - 2, 0)
            silu(KF - 1, 1, last=True)
            d_hi(0)
            d_hi(1)

            def yrows(m, s, warm):
                act.wait_ge(yt_ps, m + 1)
                if warm:
                    act.wait_ge(y_st[s], 32 * (m // 2) if isinstance(m, int) else 0)
                nc.scalar.copy(yst[:, s, 0:4, :], bank[4 + 2 * s][:, :].rearrange("p (t n) -> p t n", n=128))
                nc.scalar.copy(yst[0:TS, s, 4, :], bank[5 + 2 * s][0:TS, 0:128]).then_inc(yst_ok, 1)
                act.wait_ge(yst_ok, m + 1)
                act.dma_start(yp_v[:, :, ds(m * 128, 128)], yst[:, s, 0:4, :]).then_inc(y_st[s], 16)
                act.dma_start(ys_v[:, ds(m * 128, 128)], yst[0:TS, s, 4, :]).then_inc(y_st[s], 16)
            for m in range(8):
                for n in (2 * m + 2, 2 * m + 3):
                    if n < 16:
                        d_hi(n)
                if m >= 1:
                    yrows(m - 1, (m - 1) % 2, m >= 3)
            yrows(7, 1, True)
            for s in range(2):
                act.wait_ge(y_st[s], 32 * 4)

        @block.vector
        def _(dve):
            V = nc.vector
            for k in range(KT):
                dve.wait_ge(xT_ps, k + 1)
                V.tensor_copy(xT[:, k, 0:TP], bank[2 * (k % 2)][:, :])
                V.tensor_copy(xT[:, k, TP:T], bank[2 * (k % 2) + 1][:, 0:TS]).then_inc(xT_sb, 1)

            def lo(dst, whole, part, done_hi, n, done):
                dve.wait_ge(done_hi, n)
                V.tensor_tensor(dst, whole, part.bitcast(f32), ALU.subtract).then_inc(done, 1)

            def scaled(std, rok, ok, g, src, sdt, tmp, whole_ok, hi_ok):
                dve.wait_ge(std, 2)
                V.reciprocal(sdt, sdt).then_inc(rok, 1)
                dve.wait_ge(rok, 1)
                for k in range(KT + 1):
                    if k < KT:
                        if k >= 2:
                            dve.wait_ge(ok, k - 1)
                        V.scalar_tensor_tensor(tmp[:, k % 2], src[:, k], g[:, k:k + 1], sdt, ALU.mult, ALU.mult).then_inc(whole_ok, 1)
                    if k >= 1:
                        lo(X2[:, 1, k - 1], tmp[:, (k - 1) % 2], X2[:, 0, k - 1], hi_ok, k, ok)
            dve.wait_ge(xT_sb, KT)
            dve.wait_ge(c_in, 16 * N_CONST)
            lo(wfs[:, 1], wf, wfs[:, 0], wfh_ok, 1, wfl_ok)
            scaled(std_ok, rstd_ok, xn_ok, g1, xT, rstd, tmpA, xt_ok, xh_ok)
            wq_lo = lambda n: lo(WQs[:, n % 2, 1], WQ[:, n % 2], WQs[:, n % 2, 0], wqh_ok, n + 1, wql_ok)
            wq_lo(0)
            wq_lo(1)
            dve.wait_ge(f_ps, 1)
            dve.wait_ge(z_init, 3)
            fp = bank[5][:, 0:40].rearrange("p (t h) -> p t h", h=H)
            bfb = bf.rearrange("p (a h) -> p a h", a=1)
            V.tensor_tensor(lfx[:, 0:4], fp[:, 0:4], bfb.to_broadcast([128, 4, H]), ALU.add).then_inc(lfx_ok, 1)
            V.tensor_tensor(lfx[0:TS, 4], fp[96:128, 4], bf[96:128], ALU.add).then_inc(lfx_ok, 1)
            dve.wait_ge(lfx_ok, 2)
            V.scalar_tensor_tensor(lfe, lfx, -1.0, lfx, ALU.mult, ALU.max).then_inc(lfx_ok, 1)
            V.tensor_scalar(lfa, lfx, 0.0, None, ALU.min).then_inc(lf_ok, 1)
            dve.wait_ge(lf_ok, 1)
            dve.wait_ge(lfe_ok, 2)
            V.tensor_tensor(lfx, lfa, lfe, ALU.subtract).then_inc(lf_ok, 2)

            def norm_block(blk, rope, i0):
                wq_lo(2 * blk + 2)
                for t in range(5):
                    P = PT_[t]
                    dve.wait_ge(zs_ok, 5 * blk + t + 1)
                    V.reduce_sum(ssum[0:P, blk, t, :], sq[0:P, t % 2, 0:W].rearrange("p (h d) -> p h d", d=HD), AX.X).then_inc(zs_sum, 1)
                wq_lo(2 * blk + 3)
                dve.wait_ge(zs_std, blk + 1)
                V.reciprocal(ssum[:, blk], ssum[:, blk]).then_inc(zs_inv, 1)
                dve.wait_ge(zs_inv, blk + 1)
                n = i0
                for t in range(5):
                    P = PT_[t]
                    r = rows[0:P, blk, t, :].rearrange("p (h d) -> p h d", d=HD)
                    inv = ssum[0:P, blk, t, :].rearrange("p (h e) -> p h e", e=1)
                    g = gains[0:P, blk:blk + 1, :]
                    V.tensor_tensor(r, r, inv.to_broadcast([P, H, HD]), ALU.mult).then_inc(row_s, 1)
                    n = n + 1
                    dve.wait_ge(row_s, n)
                    if not rope:
                        V.tensor_tensor(r, r, g.to_broadcast([P, H, HD]), ALU.mult).then_inc(row_ok, 1)
                        continue
                    V.tensor_tensor(r, r, g.to_broadcast([P, H, HD]), ALU.mult).then_inc(row_s, 1)
                    n = n + 1
                    dve.wait_ge(row_s, n)
                    a, bb = [rt[0:P, e].rearrange("p (h d) -> p h d", d=HD) for e in range(2)]
                    V.tensor_tensor(a, r, cosr[0:P, t:t + 1, :].to_broadcast([P, H, HD]), ALU.mult).then_inc(row_s, 1)
                    for e in range(2):
                        V.tensor_tensor(bb[:, :, 32 * e:32 * e + 32], r[:, :, 32 - 32 * e:64 - 32 * e],
                                        sinr[0:P, t:t + 1, 32 * e:32 * e + 32].to_broadcast([P, H, 32]), ALU.mult).then_inc(row_s, 1)
                    n = n + 3
                    dve.wait_ge(row_s, n)
                    V.tensor_tensor(r, a, bb, ALU.add).then_inc(row_ok, 1)
                return n
            n = 0
            for blk in range(4):
                n = norm_block(blk, blk >= 2, n)
            wq_lo(10)
            wq_lo(11)
            for u in range(1, 16, 2):
                blk, c = u // 4, u % 4
                dst = qkT[:, 8 * (blk % 2) + 4 * (blk // 2) + c]
                sc = 1.0 if blk % 2 == 0 else HD ** -0.5
                dve.wait_ge(tr_ps, u + 1)
                b0 = 2 * (u % 3)
                V.tensor_scalar(dst[:, 0:TP], bank[b0][:, :], sc, None, ALU.mult)
                V.tensor_scalar(dst[:, TP:T], bank[b0 + 1][:, 0:TS], sc, None, ALU.mult).then_inc(tr_v, 1)
            dve.wait_ge(nd_ok, H)
            dve.wait_ge(cb_sb, H)

            def step(p, u, kind, first=False, last=False):
                if not last:
                    i, j, e = u // 2, u % 2, u % 4
                    N = 128 * (i + 1)
                    n = 8 * p + u
                    dve.wait_ge(s_ps, n + 1)
                    if not (first and u < 2):
                        dve.wait_ge(pt_ps, n - 1)
                    mxs = (14 * p + sum(2 if v >= 2 else 1 for v in range(u))) if kind == FOX else (56 + 8 * (p - 4) + u)
                    if kind == FOX:
                        h = 2 * p + j
                        V.tensor_tensor_reduce(PP[:, u % 2, i * 128:N], bank[u % 2][:, i * 128:N],
                                               ndiag[:, h, i, :],
                                               1.0, NEG, ALU.add, ALU.max, mx[:, e]).then_inc(s_mx, 1)
                        mxs = mxs + 1
                        last_mx = mx
                        if i > 0:
                            dve.wait_ge(s_mx, mxs)
                            V.tensor_tensor_reduce(PP[:, u % 2, 0:i * 128], bank[u % 2][:, 0:i * 128],
                                                   negc[:, h, 0:i * 128],
                                                   1.0, mx[:, e], ALU.add, ALU.max, mx2[:, e]).then_inc(s_mx, 1)
                            mxs = mxs + 1
                            last_mx = mx2
                    else:
                        V.tensor_tensor_reduce(PP[:, u % 2, 0:N], bank[u % 2][:, 0:N], logc[:, (3 - i) * 128:512],
                                               1.0, NEG, ALU.add, ALU.max, mx[:, e]).then_inc(s_mx, 1)
                        mxs = mxs + 1
                        last_mx = mx
                    dve.wait_ge(s_mx, mxs)
                    V.tensor_scalar(negm[:, e], last_mx[:, e], -1.0, None, ALU.mult).then_inc(s_nm, 1)
                if (u - 1) % 2 == 1 and not (first and u < 1):
                    v = (u - 1) % 8
                    N = 128 * (v // 2 + 1)
                    dve.wait_ge(pt_ps, 8 * p + u)
                    V.tensor_copy(PTs[:, 1, 0:N], bank[3][:, 0:N]).then_inc(pt_v, 1)
                if not (first and u < 2):
                    v = (u - 2) % 8
                    n = 8 * p + u - 2
                    V.reciprocal(rinv[:, v % 4], rs[:, v % 4]).then_inc(r_ok, 1)
                    dve.wait_ge(r_ok, n + 1)
                    dve.wait_ge(o_ps, n + 1)
                    if not (first and u < 6):
                        dve.wait_ge(at_ps, (8 * p + u - 2 - v % 2) // 2 - 1)
                    V.tensor_scalar(Arow[:, (v // 2) % 2, 64 * (v % 2):64 * (v % 2) + 64], bank[4 + v % 2][:, 0:HD], rinv[:, v % 4], None, ALU.mult).then_inc(a_ok, 1)
            for p in range(8):
                for u in range(8):
                    step(p, u, FOX if p < 4 else DSW, first=p == 0)
            for u in range(2):
                step(8, u, DSW, last=True)

            hq = lambda a: a.rearrange("p c (h q) -> p c h q", q=DS)
            part = [slice(0, NCH[0]), slice(NCH[0], NALL)]

            def own(k, j):
                at = 32 * k + DS * j
                return bank[3][64 * j:64 * j + 64, :].rearrange("p (c x) -> p c x", x=128)[:, :, at:at + DS]
            def w_lo(c, s):
                dve.wait_ge(wh_ok, c + 1)
                V.tensor_tensor(WS[:, s % 2, 1], WR[:, s], WS[:, s % 2, 0].bitcast(f32), ALU.subtract).then_inc(wl_ok, 1)

            dve.wait_ge(z_init, 8)
            w_lo(0, 0)
            w_lo(1, 1)

            def batch(b, e):
                dve.wait_ge(cc_ps, b + 1)
                V.tensor_copy(cneg, bank[5][:, 0:72].rearrange("p (c h) -> p c h", h=H)).then_inc(cc_ok, 1)
                for ch in range(1, NALL, 2):
                    dve.wait_ge(kt_ps, b * NALL + ch + 1)
                    V.tensor_copy(KTs[:, ch % 3], bank[TB[ch % 3]][:, :]).then_inc(kt_v, 1)
                dve.wait_ge(cc_ok, b + 1)
                dve.wait_ge(sc_ps, b + 1)
                sc = hq(bank[2][:, 0:NALL * 32].rearrange("p (c n) -> p c n", n=32))
                V.tensor_tensor(hq(S1)[:, part[0]], sc[:, part[0]], cneg.rearrange("p c (h e) -> p c h e", e=1).to_broadcast([128, NCH[0], H, DS]), ALU.add).then_inc(s1_ok, 1)
                V.tensor_tensor(hq(S1)[:, part[1]], sc[:, part[1]], dmask.rearrange("p c (e q) -> p c e q", e=1).to_broadcast([128, NCH[1], H, DS]), ALU.add).then_inc(s1_ok, 1)
                dve.wait_ge(s1_ok, 3 * b + 1)
                V.tensor_tensor(hq(S1)[:, NPG], hq(S1)[:, NPG], fmask.rearrange("p (a q) -> p a q", a=1).to_broadcast([128, H, DS]), ALU.add).then_inc(s1_ok, 1)
                dve.wait_ge(s1_ok, 3 * b + 3)
                for k in range(2):
                    V.reduce_max(mp[:, 32 * k:32 * k + 32], S1[:, part[k]].rearrange("p c n -> p n c"), AX.X).then_inc(mp_ok, 1)
                w_lo(2 * b + 2, (2 * e + 2) % 4)
                dve.wait_ge(mt_ps, b + 1)
                V.reduce_max(mcol[0:64], bank[5][0:64, 0:128], AX.X).then_inc(m_col, 1)
                dve.wait_ge(m_col, b + 1)
                V.tensor_scalar(dg[0:64], ident[0:64, 0:64], mcol[0:64], None, ALU.mult).then_inc(dg_ok, 1)
                dve.wait_ge(mb_ps, b + 1)
                for k in range(2):
                    V.tensor_tensor(S1[:, part[k]], S1[:, part[k]], bank[5][:, 32 * k:32 * k + 32].rearrange("p (a n) -> p a n", a=1).to_broadcast([128, NCH[k], 32]), ALU.subtract).then_inc(sub_ok, 1)
                dve.wait_ge(sp_ok, b + 1)
                for k in range(2):
                    V.reduce_sum(ps_[:, 32 * k:32 * k + 32], S1[:, part[k]].rearrange("p c n -> p n c"), AX.X).then_inc(sum_ok, 1)
                w_lo(2 * b + 3, (2 * e + 3) % 4)
                dve.wait_ge(so_ps, b + 1)
                V.reciprocal(ri[0:64], bank[5][0:64, 0:1]).then_inc(ri_ok, 1)
                dve.wait_ge(ri_ok, b + 1)
                V.tensor_scalar(onr[0:64], bank[4][0:64, :], ri[0:64], None, ALU.mult).then_inc(on_ok, 1)
                dve.wait_ge(ot_ps, b + 1)
                for k in range(2):
                    for j in range(2):
                        V.tensor_copy(AT[64 * j:64 * j + 64, k, :, ds(TP + b * DS, DS)], own(k, j)).then_inc(sat_ok, 1)

            with dve.Fori(0, DB // 2) as i:
                for e in range(2):
                    batch(2 * i + e, e)
            for k in range(2 * NPAIR):
                lo(Ahl[:, 1, k], AT[:, k // NPAIR, k % NPAIR], Ahl[:, 0, k], ah_ok, k + 1, al_ok)

            for m in range(8):
                c0, b0 = 16 + m, 4 * (m % 2)
                dve.wait_ge(prod_ps, 2 * c0 + 2)
                dve.wait_ge(sg_ok, m + 1)
                if m >= 1:
                    dve.wait_ge(mt_ok, m)
                for k in range(2):
                    for hf in range(2):
                        c = slice(hf * HALF, (hf + 1) * HALF)
                        V.tensor_tensor(tg[:, k, c], zg[:, m + 8 * k, c], bank[b0 + 2 * k + hf][:, 0:HALF], ALU.mult).then_inc(tg_ok, 1)
                w_lo(18 + m, (18 + m) % 4)
                dve.wait_ge(tg_ok, 4 * m + 4)
                V.tensor_tensor(tmpM[:, m % 2], tg[:, 0], tg[:, 1], ALU.add).then_inc(mt_ok, 1)
                lo(X2[:, 1, m], tmpM[:, m % 2], X2[:, 0, m], mh_ok, m + 1, m_ok)
            for m in range(8):
                b0 = 2 * (m % 2)
                if m < 6:
                    w_lo(26 + m, (26 + m) % 4)
                dve.wait_ge(prod_ps, 2 * (24 + m) + 2)
                for hf in range(2):
                    c = slice(hf * HALF, (hf + 1) * HALF)
                    i = V.tensor_tensor(xT[:, m, c], xT[:, m, c], bank[b0 + hf][:, 0:HALF], ALU.add)
                i.then_inc(h_ok, 1)
            w_lo(32, 0)
            w_lo(33, 1)
            dve.wait_ge(h_ok, KT)
            scaled(std2_ok, rstd2_ok, u_ok, g2, xT, std2, tmpM, ut_ok, uh_ok)

            def hidden(m, s, last=False):
                b0, c0 = 4 * s, 32 + 2 * m
                dve.wait_ge(sil_ok, 2 * m + 2)
                for hf in range(2):
                    c = slice(hf * HALF, (hf + 1) * HALF)
                    V.tensor_tensor(sg[:, s, c], sg[:, s, c], bank[b0 + hf][:, 0:HALF], ALU.mult).then_inc(gm_ok, 1)
                if not last:
                    w_lo(c0 + 2, (2 * s + 2) % 4)
                dve.wait_ge(gm_ok, 2 * m + 2)
                dve.wait_ge(prod_ps, 2 * c0 + 4)
                for hf in range(2):
                    c = slice(hf * HALF, (hf + 1) * HALF)
                    i = V.tensor_tensor(tmpH[:, c], sg[:, s, c], bank[b0 + 2 + hf][:, 0:HALF], ALU.mult)
                i.then_inc(ht_ok, 1)
                dve.wait_ge(hh_ok, m + 1)
                V.tensor_tensor(Hhl[:, 1, ds(m, 1)].rearrange("p a n -> p (a n)"), tmpH,
                                Hhl[:, 0, ds(m, 1)].rearrange("p a n -> p (a n)").bitcast(f32), ALU.subtract).then_inc(hid_ok, 1)
                dve.wait_ge(hid_ok, m + 1)
                if not last:
                    w_lo(c0 + 3, (2 * s + 3) % 4)
            with dve.Fori(0, KF // 2 - 1) as i:
                for s in range(2):
                    hidden(2 * i + s, s)
            hidden(KF - 2, 0)
            hidden(KF - 1, 1, last=True)
            d_lo = lambda n: lo(WSD[:, n % 2, 1], WDr[:, n % 2].rearrange("p k n -> p (k n)"), WSD[:, n % 2, 0], dh_ok, n + 1, dl_ok)
            d_lo(0)
            d_lo(1)
            for m in range(8):
                for n in (2 * m + 2, 2 * m + 3):
                    if n < 16:
                        d_lo(n)
                dve.wait_ge(d_ps, 2 * m + 2)
                if m >= 2:
                    dve.wait_ge(yt_ps, m - 1)
                for hf in range(2):
                    c = slice(hf * HALF, (hf + 1) * HALF)
                    i = V.tensor_tensor(yT[:, m % 2, c], xT[:, m, c], bank[2 * (m % 2) + hf][:, 0:HALF], ALU.add)
                i.then_inc(y_ok, 1)

        @block.tensor
        def _(pe):
            mm = nc.tensor.matmul

            def halves(banks, w, src, ks, done, first=True, last=True):
                for hf in range(2):
                    for n, (a, b) in enumerate(PASSES):
                        for e, k in enumerate(ks):
                            x = mm(banks[hf][:, 0:HALF], w(a, e), src[:, b, k, hf * HALF:(hf + 1) * HALF],
                                   start=(first and n == 0 and e == 0), stop=(last and n == 2 and e == len(ks) - 1))
                    if done is not None:
                        x.then_inc(done, 1)
                return x

            pe.wait_ge(c_in, 16 * N_CONST)
            pe.wait_ge(x_in, 32)
            for k in range(KT):
                if k >= 2:
                    pe.wait_ge(xT_sb, k - 1)
                for t in range(4):
                    nc.tensor.transpose(bank[2 * (k % 2)][:, t * 128:(t + 1) * 128], xrow[:, t, k * 128:(k + 1) * 128], ident)
                nc.tensor.transpose(bank[2 * (k % 2) + 1][:, 0:TS], xrow[0:TS, 4, k * 128:(k + 1) * 128], ident[0:TS, 0:TS]).then_inc(xT_ps, 1)

            def mean_square(ok, used, src):
                for k in range(KT):
                    pe.wait_ge(ok, k + 1)
                    for hf in range(2):
                        i = mm(bank[6 + hf][:, 0:HALF], mean1, src[:, k % 2, hf * HALF:(hf + 1) * HALF], start=(k == 0), stop=(k == KT - 1))
                    i.then_inc(used, 1)
            mean_square(sq_ok, sq_used, sq)
            tile = [slice(t * 128, t * 128 + 128) for t in range(4)] + [slice(T - 128, T)]
            pe.wait_ge(xn_ok, KT)
            pe.wait_ge(wfl_ok, 1)
            for t in range(5):
                for n, (a, b) in enumerate(PASSES):
                    for k in range(KT):
                        i = mm(bank[5][:, 8 * t:8 * t + 8], X2[:, a, k, tile[t]], wfs[:, b, k, :], start=(n == 0 and k == 0), stop=(n == 2 and k == KT - 1))
            i.then_inc(f_ps, 1)

            def qkv(blk, first):
                for kh in range(2):
                    pe.wait_ge(wql_ok, 2 * blk + kh + 1)
                    for t in range(5):
                        if not first and kh == 0:
                            pe.wait_ge(z_used, 5 * blk + t - 4)
                        for n, (a, b) in enumerate(PASSES):
                            for k in range(4):
                                x = mm(bank[t][:, :], X2[:, a, 4 * kh + k, tile[t]], WQs[:, kh, b, k, :],
                                       start=(kh == 0 and n == 0 and k == 0), stop=(kh == 1 and n == 2 and k == 3))
                        x.then_inc(z_ps, 1)
            qkv(0, True)
            with pe.Fori(1, 6) as blk:
                qkv(blk, False)
            pe.wait_ge(lf_ok, 3)
            for j in range(4):
                i = mm(bank[6][0:8, :], lfx[:, j, :], ntri[:, 384 - 128 * j:896 - 128 * j], start=(j == 0), stop=(j == 3))
            i.then_inc(cT_ps, 1)
            for u in range(16):
                blk, c = u // 4, u % 4
                b0 = 2 * (u % 3)
                if c == 0:
                    pe.wait_ge(row_ok, 5 * blk + 5)
                if u == 0:
                    pe.wait_ge(z_used, 30)
                if u >= 3:
                    pe.wait_ge(tr_v if u % 2 == 0 else tr_a, (u - 3) // 2 + 1)
                for t in range(4):
                    nc.tensor.transpose(bank[b0][:, t * 128:(t + 1) * 128], rows[:, blk, t, c * 128:(c + 1) * 128], ident)
                nc.tensor.transpose(bank[b0 + 1][:, 0:TS], rows[0:TS, blk, 4, c * 128:(c + 1) * 128], ident[0:TS, 0:TS]).then_inc(tr_ps, 1)
            pe.wait_ge(cT_sb, 1)
            for h in range(H):
                if h >= 2:
                    pe.wait_ge(cb_sb, h - 1)
                mm(bank[6 + h % 2][:, :], sel[0:8, h, :], negcT[0:8], start=True, stop=True).then_inc(cb_ps, 1)
            pe.wait_ge(tr_a, 8)
            pe.wait_ge(tr_v, 8)
            pe.wait_ge(cb_sb, 8)

            def step(p, u, first=False, last=False):
                if not last:
                    i, j = u // 2, u % 2
                    N = 128 * (i + 1)
                    n = 8 * p + u
                    if not (first and u < 2):
                        pe.wait_ge(s_nm, n - 1)
                    mm(bank[u % 2][:, 0:N], qkT[64 * j:64 * j + 64, 8 + p, i * 128:(i + 1) * 128], qkT[64 * j:64 * j + 64, p, 0:N],
                       start=True, stop=True).then_inc(s_ps, 1)
                if not (first and u < 1) and not (last and u > 0):
                    v = (u - 1) % 8
                    n = 8 * p + u - 1
                    pe.wait_ge(p_ok, n + 1)
                    if not (first and u < 3):
                        e = (8 * p + u - 1 - v % 2) // 2
                        pe.wait_ge(pt_v if v % 2 else pt_a, e)
                    for c in range(v // 2 + 1):
                        x = nc.tensor.transpose(bank[2 + v % 2][:, c * 128:(c + 1) * 128], PP[:, v % 2, c * 128:(c + 1) * 128], ident)
                    x.then_inc(pt_ps, 1)
                if not (first and u < 2):
                    v = (u - 2) % 8
                    n = 8 * p + u - 2
                    e = (8 * p + u - 2 - v % 2) // 2
                    pe.wait_ge(pt_v if v % 2 else pt_a, e + 1)
                    if not (first and u < 4):
                        pe.wait_ge(a_ok, n - 1)
                    hcol = (2 * p + (v % 2)) * HD if u >= 2 else (2 * (p - 1) + (v % 2)) * HD
                    for c in range(v // 2 + 1):
                        x = mm(bank[4 + v % 2][:, 0:HD], PTs[:, v % 2, c * 128:(c + 1) * 128], vrows[:, c, hcol:hcol + HD], start=(c == 0), stop=(c == v // 2))
                    x.then_inc(o_ps, 1)
                if (u - 3) % 2 == 1 and not (first and u < 4):
                    block_out(p if u >= 4 else p - 1, ((u - 3) % 8) // 2, first)

            def block_out(p, i, first=False):
                pe.wait_ge(a_ok, 8 * p + 2 * i + 2)
                if not (first and i < 2):
                    pe.wait_ge(at_ok, 4 * p + i - 1)
                nc.tensor.transpose(bank[6 + i % 2][:, 0:128], Arow[:, i % 2, :], ident).then_inc(at_ps, 1)
            for p in range(8):
                for u in range(8):
                    step(p, u, first=p == 0)
            for u in range(2):
                step(8, u, last=True)
            block_out(7, 3)

            pe.wait_ge(at_ok, 32)
            pe.wait_ge(z_init, 8)
            pe.wait_ge(Qs_ok, 4)

            def keys_T(b, ch, first):
                if ch >= 3:
                    if ch % 2:
                        pe.wait_ge(kt_a, 8 * b + (ch - 3) // 2 + 1)
                    else:
                        pe.wait_ge(kt_v, 7 * b + (ch - 3) // 2 + 1)
                elif not first:
                    if ch == 2:
                        pe.wait_ge(sat_ok, 4 * b)
                    pe.wait_ge(kt_v if ch == 1 else kt_a, (8 * b - 1, 7 * b, 8 * b)[ch])
                pe.wait_ge(k_in[ch % NKR], 16 * (NALL // NKR * b + ch // NKR) + 16)
                for c in range(NPAIR):
                    x = nc.tensor.transpose(bank[TB[ch % 3]][:, c * 128:(c + 1) * 128], Kr[:, ch % NKR, c * 128:(c + 1) * 128], ident)
                x.then_inc(kt_ps, 1)

            def scores(b, ch):
                pe.wait_ge(kt_v if ch % 2 else kt_a, (7 if ch % 2 else 8) * b + ch // 2 + 1)
                k = 0 if ch < NCH[0] else 1
                for c in range(NPAIR):
                    x = mm(bank[2][:, ch * 32 + c * 8:ch * 32 + c * 8 + 8], KTs[:, ch % 3, c * 128:(c + 1) * 128],
                           Qs[:, k, ds(b, 1), c].rearrange("p a j q -> p (a j q)"), start=True, stop=True)
                return x

            def gate_wait(b, s, hf, first):
                if hf == 0:
                    pe.wait_ge(wl_ok, 2 * b + s + 1)
                if not (first and s == 0):
                    pe.wait_ge(g_ok, 4 * b + 2 * s + hf - 1)

            def gate(s, n):
                hf, p, k = n // 24, n // 8 % 3, n % 8
                a, b = PASSES[p]
                x = mm(bank[6 + hf][:, 0:HALF], WS[:, s, a, k * 128:(k + 1) * 128], X2[:, b, k, hf * HALF:(hf + 1) * HALF], start=(n % 24 == 0), stop=(n % 24 == 23))
                if n % 24 == 23:
                    x.then_inc(prod_ps, 1)

            def batch(b, first):
                pe.wait_ge(l_in, 16 * 9 * (b + 1))
                if not first:
                    pe.wait_ge(sub_ok, 2 * b)
                mm(bank[5][:, 0:72], ntri[:, 384:512], lfp.rearrange("p c h -> p (c h)"), start=True, stop=False)
                for c in range(NPG):
                    x = mm(bank[5][:, 8 * (c + 1):72].rearrange("p (c h) -> p c h", h=H), ntri[:, 768:896],
                           lfp[:, c:c + 1, :].to_broadcast([128, NPG - c, H]), start=False, stop=(c == NPG - 1))
                x.then_inc(cc_ps, 1)
                keys_T(b, 0, first)
                keys_T(b, 1, first)
                gate_wait(b, 0, 0, first)
                gate_wait(b, 0, 1, first)
                if not first:
                    pe.wait_ge(s1_ok, 3 * b - 1)
                for ch in range(NALL):
                    if ch + 2 < NALL:
                        keys_T(b, ch + 2, first)
                    for n in range(3):
                        gate(0, 3 * ch + n)
                    x = scores(b, ch)
                x.then_inc(sc_ps, 1)
                for n in range(45, 48):
                    gate(0, n)
                gate_wait(b, 1, 0, first)
                for n in range(24):
                    gate(1, n)
                pe.wait_ge(mp_ok, 2 * b + 2)
                nc.tensor.transpose(bank[5][:, 0:128], mp, ident).then_inc(mt_ps, 1)
                gate_wait(b, 1, 1, first)
                for n in range(24, 36):
                    gate(1, n)
                pe.wait_ge(dg_ok, b + 1)
                mm(bank[5][:, 0:64], ones[0:64], dg[0:64], start=True, stop=True).then_inc(mb_ps, 1)
                for n in range(36, 48):
                    gate(1, n)
                pe.wait_ge(sum_ok, 2 * b + 2)
                if not first:
                    pe.wait_ge(sat_ok, 4 * b)
                mm(bank[5][0:64, 0:1], ps_, ones[:, 0:1], start=True, stop=True)
                pe.wait_ge(vf_in, 16 * NCH[0] * (b + 1))
                pe.wait_ge(vd_in, 16 * NCH[1] * (b + 1))
                for k in range(2):
                    for ch in range(NCH[k]):
                        x = mm(bank[4][32 * k:32 * k + 32, :], S1[:, ch + k * NCH[0]], (Vf, Vd)[k][:, ch, :], start=(ch == 0), stop=(ch == NCH[k] - 1))
                x.then_inc(so_ps, 1)
                pe.wait_ge(on_ok, b + 1)
                for c in range(NPAIR):
                    x = nc.tensor.transpose(bank[3][:, c * 120:c * 120 + 128], onr[:, c * 128:(c + 1) * 128], ident)
                x.then_inc(ot_ps, 1)
            batch(0, True)
            with pe.Fori(1, DB) as b:
                batch(b, False)

            pe.wait_ge(sat_ok, 4 * DB)
            pe.wait_ge(g_ok, 4 * DB)
            pe.wait_ge(al_ok, 2 * NPAIR)

            def merged(m, s, first):
                pe.wait_ge(wl_ok, 16 + m + 1)
                if not first:
                    pe.wait_ge(tg_ok, 4 * m - 4)
                for hf in range(2):
                    for k in range(2):
                        for n, (a, b) in enumerate(PASSES):
                            for e in range(NPAIR):
                                x = mm(bank[4 * s + 2 * k + hf][:, 0:HALF], WS[:, s, a, (4 * k + e) * 128:(4 * k + e + 1) * 128],
                                       Ahl[:, b, 4 * k + e, hf * HALF:(hf + 1) * HALF], start=(n == 0 and e == 0), stop=(n == 2 and e == NPAIR - 1))
                    x.then_inc(prod_ps, 1)
            for m in range(2):
                merged(m, m, True)
            with pe.Fori(1, 4) as i:
                for s in range(2):
                    merged(2 * i + s, s, False)
            pe.wait_ge(m_ok, 8)
            ring_w = lambda s: (lambda a, k: WS[:, s, a, k * 128:(k + 1) * 128])

            def out_proj(m, s, first):
                pe.wait_ge(wl_ok, 24 + m + 1)
                if not first:
                    pe.wait_ge(h_ok, m - 1)
                halves(bank[2 * s:2 * s + 2], ring_w(s), X2, range(KT), prod_ps)
            for m in range(2):
                out_proj(m, m, True)
            with pe.Fori(1, 4) as i:
                for s in range(2):
                    out_proj(2 * i + s, s, False)
            mean_square(sq2_ok, sq2_used, sq2)

            pe.wait_ge(u_ok, KT)
            def up(m, s, first):
                if not first:
                    pe.wait_ge(ht_ok, m - 1)
                for k in range(2):
                    pe.wait_ge(wl_ok, 32 + 2 * m + k + 1)
                    halves(bank[4 * s + 2 * k:4 * s + 2 * k + 2], ring_w(k), X2, range(KT), prod_ps)
            for m in range(2):
                up(m, m, True)
            with pe.Fori(1, KF // 2) as i:
                for s in range(2):
                    up(2 * i + s, s, False)
            pe.wait_ge(hid_ok, KF)

            def y_out(m):
                pe.wait_ge(y_ok, m + 1)
                if m >= 2:
                    pe.wait_ge(yst_ok, m - 1)
                b0 = 4 + 2 * (m % 2)
                for t in range(4):
                    nc.tensor.transpose(bank[b0][:, t * 128:(t + 1) * 128], yT[:, m % 2, t * 128:(t + 1) * 128], ident)
                nc.tensor.transpose(bank[b0 + 1][0:TS, 0:128], yT[:, m % 2, TP:T], ident).then_inc(yt_ps, 1)
            for m in range(8):
                if m >= 2:
                    pe.wait_ge(y_ok, m - 1)
                for kh in range(2):
                    pe.wait_ge(dl_ok, 2 * m + kh + 1)
                    halves(bank[2 * (m % 2):2 * (m % 2) + 2], lambda a, k: WSD[:, kh, a, k * 128:(k + 1) * 128], Hhl,
                           range(KD * kh, KD * kh + KD), None, first=(kh == 0), last=(kh == 1)).then_inc(d_ps, 1)
                if m >= 1:
                    y_out(m - 1)
            y_out(7)


_INS = ["x_prompt", "x_sample", "cache_k_fox", "cache_v_fox", "cache_logf_fox", "state_k_dsw", "state_v_dsw", "page_table",
        "norm1_g", "w_in", "b_f", "q_norm_fox", "k_norm_fox", "q_norm_dsw", "k_norm_dsw", "w_o_fox", "w_o_dsw", "w_out",
        "norm2_g", "w_gate", "w_up", "w_down"]


def constants():
    import numpy as np
    p = np.arange(128)
    c = np.zeros((128, C_END), np.float32)
    c[:, C_ID:C_ID + 128] = np.eye(128)
    c[:, C_MEAN:C_MEAN + 128] = 1.0 / D
    c[:, C_ONE:C_ONE + 128] = 1.0
    c[:, C_TRI:C_TRI + 128] = np.where(p[None, :] <= p[:, None], 0.0, NEG)
    c[:, C_NTRI:C_NTRI + 896] = np.where(np.arange(896)[None, :] - 384 >= p[:, None], -1.0, 0.0)

    def log_count(dist):
        n = ((dist >= 0) & (dist <= 128)) * 1 + ((dist >= 0) & (dist <= 512) & (dist % 4 == 0)) + ((dist >= 0) & (dist <= 2048) & (dist % 16 == 0))
        return np.where(n > 0, np.log(np.maximum(n, 1)), NEG)
    for s in range(4):
        c[:, C_LC + 128 * s:C_LC + 128 * (s + 1)] = log_count(128 * (3 - s) + p[:, None] - p[None, :])
    half = HD // 2
    inv = np.float32(10000.0) ** (-np.arange(half, dtype=np.float32) / np.float32(half))
    for t in range(5):
        pos = (128 * t + p) if t < 4 else PAST + p % DS
        ang = pos.astype(np.float32)[:, None] * inv.astype(np.float32)[None, :]
        co, si = np.cos(ang), np.sin(ang)
        c[:, C_COS + 64 * t:C_COS + 64 * t + 64] = np.concatenate([co, co], 1)
        c[:, C_SIN + 64 * t:C_SIN + 64 * t + 64] = np.concatenate([-si, si], 1)
    for ch in range(6):
        key = 512 + 128 * ch + p if ch < 4 else 16 * (p // 4) + p % 4 if ch == 4 else PAST + p
        for q in range(DS):
            v = log_count(PAST + q - key)
            c[:, C_DM + 4 * ch + q] = np.where(p < DS, v, NEG) if ch == 5 else v
    for q in range(DS):
        c[:, C_FM + q] = np.where((p < DS) & (p <= q), 0.0, NEG)
    s = np.zeros((8, 8, 128), np.float32)
    for h in range(8):
        s[h, h, :] = 1.0
    return c, s.reshape(8, 1024)


def kernel(**inputs):
    import numpy as np
    import concourse.bacc as bacc
    from concourse.bass_utils import run_bass_kernel_spmd
    nc = bacc.Bacc("TRN2", target_bir_lowering=False, num_devices=1)
    arrays, args = {}, []
    cpack, selin = constants()
    for name, a in [(n, inputs[n]) for n in _INS] + [("cpack", cpack), ("selin", selin)]:
        a = np.ascontiguousarray(a)
        arrays["in_" + name] = a
        args.append(nc.dram_tensor("in_" + name, a.shape, mybir.dt.from_np(a.dtype), kind="ExternalInput").ap())
    L = 1
    outs = [(1, TP, D), (DB, DS, D), (L, 1, TP, H, HD), (L, 1, TP, H, HD), (L, 1, TP, H), (L, 1, TP, H, HD), (L, 1, TP, H, HD),
            (L, DB, DS, H, HD), (L, DB, DS, H, HD), (L, DB, DS, H), (L, DB, PAST, H, HD), (L, DB, PAST, H, HD)]
    for i, shape in enumerate(outs):
        args.append(nc.dram_tensor(f"out_{i}", shape, mybir.dt.float32, kind="ExternalOutput").ap())
    program(nc, *args)
    r = run_bass_kernel_spmd(nc, [arrays], core_ids=[0])
    return tuple(r.results[0][f"out_{i}"] for i in range(len(outs)))
```

```python
import concourse.bass as bass
from concourse import mybir
from contextlib import ExitStack

D, TP, DB, DS = 1024, 512, 8, 4
TS = DB * DS
T = TP + TS
HALF = T // 2
KT = D // 128
HD, H = 64, 8
W = H * HD
NPAIR = W // 128
FFN, KF = 2816, 22
PAST, PAGE = 1024, 128
NPG = PAST // PAGE
EPS = 1e-6
NEG = -1e30
PT_ = [128, 128, 128, 128, TS]
FOX, DSW = 0, 1
NCH = [NPG + 1, 6]
NALL = NCH[0] + NCH[1]
NKF = 3
KD = KF // 2
PASSES = ((0, 0), (0, 1), (1, 0))
COL_F, COL_G = 3 * W, 3 * W + H + 3 * W
BLOCKS = [W, 0, 3 * W + H + W, 3 * W + H, 2 * W, 3 * W + H + 2 * W]

C_ID, C_MEAN, C_ONE, C_TRI, C_NTRI, C_LC, C_COS, C_SIN, C_DM, C_FM = 0, 128, 256, 384, 512, 1408, 1920, 2240, 2560, 2584
C_END = 2588


def program(nc, x_prompt, x_sample, cache_k, cache_v, cache_lf, state_k, state_v, page_table, norm1_g, w_in, b_f,
            qn_f, kn_f, qn_d, kn_d, w_o_fox, w_o_dsw, w_out, norm2_g, w_gate, w_up, w_down, cpack, selin,
            y_p, y_s, kf_p, vf_p, lf_p, kd_p, vd_p, kf_s, vf_s, lf_s, kd_s, vd_s):
    f32, i32 = mybir.dt.float32, mybir.dt.int32
    ALU, ACT, AX = mybir.AluOpType, mybir.ActivationFunctionType, mybir.AxisListType
    ds = bass.ds
    ctx = ExitStack()
    with ctx:
        ctx.enter_context(nc.allow_non_contiguous_dma(reason="small parameter vectors"))
        names = set()

        def sem(name):
            return ctx.enter_context(nc.semaphore(name))

        ARENA = 53184
        arena_at = 16512
        count = [0]
        cur = [0]

        def shaped(v, shape):
            if len(shape) == 1:
                return v
            nm = "abcdef"[:len(shape)]
            return v.rearrange(f"p ({' '.join(nm)}) -> p {' '.join(nm)}", **{a: s for a, s in zip(nm, shape)})

        def put(shape, at=None, part=128):
            n = 1
            for s in shape:
                n *= s
            if at is None:
                at = cur[0]
                cur[0] += n + -n % 8
            assert at + n <= ARENA, (at, n)
            count[0] += 1
            return shaped(nc.alloc_sbuf_tensor_at(f"buffer{count[0]}", [part, n], f32, offset=arena_at + 4 * at)[:, :], shape)

        def put_r(name, shape, at):
            n = 1
            for s in shape:
                n *= s
            assert at + n <= ARENA, (at, n)
            t = nc.alloc_sbuf_tensor_at(name, [128, n], mybir.dt.float32r, offset=arena_at + 4 * at)
            return shaped(t[:, :], shape)

        cp = put([C_END + 4])
        ident = cp[:, C_ID:C_ID + 128]
        mean1 = cp[:, C_MEAN:C_MEAN + 128]
        ones = cp[:, C_ONE:C_ONE + 128]
        tri = cp[:, C_TRI:C_TRI + 128]
        ntri = cp[:, C_NTRI:C_NTRI + 896]
        logc = cp[:, C_LC:C_LC + 512]
        cosr = cp[:, C_COS:C_COS + 320].rearrange("p (t d) -> p t d", d=64)
        sinr = cp[:, C_SIN:C_SIN + 320].rearrange("p (t d) -> p t d", d=64)
        dmask = cp[:, C_DM:C_DM + 24].rearrange("p (c q) -> p c q", q=4)
        fmask = cp[:, C_FM:C_FM + 4]
        SEL = cur[0]
        sel = put([H, 128], part=8)
        onr = put([W], SEL)
        WDr = put([2, KD, 128], C_TRI)
        epsc = put([1])
        gains = put([4, HD])
        g1 = put([KT])
        g2 = put([KT])
        bf = put([H])
        ptab = put([64]).bitcast(i32)
        rstd = put([T])
        ssum = put([4, 5, H])
        lfx = put([5, H])
        lfe = put([5, H])
        lfa = put([5, H])
        negcT = put([TP], part=8)
        Qs = put([2, DB, NPAIR, 2, DS])
        mx = put([4, 1])
        mx2 = put([4, 1])
        negm = put([4, 1])
        rs = put([4, 1])
        rinv = put([4, 1])
        xT = put([KT, T])
        X2at = cur[0]
        put([2, KT, T])
        X2 = put_r("x_split", [2, KT, T], X2at)
        Z = cur[0]
        WQ = put([2, 4, W], Z)
        WQs = put_r("wqkv_split", [2, 2, 4, W], Z + 4096)
        rows = put([4, 5, W], Z + 12288)
        xrow = put([5, D], Z + 12288)
        vrows = put([5, 2 * W], Z + 22528)
        sq = put([2, T], Z + 27648)
        rt = put([2, W], Z + 28736)
        wf = put([KT, H], Z + 29760)
        wfs = put_r("wf_split", [2, KT, H], Z + 29824)
        tmpA = put([2, T], Z + 29952)
        qkT = put([16, T], Z)
        negc = put([H, TP], Z + 12288)
        ndiag = put([H, 4, 128], Z + 16384)
        PP = put([2, TP], Z + 20480)
        PTs = put([2, TP], Z + 21504)
        Arow = put([2, 128], Z + 27648)
        AT = put([2, NPAIR, T], Z + 27904)
        WR = put([4, 1024], Z)
        WS = put_r("w_split", [2, 2, 1024], Z + 4096)
        zg = put([16, T], Z + 8192)
        Vf = put([NCH[0], W], Z + 16896)
        Vd = put([NCH[1], W], Z + 21504)
        Kr = put([5, W], Z + 24576)
        Kx = put([4, W], Z + 2048)
        lfp = put([NCH[0], H], Z + 27136)
        cneg = put([NCH[0], H], Z + 27208)
        mp = put([128], Z + 27280)
        mcol = put([1], Z + 27408)
        dg = put([64], Z + 27416)
        ps_ = put([64], Z + 27480)
        ri = put([1], Z + 27544)
        KTs = put([3, W], Z + 32256)
        S1 = put([NALL, 32], Z + 33792)
        Ahl = put_r("a_split", [2, 2 * NPAIR, T], Z + 16896)
        tg = put([2, T], Z + 25600)
        sq2 = put([2, T], Z + 26688)
        std2 = put([T], Z + 32256)
        tmpM = put([2, T], Z + 32800)
        Hhl = put_r("h_split", [2, KF, T], Z + 8192)
        sg = put([2, T], Z + 32128)
        tmpH = put([T], Z + 33216)
        WSD = put_r("wd_split", [2, 2, KD * 128], Z)
        yT = put([2, T], X2at)
        yst = put([2, 5, 128], X2at + 1088)
        bank = [ctx.enter_context(nc.psum_tensor(f"bank{i}", [128, 512], f32)) for i in range(8)]

        def key_slot(ch):
            return ch % NKF if ch < NCH[0] else NKF + ch - NCH[0]

        def key_rows(ch):
            n = key_slot(ch)
            return Kr[:, n, :] if n < 5 else Kx[:, n - 5, :]

        TB = (0, 1, 3)

        xp_v = x_prompt[0].rearrange("(t p) n -> p t n", p=128)
        xs_v = x_sample.rearrange("b s n -> (b s) n")
        win_v = w_in[0].rearrange("(k p) n -> p k n", p=128)
        lay = lambda a: a.rearrange("l b s h d -> (l b) s (h d)")
        kfp_v, vfp_v, kdp_v, vdp_v = [lay(a)[0].rearrange("(t p) n -> p t n", p=128) for a in (kf_p, vf_p, kd_p, vd_p)]
        kfs_v, vfs_v, kds_v, vds_v = [lay(a) for a in (kf_s, vf_s, kd_s, vd_s)]
        sk_v, sv_v = lay(state_k), lay(state_v)
        ck_v, cv_v = [a.rearrange("l n g h d -> (l n) g (h d)") for a in (cache_k, cache_v)]
        cl_v = cache_lf[0]
        lfs_v = lf_s[0]
        wof_v = [w[0].rearrange("(k p) n -> p k n", p=128) for w in (w_o_fox, w_o_dsw)]
        wx_v = w_out[0].rearrange("(k p) n -> p k n", p=128)
        wg_v = [w[0].rearrange("(k p) n -> p k n", p=128) for w in (w_gate, w_up)]
        wd_v = w_down[0].rearrange("(k p) n -> p k n", p=128)
        yp_v = y_p[0].rearrange("(t p) n -> p t n", p=128)
        ys_v = y_s.rearrange("b s n -> (b s) n")
        n_phys = ck_v.shape[0]

        c_in, x_in, f_in = sem("consts_in"), sem("x_in"), sem("wf_in")
        xT_ps, xT_sb = sem("xT_in_psum"), sem("xT_ready")
        sq_ok, sq_used, std_ok, rstd_ok, xn_ok = [sem("n1_" + s) for s in ("squared", "summed", "std", "rstd", "xn_ready")]
        sq2_ok, sq2_used, std2_ok, rstd2_ok, u_ok = [sem("n2_" + s) for s in ("squared", "summed", "std", "rstd", "u_ready")]
        z_init, eps_ok = sem("zeroed"), sem("eps_laid")
        f_ps, lfx_ok, lfe_ok, lf_ok = sem("f_in_psum"), sem("f_biased"), sem("f_act"), sem("logf_ready")
        wq_in = [sem(f"wqkv_in{s}") for s in range(2)]
        wqh_ok, wql_ok, wfh_ok, wfl_ok = sem("wqkv_hi"), sem("wqkv_lo"), sem("wf_hi"), sem("wf_lo")
        xt_ok, xh_ok, ut_ok, uh_ok, ah_ok, al_ok = [sem(n) for n in ("xn_whole", "xn_hi", "u_whole", "u_hi", "a_hi", "a_lo")]
        z_ps, z_used = sem("z_in_psum"), sem("z_copied")
        zs_ok, zs_sum, zs_std, zs_inv, row_s, row_ok = [sem("row_" + s) for s in ("squared", "summed", "std", "inverse", "step", "done")]
        tr_ps, tr_a, tr_v = sem("qkT_in_psum"), sem("qkT_copied_act"), sem("qkT_copied_dve")
        st_k = sem("rows_stored")
        st_lf = sem("logf_stored")
        sts = sem("sample_rows_stored")
        cT_ps, cT_sb, cb_ps, cb_sb, nd_ok = sem("cT_in_psum"), sem("cT_ready"), sem("c_in_psum"), sem("negc_ready"), sem("ndiag_ready")
        Qs_ok = sem("Qs_ready")
        s_ps, s_mx, s_nm, p_ok, pt_ps, pt_a, pt_v, o_ps, r_ok, a_ok, at_ps, at_ok = [sem("pa_" + s) for s in (
            "scores", "max_step", "negmax", "probs", "probsT_psum", "probsT_act", "probsT_dve", "out_psum", "recip",
            "out_rows", "outT_psum", "outT_ready")]
        vf_in, l_in, vd_in = [sem(s) for s in ("vfox_in", "lfox_in", "vdsw_in")]
        k_in = [sem(f"keys_in{s}") for s in range(NKF + NCH[1])]
        w_in_ = [sem(f"w_in{s}") for s in range(4)]
        wh_ok, wl_ok, prod_ps, g_ok = sem("w_hi"), sem("w_lo"), sem("product_halves"), sem("gate_copied")
        cc_ps, cc_ok = sem("sc_in_psum"), sem("sc_ready")
        kt_ps, kt_a, kt_v, ktq = sem("skT_psum"), sem("skT_act"), sem("skT_dve"), sem("skT_used")
        sc_ps, s1_ok, mp_ok, mt_ps, m_col, dg_ok, mb_ps, sub_ok, sp_ok, sum_ok, so_ps, ri_ok, on_ok, ot_ps, sat_ok = [sem("sa_" + n) for n in (
            "scores", "biased", "chunk_max", "max_T", "max", "max_diag", "max_bc", "shifted", "probs", "sums", "outputs", "recip", "rows", "rows_T", "outT")]
        cpy = sem("state_copied")
        sg_ok, tg_ok, mt_ok, mh_ok, m_ok = sem("gates_sigmoid"), sem("merge_step"), sem("m_whole"), sem("m_hi"), sem("m_ready")
        h_ok = sem("h_ready")
        sil_ok, gm_ok, ht_ok, hh_ok, hid_ok = sem("ffn_sigmoid"), sem("ffn_gate_mul"), sem("hidden_whole"), sem("hidden_hi"), sem("hidden_ready")
        wd_in = [sem(f"wd_in{s}") for s in range(2)]
        dh_ok, dl_ok = sem("wd_hi"), sem("wd_lo")
        d_ps, y_ok, yt_ps, yst_ok = sem("down_out"), sem("yT_ready"), sem("y_in_psum"), sem("y_rows_ready")
        y_st = [sem(f"y_stored{s}") for s in range(2)]
        N_CONST = 10

        block = ctx.enter_context(nc.Block())

        @block.sync
        def _(sp):
            sp.dma_start(cp[:, 0:C_END], cpack).then_inc(c_in, 16)
            sp.dma_start(xrow[:, 0:4, :], xp_v).then_inc(x_in, 16)
            sp.dma_start(xrow[0:TS, 4, :], xs_v).then_inc(x_in, 16)
            sp.dma_start(sel[0:8], selin.rearrange("h (a c) -> h a c", c=128)).then_inc(c_in, 16)
            sp.dma_start(g1, norm1_g[0].rearrange("(k p) -> p k", p=128)).then_inc(c_in, 16)
            sp.dma_start(g2, norm2_g[0].rearrange("(k p) -> p k", p=128)).then_inc(c_in, 16)
            for n, g in enumerate((kn_f, qn_f, kn_d, qn_d)):
                sp.dma_start(gains[:, n, :], g[0:1, :].to_broadcast([128, HD])).then_inc(c_in, 16)
            sp.dma_start(bf, b_f[0:1, :].to_broadcast([128, H])).then_inc(c_in, 16)
            sp.dma_start(ptab[0:1, :], page_table.rearrange("b n -> (b n)").rearrange("(a n) -> a n", a=1)).then_inc(c_in, 16)
            sp.dma_start(wf, win_v[:, :, COL_F:COL_F + H]).then_inc(f_in, 16)
            def shift(b):
                sp.dma_start(kds_v[b, 0:PAST - DS], sk_v[b, DS:PAST]).then_inc(cpy, 16)
                sp.dma_start(vds_v[b, 0:PAST - DS], sv_v[b, DS:PAST]).then_inc(cpy, 16)
            for n in range(12):
                blk, kh = n // 2, n % 2
                if n >= 2:
                    sp.wait_ge(wql_ok, n - 1)
                sp.dma_start(WQ[:, n % 2], win_v[:, 4 * kh:4 * kh + 4, BLOCKS[blk]:BLOCKS[blk] + W]).then_inc(wq_in[n % 2], 16)
                if n % 2 and n >= 3:
                    shift(blk - 1)
            sp.wait_ge(sts, 16 * 5)
            sp.wait_ge(at_ok, 32)
            sp.wait_ge(z_init, 9)

            ring = lambda s: WR[:, s].rearrange("p (k n) -> p k n", n=128)

            def pages(b, first):
                page = [sp.value_load(ptab[0:1, ds(b * NPG + n, 1)], min_val=0, max_val=n_phys - 1) for n in range(NPG)]
                if not first:
                    sp.wait_ge(cc_ps, b)
                sp.dma_start(lfp[0:DS, NPG, :], lfs_v[ds(b, 1)].rearrange("a g n -> (a g) n")).then_inc(l_in, 16)
                for n in range(NPG):
                    sp.dma_start(lfp[:, n, :], cl_v[ds(page[n], 1)].rearrange("a g n -> (a g) n")).then_inc(l_in, 16)
                if not first:
                    sp.wait_ge(wl_ok, 2 * b - 1)
                sp.dma_start(ring(0), win_v[:, :, ds(COL_G + b * 256, 128)]).then_inc(w_in_[0], 32)

                def keys(ch, src, rows=128):
                    sp.dma_start(key_rows(ch)[0:rows], src).then_inc(k_in[key_slot(ch)], 16)
                for ch in range(NCH[0]):
                    if not (first and ch < NKF):
                        sp.wait_ge(kt_ps, b * NALL + (ch - NKF + 1 if ch >= NKF else ch - 8))
                    if ch < NPG:
                        keys(ch, ck_v[ds(page[ch], 1)].rearrange("a g n -> (a g) n"))
                    else:
                        keys(ch, kfs_v[ds(b, 1)].rearrange("a g n -> (a g) n"), DS)
                for n in range(4):
                    if not first:
                        sp.wait_ge(kt_ps, b * NALL - NCH[1] + n + 1)
                    keys(NCH[0] + n, sk_v[ds(b, 1), 512 + 128 * n:640 + 128 * n].rearrange("a g n -> (a g) n"))
                if not first:
                    sp.wait_ge(kt_ps, b * NALL)
                keys(NALL - 1, kds_v[ds(b, 1), PAST - DS:PAST].rearrange("a g n -> (a g) n"), DS)
                keys(NALL - 2, sk_v[ds(b, 1), 0:512].rearrange("a (g r) n -> (a g) r n", r=16)[:, 0:4, :])
                if not first:
                    sp.wait_ge(wl_ok, 2 * b)
                sp.dma_start(ring(1), win_v[:, :, ds(COL_G + b * 256 + 128, 128)]).then_inc(w_in_[1], 32)
                if not first:
                    sp.wait_ge(so_ps, 2 * b - 1)
                for n in range(NPG):
                    sp.dma_start(Vf[:, n, :], cv_v[ds(page[n], 1)].rearrange("a g n -> (a g) n")).then_inc(vf_in, 16)
                sp.dma_start(Vf[0:DS, NPG, :], vfs_v[ds(b, 1)].rearrange("a g n -> (a g) n")).then_inc(vf_in, 16)
                if not first:
                    sp.wait_ge(so_ps, 2 * b)
                for n in range(4):
                    sp.dma_start(Vd[:, n, :], sv_v[ds(b, 1), 512 + 128 * n:640 + 128 * n].rearrange("a g n -> (a g) n")).then_inc(vd_in, 16)
                sp.dma_start(Vd[:, 4, :], sv_v[ds(b, 1), 0:512].rearrange("a (g r) n -> (a g) r n", r=16)[:, 0:4, :]).then_inc(vd_in, 16)
                sp.dma_start(Vd[0:DS, 5, :], vds_v[ds(b, 1), PAST - DS:PAST].rearrange("a g n -> (a g) n")).then_inc(vd_in, 16)

            pages(0, True)
            with sp.Fori(1, DB) as b:
                pages(b, False)
            for m in range(8):
                if m < 2:
                    sp.wait_ge(wl_ok, 16 + m - 1)
                elif m < 4:
                    sp.wait_ge(kt_ps, DB * NALL)
                else:
                    sp.wait_ge(wl_ok, 16 + m - 3)
                for k in range(2):
                    sp.dma_start(ring(m % 4)[:, 4 * k:4 * k + 4], wof_v[k][:, :, m * 128:(m + 1) * 128]).then_inc(w_in_[m % 4], 16)
            for m in range(8):
                sp.wait_ge(wl_ok, 24 + m - 3)
                sp.dma_start(ring(m % 4), wx_v[:, :, m * 128:(m + 1) * 128]).then_inc(w_in_[m % 4], 32)
            with sp.Fori(0, KF // 2) as i:
                for s in range(4):
                    sp.wait_ge(wl_ok, 32 + 4 * i + s - 3)
                    sp.dma_start(ring(s), wg_v[s % 2][:, :, ds((2 * i + s // 2) * 128, 128)]).then_inc(w_in_[s], 32)
            sp.wait_ge(sat_ok, 4 * DB)
            for b in range(5, DB):
                shift(b)
            for n in range(16):
                m, kh = n // 2, n % 2
                if n >= 2:
                    sp.wait_ge(dl_ok, n - 1)
                sp.dma_start(WDr[:, kh], wd_v[:, KD * kh:KD * kh + KD, m * 128:(m + 1) * 128]).then_inc(wd_in[kh], 16)
            sp.wait_ge(cpy, 16 * 2 * DB)
            sp.wait_ge(st_k, 16 * 4)
            sp.wait_ge(st_lf, 16)
            sp.wait_ge(sts, 16 * 5)

        @block.gpsimd
        def _(pool):
            nc.gpsimd.memset(epsc, EPS).then_inc(eps_ok, 1)
            nc.gpsimd.memset(Qs, 0.0).then_inc(z_init, 1)
            nc.gpsimd.memset(lfx, 0.0).then_inc(z_init, 1)
            nc.gpsimd.memset(ssum, 1.0).then_inc(z_init, 1)
            pool.wait_ge(lf_ok, 3)
            pool.dma_start(lf_p[0, 0].rearrange("(t p) h -> p t h", p=128), lfx[:, 0:4, :]).then_inc(st_lf, 16)
            pool.dma_start(lfs_v.rearrange("b s h -> (b s) h"), lfx[0:TS, 4, :]).then_inc(sts, 16)
            for blk, out_p, out_s in ((0, kfp_v, kfs_v), (2, kdp_v, kds_v)):
                pool.wait_ge(row_ok, 5 * blk + 5)
                pool.dma_start(out_p, rows[:, blk, 0:4, :]).then_inc(st_k, 16)
                if blk == 0:
                    pool.dma_start(out_s.rearrange("b s n -> (b s) n"), rows[0:TS, blk, 4, :]).then_inc(sts, 16)
                else:
                    pool.dma_start(out_s[:, PAST - DS:PAST, :], rows[0:TS, blk, 4, :]).then_inc(sts, 16)
            for k, out_p, out_s in ((0, vfp_v, vfs_v), (1, vdp_v, vds_v)):
                pool.wait_ge(z_used, 5 * (4 + k) + 5)
                pool.dma_start(out_p, vrows[:, 0:4, k * W:(k + 1) * W]).then_inc(st_k, 16)
                if k == 0:
                    pool.dma_start(out_s.rearrange("b s n -> (b s) n"), vrows[0:TS, 4, k * W:(k + 1) * W]).then_inc(sts, 16)
                else:
                    pool.dma_start(out_s[:, PAST - DS:PAST, :], vrows[0:TS, 4, k * W:(k + 1) * W]).then_inc(sts, 16)
            pool.wait_ge(tr_a, 8)
            pool.wait_ge(tr_v, 8)
            pool.wait_ge(z_init, 3)
            for k in range(2):
                for j in range(2):
                    nc.gpsimd.tensor_copy(Qs[64 * j:64 * j + 64, k, :, :, j, :],
                                          qkT[64 * j:64 * j + 64, 8 + 4 * k:12 + 4 * k, TP:T].rearrange("p c (b q) -> p b c q", q=DS)).then_inc(Qs_ok, 1)
            pool.wait_ge(Qs_ok, 4)
            for h in range(H):
                pool.wait_ge(cb_sb, h + 1)
                nc.gpsimd.tensor_tensor(ndiag[:, h], negc[:, h].rearrange("p (c n) -> p c n", n=128),
                                        tri.rearrange("p (a n) -> p a n", a=1).to_broadcast([128, 4, 128]), ALU.add).then_inc(nd_ok, 1)
            pool.wait_ge(at_ok, 32)
            nc.gpsimd.memset(mp, 0.0).then_inc(z_init, 1)
            nc.gpsimd.memset(onr, 0.0).then_inc(z_init, 1)
            for t in (Vf, lfp):
                nc.gpsimd.memset(t[:, NPG, :], 0.0).then_inc(z_init, 1)
            nc.gpsimd.memset(Vd[:, 5, :], 0.0).then_inc(z_init, 1)
            nc.gpsimd.memset(key_rows(NALL - 1), 0.0).then_inc(z_init, 1)

        @block.scalar
        def _(act):
            def squares(ok, used, inn, src, dst):
                for k in range(KT):
                    act.wait_ge(inn, k + 1)
                    if k >= 2:
                        act.wait_ge(used, k - 1)
                    nc.scalar.activation(dst[:, k % 2], src[:, k], ACT.Square).then_inc(ok, 1)

            def stds(used, ok, dst):
                act.wait_ge(used, KT)
                for hf in range(2):
                    nc.scalar.activation(dst[:, hf * HALF:(hf + 1) * HALF], bank[6 + hf][:, 0:HALF], ACT.Sqrt, bias=epsc).then_inc(ok, 1)

            def hi(dst, src, whole, n, done):
                act.wait_ge(whole, n)
                nc.scalar.copy(dst, src).then_inc(done, 1)

            def wq_hi(n):
                act.wait_ge(wq_in[n % 2], 16 * (n // 2) + 16)
                if n >= 2:
                    act.wait_ge(z_ps, 5 * (n - 1))
                nc.scalar.copy(WQs[:, n % 2, 0], WQ[:, n % 2]).then_inc(wqh_ok, 1)
            act.wait_ge(c_in, 16 * N_CONST)
            act.wait_ge(eps_ok, 1)
            squares(sq_ok, sq_used, xT_sb, xT, sq)
            stds(sq_used, std_ok, rstd)
            hi(wfs[:, 0], wf, f_in, 16, wfh_ok)
            for k in range(KT):
                hi(X2[:, 0, k], tmpA[:, k % 2], xt_ok, k + 1, xh_ok)
            wq_hi(0)
            wq_hi(1)
            act.wait_ge(lfx_ok, 3)
            nc.scalar.activation(lfe, lfe, ACT.Exp, scale=-1.0).then_inc(lfe_ok, 1)
            act.wait_ge(lfe_ok, 1)
            nc.scalar.activation(lfe, lfe, ACT.Ln, bias=1.0).then_inc(lfe_ok, 1)

            def rows_block(blk):
                wq_hi(2 * blk + 2)
                for t in range(5):
                    P = PT_[t]
                    act.wait_ge(z_ps, 10 * blk + 5 + t + 1)
                    nc.scalar.copy(rows[0:P, blk, t, :], bank[t][128 - P:128, :]).then_inc(z_used, 1)
                    act.wait_ge(z_used, 5 * blk + t + 1)
                    if 5 * blk + t >= 2:
                        act.wait_ge(zs_sum, 5 * blk + t - 1)
                    nc.scalar.activation(sq[0:P, t % 2, 0:W], rows[0:P, blk, t, :], ACT.Square).then_inc(zs_ok, 1)
                wq_hi(2 * blk + 3)
                act.wait_ge(zs_sum, 5 * blk + 5)
                nc.scalar.activation(ssum[:, blk], ssum[:, blk], ACT.Sqrt, bias=epsc, scale=1.0 / HD).then_inc(zs_std, 1)
            act.wait_ge(z_init, 3)
            for blk in range(4):
                rows_block(blk)
            for k in range(2):
                if k == 0:
                    wq_hi(10)
                for t in range(5):
                    P = PT_[t]
                    act.wait_ge(z_ps, 10 * (4 + k) + 5 + t + 1)
                    nc.scalar.copy(vrows[0:P, t, k * W:(k + 1) * W], bank[t][128 - P:128, :]).then_inc(z_used, 1)
                if k == 0:
                    wq_hi(11)
            act.wait_ge(cT_ps, 1)
            nc.scalar.copy(negcT[0:8], bank[6][0:8, :]).then_inc(cT_sb, 1)
            for u in range(0, 16, 2):
                blk, c = u // 4, u % 4
                dst = qkT[:, 8 * (blk % 2) + 4 * (blk // 2) + c]
                sc = 1.0 if blk % 2 == 0 else HD ** -0.5
                act.wait_ge(tr_ps, u + 1)
                b0 = 2 * (u % 3)
                nc.scalar.activation(dst[:, 0:TP], bank[b0][:, :], ACT.Copy, scale=sc)
                nc.scalar.activation(dst[:, TP:T], bank[b0 + 1][:, 0:TS], ACT.Copy, scale=sc).then_inc(tr_a, 1)
            act.wait_ge(st_k, 16 * 4)
            act.wait_ge(sts, 16 * 5)
            for h in range(H):
                act.wait_ge(cb_ps, h + 1)
                nc.scalar.copy(negc[:, h], bank[6 + h % 2][:, :]).then_inc(cb_sb, 1)

            def outT(p, i):
                n = 4 * p + i
                act.wait_ge(at_ps, n + 1)
                nc.scalar.copy(AT[:, p // 4, p % 4, i * 128:(i + 1) * 128],
                               bank[6 + i % 2][:, 0:128]).then_inc(at_ok, 1)

            def step(p, u, first=False, last=False):
                if not last:
                    i = u // 2
                    N = 128 * (i + 1)
                    act.wait_ge(s_nm, 8 * p + u + 1)
                    nc.scalar.activation(PP[:, u % 2, 0:N], PP[:, u % 2, 0:N], ACT.Exp, bias=negm[:, u % 4],
                                         accum_out=rs[:, u % 4]).then_inc(p_ok, 1)
                if (u - 1) % 2 == 0 and not (first and u < 1):
                    N = 128 * ((u - 1) // 2 + 1)
                    act.wait_ge(pt_ps, 8 * p + u)
                    nc.scalar.copy(PTs[:, 0, 0:N], bank[2][:, 0:N]).then_inc(pt_a, 1)
                if (u - 4) % 2 == 1 and not (first and u < 5):
                    v = (u - 4) % 8
                    outT(p if u >= 4 else p - 1, v // 2)
            for p in range(8):
                for u in range(8):
                    step(p, u, first=p == 0)
            for u in (1, 3):
                outT(7, (u + 4) // 2)
            def w_hi(c, s, first=False, gates=False):
                if isinstance(c, int) and c < 16 or gates:
                    act.wait_ge(w_in_[s], 16 * (c - s) + 32)
                else:
                    act.wait_ge(w_in_[s], 8 * (c - s) - 128 + (256 if s < 2 else 0) + 32)
                if not first:
                    act.wait_ge(prod_ps, 2 * c - 2)
                nc.scalar.copy(WS[:, s % 2, 0], WR[:, s]).then_inc(wh_ok, 1)

            def gate(b, s, hf):
                act.wait_ge(prod_ps, 4 * b + 2 * s + hf + 1)
                act.wait_ge(c_in, 16)
                nc.scalar.copy(zg[:, ds(2 * b + s, 1), hf * HALF:(hf + 1) * HALF].rearrange("p a n -> p (a n)"),
                               bank[6 + hf][:, 0:HALF]).then_inc(g_ok, 1)

            act.wait_ge(z_init, 9)
            def keysT(b, ch):
                act.wait_ge(kt_ps, b * NALL + ch + 1)
                nc.scalar.copy(KTs[:, ch % 3], bank[TB[ch % 3]][:, :]).then_inc(kt_a, 1)

            def batch(b, first=False, last=False):
                def keys_next(*chs):
                    for ch in chs:
                        if not last:
                            keysT(b + 1, ch)
                w_hi(2 * b + 1, 1, first, gates=True)
                keys_next(0)
                gate(b, 0, 0)
                keys_next(2)
                act.wait_ge(sub_ok, 2 * b + 2)
                nc.scalar.activation(S1, S1, ACT.Exp).then_inc(sp_ok, 1)
                keys_next(4, 6, 8)
                gate(b, 0, 1)
                w_hi(2 * b + 2, 0, gates=True)
                keys_next(10)
                gate(b, 1, 0)
                keys_next(12, 14)
                gate(b, 1, 1)
            w_hi(0, 0, True)
            for ch in range(0, NALL, 2):
                keysT(0, ch)
            batch(0, first=True)
            with act.Fori(1, DB - 1) as b:
                batch(b)
            batch(DB - 1, last=True)
            w_hi(17, 1)
            for k in range(2 * NPAIR):
                hi(Ahl[:, 0, k], AT[:, k // NPAIR, k % NPAIR], sat_ok, 4 * DB, ah_ok)
            for m in range(8):
                if m == 0:
                    act.wait_ge(g_ok, 4 * DB)
                nc.scalar.activation(zg[:, m:m + 9:8, :], zg[:, m:m + 9:8, :], ACT.Sigmoid).then_inc(sg_ok, 1)
            for m in range(8):
                w_hi(18 + m, (18 + m) % 4)
                hi(X2[:, 0, m], tmpM[:, m % 2], mt_ok, m + 1, mh_ok)
            for c in range(26, 34):
                w_hi(c, c % 4)
            for m in range(8):
                act.wait_ge(h_ok, m + 1)
                if m >= 2:
                    act.wait_ge(sq2_used, m - 1)
                nc.scalar.activation(sq2[:, m % 2], xT[:, m], ACT.Square).then_inc(sq2_ok, 1)
            stds(sq2_used, std2_ok, std2)
            for k in range(KT):
                hi(X2[:, 0, k], tmpM[:, k % 2], ut_ok, k + 1, uh_ok)

            def d_hi(n):
                s = n % 2
                act.wait_ge(wd_in[s], 16 * (n // 2) + 16)
                if n >= 2:
                    act.wait_ge(d_ps, n - 1)
                else:
                    act.wait_ge(prod_ps, 2 * 76)
                nc.scalar.copy(WSD[:, s, 0], WDr[:, s].rearrange("p k n -> p (k n)")).then_inc(dh_ok, 1)

            def silu(m, s, last=False):
                c = 32 + 2 * m
                act.wait_ge(prod_ps, 2 * c + 2)
                for hf in range(2):
                    nc.scalar.activation(sg[:, s, hf * HALF:(hf + 1) * HALF], bank[4 * s + hf][:, 0:HALF], ACT.Sigmoid).then_inc(sil_ok, 1)
                if not last:
                    w_hi(c + 2, (2 * s + 2) % 4)
                act.wait_ge(ht_ok, m + 1)
                act.wait_ge(c_in, 16)
                nc.scalar.copy(Hhl[:, 0, ds(m, 1)].rearrange("p a n -> p (a n)"), tmpH).then_inc(hh_ok, 1)
                if not last:
                    w_hi(c + 3, (2 * s + 3) % 4)
            with act.Fori(0, KF // 2 - 1) as i:
                for s in range(2):
                    silu(2 * i + s, s)
            silu(KF - 2, 0)
            silu(KF - 1, 1, last=True)
            d_hi(0)
            d_hi(1)

            def yrows(m, s, warm):
                act.wait_ge(yt_ps, m + 1)
                if warm:
                    act.wait_ge(y_st[s], 32 * (m // 2) if isinstance(m, int) else 0)
                nc.scalar.copy(yst[:, s, 0:4, :], bank[4 + 2 * s][:, :].rearrange("p (t n) -> p t n", n=128))
                nc.scalar.copy(yst[0:TS, s, 4, :], bank[5 + 2 * s][0:TS, 0:128]).then_inc(yst_ok, 1)
                act.wait_ge(yst_ok, m + 1)
                act.dma_start(yp_v[:, :, ds(m * 128, 128)], yst[:, s, 0:4, :]).then_inc(y_st[s], 16)
                act.dma_start(ys_v[:, ds(m * 128, 128)], yst[0:TS, s, 4, :]).then_inc(y_st[s], 16)
            for m in range(8):
                for n in (2 * m + 2, 2 * m + 3):
                    if n < 16:
                        d_hi(n)
                if m >= 1:
                    yrows(m - 1, (m - 1) % 2, m >= 3)
            yrows(7, 1, True)
            for s in range(2):
                act.wait_ge(y_st[s], 32 * 4)

        @block.vector
        def _(dve):
            V = nc.vector
            for k in range(KT):
                dve.wait_ge(xT_ps, k + 1)
                V.tensor_copy(xT[:, k, 0:TP], bank[2 * (k % 2)][:, :])
                V.tensor_copy(xT[:, k, TP:T], bank[2 * (k % 2) + 1][:, 0:TS]).then_inc(xT_sb, 1)

            def lo(dst, whole, part, done_hi, n, done):
                dve.wait_ge(done_hi, n)
                V.tensor_tensor(dst, whole, part.bitcast(f32), ALU.subtract).then_inc(done, 1)

            def scaled(std, rok, ok, g, src, sdt, tmp, whole_ok, hi_ok):
                dve.wait_ge(std, 2)
                V.reciprocal(sdt, sdt).then_inc(rok, 1)
                dve.wait_ge(rok, 1)
                for k in range(KT + 1):
                    if k < KT:
                        if k >= 2:
                            dve.wait_ge(ok, k - 1)
                        V.scalar_tensor_tensor(tmp[:, k % 2], src[:, k], g[:, k:k + 1], sdt, ALU.mult, ALU.mult).then_inc(whole_ok, 1)
                    if k >= 1:
                        lo(X2[:, 1, k - 1], tmp[:, (k - 1) % 2], X2[:, 0, k - 1], hi_ok, k, ok)
            dve.wait_ge(xT_sb, KT)
            dve.wait_ge(c_in, 16 * N_CONST)
            lo(wfs[:, 1], wf, wfs[:, 0], wfh_ok, 1, wfl_ok)
            scaled(std_ok, rstd_ok, xn_ok, g1, xT, rstd, tmpA, xt_ok, xh_ok)
            wq_lo = lambda n: lo(WQs[:, n % 2, 1], WQ[:, n % 2], WQs[:, n % 2, 0], wqh_ok, n + 1, wql_ok)
            wq_lo(0)
            wq_lo(1)
            dve.wait_ge(f_ps, 1)
            dve.wait_ge(z_init, 3)
            fp = bank[5][:, 0:40].rearrange("p (t h) -> p t h", h=H)
            bfb = bf.rearrange("p (a h) -> p a h", a=1)
            V.tensor_tensor(lfx[:, 0:4], fp[:, 0:4], bfb.to_broadcast([128, 4, H]), ALU.add).then_inc(lfx_ok, 1)
            V.tensor_tensor(lfx[0:TS, 4], fp[96:128, 4], bf[96:128], ALU.add).then_inc(lfx_ok, 1)
            dve.wait_ge(lfx_ok, 2)
            V.scalar_tensor_tensor(lfe, lfx, -1.0, lfx, ALU.mult, ALU.max).then_inc(lfx_ok, 1)
            V.tensor_scalar(lfa, lfx, 0.0, None, ALU.min).then_inc(lf_ok, 1)
            dve.wait_ge(lf_ok, 1)
            dve.wait_ge(lfe_ok, 2)
            V.tensor_tensor(lfx, lfa, lfe, ALU.subtract).then_inc(lf_ok, 2)

            def norm_block(blk, rope, i0):
                wq_lo(2 * blk + 2)
                for t in range(5):
                    P = PT_[t]
                    dve.wait_ge(zs_ok, 5 * blk + t + 1)
                    V.reduce_sum(ssum[0:P, blk, t, :], sq[0:P, t % 2, 0:W].rearrange("p (h d) -> p h d", d=HD), AX.X).then_inc(zs_sum, 1)
                wq_lo(2 * blk + 3)
                dve.wait_ge(zs_std, blk + 1)
                V.reciprocal(ssum[:, blk], ssum[:, blk]).then_inc(zs_inv, 1)
                dve.wait_ge(zs_inv, blk + 1)
                n = i0
                for t in range(5):
                    P = PT_[t]
                    r = rows[0:P, blk, t, :].rearrange("p (h d) -> p h d", d=HD)
                    inv = ssum[0:P, blk, t, :].rearrange("p (h e) -> p h e", e=1)
                    g = gains[0:P, blk:blk + 1, :]
                    V.tensor_tensor(r, r, inv.to_broadcast([P, H, HD]), ALU.mult).then_inc(row_s, 1)
                    n = n + 1
                    dve.wait_ge(row_s, n)
                    if not rope:
                        V.tensor_tensor(r, r, g.to_broadcast([P, H, HD]), ALU.mult).then_inc(row_ok, 1)
                        continue
                    V.tensor_tensor(r, r, g.to_broadcast([P, H, HD]), ALU.mult).then_inc(row_s, 1)
                    n = n + 1
                    dve.wait_ge(row_s, n)
                    a, bb = [rt[0:P, e].rearrange("p (h d) -> p h d", d=HD) for e in range(2)]
                    V.tensor_tensor(a, r, cosr[0:P, t:t + 1, :].to_broadcast([P, H, HD]), ALU.mult).then_inc(row_s, 1)
                    for e in range(2):
                        V.tensor_tensor(bb[:, :, 32 * e:32 * e + 32], r[:, :, 32 - 32 * e:64 - 32 * e],
                                        sinr[0:P, t:t + 1, 32 * e:32 * e + 32].to_broadcast([P, H, 32]), ALU.mult).then_inc(row_s, 1)
                    n = n + 3
                    dve.wait_ge(row_s, n)
                    V.tensor_tensor(r, a, bb, ALU.add).then_inc(row_ok, 1)
                return n
            n = 0
            for blk in range(4):
                n = norm_block(blk, blk >= 2, n)
            wq_lo(10)
            wq_lo(11)
            for u in range(1, 16, 2):
                blk, c = u // 4, u % 4
                dst = qkT[:, 8 * (blk % 2) + 4 * (blk // 2) + c]
                sc = 1.0 if blk % 2 == 0 else HD ** -0.5
                dve.wait_ge(tr_ps, u + 1)
                b0 = 2 * (u % 3)
                V.tensor_scalar(dst[:, 0:TP], bank[b0][:, :], sc, None, ALU.mult)
                V.tensor_scalar(dst[:, TP:T], bank[b0 + 1][:, 0:TS], sc, None, ALU.mult).then_inc(tr_v, 1)
            dve.wait_ge(nd_ok, H)
            dve.wait_ge(cb_sb, H)

            def step(p, u, kind, first=False, last=False):
                if not last:
                    i, j, e = u // 2, u % 2, u % 4
                    N = 128 * (i + 1)
                    n = 8 * p + u
                    dve.wait_ge(s_ps, n + 1)
                    if not (first and u < 2):
                        dve.wait_ge(pt_ps, n - 1)
                    mxs = (14 * p + sum(2 if v >= 2 else 1 for v in range(u))) if kind == FOX else (56 + 8 * (p - 4) + u)
                    if kind == FOX:
                        h = 2 * p + j
                        V.tensor_tensor_reduce(PP[:, u % 2, i * 128:N], bank[u % 2][:, i * 128:N],
                                               ndiag[:, h, i, :],
                                               1.0, NEG, ALU.add, ALU.max, mx[:, e]).then_inc(s_mx, 1)
                        mxs = mxs + 1
                        last_mx = mx
                        if i > 0:
                            dve.wait_ge(s_mx, mxs)
                            V.tensor_tensor_reduce(PP[:, u % 2, 0:i * 128], bank[u % 2][:, 0:i * 128],
                                                   negc[:, h, 0:i * 128],
                                                   1.0, mx[:, e], ALU.add, ALU.max, mx2[:, e]).then_inc(s_mx, 1)
                            mxs = mxs + 1
                            last_mx = mx2
                    else:
                        V.tensor_tensor_reduce(PP[:, u % 2, 0:N], bank[u % 2][:, 0:N], logc[:, (3 - i) * 128:512],
                                               1.0, NEG, ALU.add, ALU.max, mx[:, e]).then_inc(s_mx, 1)
                        mxs = mxs + 1
                        last_mx = mx
                    dve.wait_ge(s_mx, mxs)
                    V.tensor_scalar(negm[:, e], last_mx[:, e], -1.0, None, ALU.mult).then_inc(s_nm, 1)
                if (u - 1) % 2 == 1 and not (first and u < 1):
                    v = (u - 1) % 8
                    N = 128 * (v // 2 + 1)
                    dve.wait_ge(pt_ps, 8 * p + u)
                    V.tensor_copy(PTs[:, 1, 0:N], bank[3][:, 0:N]).then_inc(pt_v, 1)
                if not (first and u < 2):
                    v = (u - 2) % 8
                    n = 8 * p + u - 2
                    V.reciprocal(rinv[:, v % 4], rs[:, v % 4]).then_inc(r_ok, 1)
                    dve.wait_ge(r_ok, n + 1)
                    dve.wait_ge(o_ps, n + 1)
                    if not (first and u < 6):
                        dve.wait_ge(at_ps, (8 * p + u - 2 - v % 2) // 2 - 1)
                    V.tensor_scalar(Arow[:, (v // 2) % 2, 64 * (v % 2):64 * (v % 2) + 64], bank[4 + v % 2][:, 0:HD], rinv[:, v % 4], None, ALU.mult).then_inc(a_ok, 1)
            for p in range(8):
                for u in range(8):
                    step(p, u, FOX if p < 4 else DSW, first=p == 0)
            for u in range(2):
                step(8, u, DSW, last=True)

            hq = lambda a: a.rearrange("p c (h q) -> p c h q", q=DS)
            part = [slice(0, NCH[0]), slice(NCH[0], NALL)]

            def own(k, j):
                at = 32 * k + DS * j
                return bank[4][64 * j:64 * j + 64, :].rearrange("p (c x) -> p c x", x=128)[:, :, at:at + DS]
            def w_lo(c, s):
                dve.wait_ge(wh_ok, c + 1)
                V.tensor_tensor(WS[:, s % 2, 1], WR[:, s], WS[:, s % 2, 0].bitcast(f32), ALU.subtract).then_inc(wl_ok, 1)

            dve.wait_ge(z_init, 9)
            w_lo(0, 0)

            def keysT(b, ch):
                dve.wait_ge(kt_ps, b * NALL + ch + 1)
                V.tensor_copy(KTs[:, ch % 3], bank[TB[ch % 3]][:, :]).then_inc(kt_v, 1)

            def sums_of_logf(b):
                dve.wait_ge(cc_ps, b + 1)
                V.tensor_copy(cneg, bank[5][:, 128:200].rearrange("p (c h) -> p c h", h=H)).then_inc(cc_ok, 1)

            def batch(b, last=False):
                def keys_next(*chs):
                    for ch in chs:
                        if not last:
                            keysT(b + 1, ch)
                dve.wait_ge(cc_ok, b + 1)
                dve.wait_ge(sc_ps, b + 1)
                sc = hq(bank[2][:, 0:NALL * 32].rearrange("p (c n) -> p c n", n=32))
                V.tensor_tensor(hq(S1)[:, part[0]], sc[:, part[0]], cneg.rearrange("p c (h e) -> p c h e", e=1).to_broadcast([128, NCH[0], H, DS]), ALU.add).then_inc(s1_ok, 1)
                V.tensor_tensor(hq(S1)[:, part[1]], sc[:, part[1]], dmask.rearrange("p c (e q) -> p c e q", e=1).to_broadcast([128, NCH[1], H, DS]), ALU.add).then_inc(s1_ok, 1)
                dve.wait_ge(s1_ok, 3 * b + 1)
                V.tensor_tensor(hq(S1)[:, NPG], hq(S1)[:, NPG], fmask.rearrange("p (a q) -> p a q", a=1).to_broadcast([128, H, DS]), ALU.add).then_inc(s1_ok, 1)
                dve.wait_ge(s1_ok, 3 * b + 3)
                for k in range(2):
                    V.reduce_max(mp[:, 32 * k:32 * k + 32], S1[:, part[k]].rearrange("p c n -> p n c"), AX.X).then_inc(mp_ok, 1)
                keys_next(1)
                dve.wait_ge(mt_ps, b + 1)
                if not last:
                    sums_of_logf(b + 1)
                V.reduce_max(mcol[0:64], bank[5][0:64, 0:128], AX.X).then_inc(m_col, 1)
                dve.wait_ge(m_col, b + 1)
                V.tensor_scalar(dg[0:64], ident[0:64, 0:64], mcol[0:64], None, ALU.mult).then_inc(dg_ok, 1)
                dve.wait_ge(mb_ps, b + 1)
                for k in range(2):
                    V.tensor_tensor(S1[:, part[k]], S1[:, part[k]], bank[5][:, 32 * k:32 * k + 32].rearrange("p (a n) -> p a n", a=1).to_broadcast([128, NCH[k], 32]), ALU.subtract).then_inc(sub_ok, 1)
                keys_next(3)
                dve.wait_ge(sp_ok, b + 1)
                for k in range(2):
                    V.reduce_sum(ps_[:, 32 * k:32 * k + 32], S1[:, part[k]].rearrange("p c n -> p n c"), AX.X).then_inc(sum_ok, 1)
                keys_next(5)
                w_lo(2 * b + 1, 1)
                keys_next(7)
                dve.wait_ge(so_ps, 2 * b + 2)
                V.reciprocal(ri[0:64], bank[5][0:64, 0:1]).then_inc(ri_ok, 1)
                dve.wait_ge(ri_ok, b + 1)
                V.tensor_scalar(onr[0:64], bank[4][0:64, :], ri[0:64], None, ALU.mult).then_inc(on_ok, 1)
                dve.wait_ge(ot_ps, b + 1)
                for k in range(2):
                    for j in range(2):
                        V.tensor_copy(AT[64 * j:64 * j + 64, k, :, ds(TP + b * DS, DS)], own(k, j)).then_inc(sat_ok, 1)
                keys_next(9)
                w_lo(2 * b + 2, 0)
                keys_next(11, 13)

            sums_of_logf(0)
            for ch in range(1, NALL, 2):
                keysT(0, ch)
            batch(0)
            with dve.Fori(1, DB - 1) as b:
                batch(b)
            batch(DB - 1, last=True)
            w_lo(17, 1)
            for k in range(2 * NPAIR):
                lo(Ahl[:, 1, k], AT[:, k // NPAIR, k % NPAIR], Ahl[:, 0, k], ah_ok, k + 1, al_ok)

            for m in range(8):
                c0, b0 = 16 + m, 4 * (m % 2)
                dve.wait_ge(prod_ps, 2 * c0 + 2)
                dve.wait_ge(sg_ok, m + 1)
                if m >= 1:
                    dve.wait_ge(mt_ok, m)
                for k in range(2):
                    for hf in range(2):
                        c = slice(hf * HALF, (hf + 1) * HALF)
                        V.tensor_tensor(tg[:, k, c], zg[:, m + 8 * k, c], bank[b0 + 2 * k + hf][:, 0:HALF], ALU.mult).then_inc(tg_ok, 1)
                w_lo(18 + m, (18 + m) % 4)
                dve.wait_ge(tg_ok, 4 * m + 4)
                V.tensor_tensor(tmpM[:, m % 2], tg[:, 0], tg[:, 1], ALU.add).then_inc(mt_ok, 1)
                lo(X2[:, 1, m], tmpM[:, m % 2], X2[:, 0, m], mh_ok, m + 1, m_ok)
            for m in range(8):
                b0 = 2 * (m % 2)
                if m < 6:
                    w_lo(26 + m, (26 + m) % 4)
                dve.wait_ge(prod_ps, 2 * (24 + m) + 2)
                for hf in range(2):
                    c = slice(hf * HALF, (hf + 1) * HALF)
                    i = V.tensor_tensor(xT[:, m, c], xT[:, m, c], bank[b0 + hf][:, 0:HALF], ALU.add)
                i.then_inc(h_ok, 1)
            w_lo(32, 0)
            w_lo(33, 1)
            dve.wait_ge(h_ok, KT)
            scaled(std2_ok, rstd2_ok, u_ok, g2, xT, std2, tmpM, ut_ok, uh_ok)

            def hidden(m, s, last=False):
                b0, c0 = 4 * s, 32 + 2 * m
                dve.wait_ge(sil_ok, 2 * m + 2)
                for hf in range(2):
                    c = slice(hf * HALF, (hf + 1) * HALF)
                    V.tensor_tensor(sg[:, s, c], sg[:, s, c], bank[b0 + hf][:, 0:HALF], ALU.mult).then_inc(gm_ok, 1)
                if not last:
                    w_lo(c0 + 2, (2 * s + 2) % 4)
                dve.wait_ge(gm_ok, 2 * m + 2)
                dve.wait_ge(prod_ps, 2 * c0 + 4)
                for hf in range(2):
                    c = slice(hf * HALF, (hf + 1) * HALF)
                    i = V.tensor_tensor(tmpH[:, c], sg[:, s, c], bank[b0 + 2 + hf][:, 0:HALF], ALU.mult)
                i.then_inc(ht_ok, 1)
                dve.wait_ge(hh_ok, m + 1)
                V.tensor_tensor(Hhl[:, 1, ds(m, 1)].rearrange("p a n -> p (a n)"), tmpH,
                                Hhl[:, 0, ds(m, 1)].rearrange("p a n -> p (a n)").bitcast(f32), ALU.subtract).then_inc(hid_ok, 1)
                dve.wait_ge(hid_ok, m + 1)
                if not last:
                    w_lo(c0 + 3, (2 * s + 3) % 4)
            with dve.Fori(0, KF // 2 - 1) as i:
                for s in range(2):
                    hidden(2 * i + s, s)
            hidden(KF - 2, 0)
            hidden(KF - 1, 1, last=True)
            d_lo = lambda n: lo(WSD[:, n % 2, 1], WDr[:, n % 2].rearrange("p k n -> p (k n)"), WSD[:, n % 2, 0], dh_ok, n + 1, dl_ok)
            d_lo(0)
            d_lo(1)
            for m in range(8):
                for n in (2 * m + 2, 2 * m + 3):
                    if n < 16:
                        d_lo(n)
                dve.wait_ge(d_ps, 2 * m + 2)
                if m >= 2:
                    dve.wait_ge(yt_ps, m - 1)
                for hf in range(2):
                    c = slice(hf * HALF, (hf + 1) * HALF)
                    i = V.tensor_tensor(yT[:, m % 2, c], xT[:, m, c], bank[2 * (m % 2) + hf][:, 0:HALF], ALU.add)
                i.then_inc(y_ok, 1)

        @block.tensor
        def _(pe):
            mm = nc.tensor.matmul

            def halves(banks, w, src, ks, done, first=True, last=True):
                for hf in range(2):
                    for n, (a, b) in enumerate(PASSES):
                        for e, k in enumerate(ks):
                            x = mm(banks[hf][:, 0:HALF], w(a, e), src[:, b, k, hf * HALF:(hf + 1) * HALF],
                                   start=(first and n == 0 and e == 0), stop=(last and n == 2 and e == len(ks) - 1))
                    if done is not None:
                        x.then_inc(done, 1)
                return x

            pe.wait_ge(c_in, 16 * N_CONST)
            pe.wait_ge(x_in, 32)
            for k in range(KT):
                if k >= 2:
                    pe.wait_ge(xT_sb, k - 1)
                for t in range(4):
                    nc.tensor.transpose(bank[2 * (k % 2)][:, t * 128:(t + 1) * 128], xrow[:, t, k * 128:(k + 1) * 128], ident)
                nc.tensor.transpose(bank[2 * (k % 2) + 1][:, 0:TS], xrow[0:TS, 4, k * 128:(k + 1) * 128], ident[0:TS, 0:TS]).then_inc(xT_ps, 1)

            def mean_square(ok, used, src):
                for k in range(KT):
                    pe.wait_ge(ok, k + 1)
                    for hf in range(2):
                        i = mm(bank[6 + hf][:, 0:HALF], mean1, src[:, k % 2, hf * HALF:(hf + 1) * HALF], start=(k == 0), stop=(k == KT - 1))
                    i.then_inc(used, 1)
            mean_square(sq_ok, sq_used, sq)
            tile = [slice(t * 128, t * 128 + 128) for t in range(4)] + [slice(T - 128, T)]
            pe.wait_ge(xn_ok, KT)
            pe.wait_ge(wfl_ok, 1)
            for t in range(5):
                for n, (a, b) in enumerate(PASSES):
                    for k in range(KT):
                        i = mm(bank[5][:, 8 * t:8 * t + 8], X2[:, a, k, tile[t]], wfs[:, b, k, :], start=(n == 0 and k == 0), stop=(n == 2 and k == KT - 1))
            i.then_inc(f_ps, 1)

            def qkv(blk, first):
                for kh in range(2):
                    pe.wait_ge(wql_ok, 2 * blk + kh + 1)
                    for t in range(5):
                        if not first and kh == 0:
                            pe.wait_ge(z_used, 5 * blk + t - 4)
                        for n, (a, b) in enumerate(PASSES):
                            for k in range(4):
                                x = mm(bank[t][:, :], X2[:, a, 4 * kh + k, tile[t]], WQs[:, kh, b, k, :],
                                       start=(kh == 0 and n == 0 and k == 0), stop=(kh == 1 and n == 2 and k == 3))
                        x.then_inc(z_ps, 1)
            qkv(0, True)
            with pe.Fori(1, 6) as blk:
                qkv(blk, False)
            pe.wait_ge(lf_ok, 3)
            for j in range(4):
                i = mm(bank[6][0:8, :], lfx[:, j, :], ntri[:, 384 - 128 * j:896 - 128 * j], start=(j == 0), stop=(j == 3))
            i.then_inc(cT_ps, 1)
            for u in range(16):
                blk, c = u // 4, u % 4
                b0 = 2 * (u % 3)
                if c == 0:
                    pe.wait_ge(row_ok, 5 * blk + 5)
                if u == 0:
                    pe.wait_ge(z_used, 30)
                if u >= 3:
                    pe.wait_ge(tr_v if u % 2 == 0 else tr_a, (u - 3) // 2 + 1)
                for t in range(4):
                    nc.tensor.transpose(bank[b0][:, t * 128:(t + 1) * 128], rows[:, blk, t, c * 128:(c + 1) * 128], ident)
                nc.tensor.transpose(bank[b0 + 1][:, 0:TS], rows[0:TS, blk, 4, c * 128:(c + 1) * 128], ident[0:TS, 0:TS]).then_inc(tr_ps, 1)
            pe.wait_ge(cT_sb, 1)
            for h in range(H):
                if h >= 2:
                    pe.wait_ge(cb_sb, h - 1)
                mm(bank[6 + h % 2][:, :], sel[0:8, h, :], negcT[0:8], start=True, stop=True).then_inc(cb_ps, 1)
            pe.wait_ge(tr_a, 8)
            pe.wait_ge(tr_v, 8)
            pe.wait_ge(cb_sb, 8)

            def step(p, u, first=False, last=False):
                if not last:
                    i, j = u // 2, u % 2
                    N = 128 * (i + 1)
                    n = 8 * p + u
                    if not (first and u < 2):
                        pe.wait_ge(s_nm, n - 1)
                    mm(bank[u % 2][:, 0:N], qkT[64 * j:64 * j + 64, 8 + p, i * 128:(i + 1) * 128], qkT[64 * j:64 * j + 64, p, 0:N],
                       start=True, stop=True).then_inc(s_ps, 1)
                if not (first and u < 1) and not (last and u > 0):
                    v = (u - 1) % 8
                    n = 8 * p + u - 1
                    pe.wait_ge(p_ok, n + 1)
                    if not (first and u < 3):
                        e = (8 * p + u - 1 - v % 2) // 2
                        pe.wait_ge(pt_v if v % 2 else pt_a, e)
                    for c in range(v // 2 + 1):
                        x = nc.tensor.transpose(bank[2 + v % 2][:, c * 128:(c + 1) * 128], PP[:, v % 2, c * 128:(c + 1) * 128], ident)
                    x.then_inc(pt_ps, 1)
                if not (first and u < 2):
                    v = (u - 2) % 8
                    n = 8 * p + u - 2
                    e = (8 * p + u - 2 - v % 2) // 2
                    pe.wait_ge(pt_v if v % 2 else pt_a, e + 1)
                    if not (first and u < 4):
                        pe.wait_ge(a_ok, n - 1)
                    hcol = (2 * p + (v % 2)) * HD if u >= 2 else (2 * (p - 1) + (v % 2)) * HD
                    for c in range(v // 2 + 1):
                        x = mm(bank[4 + v % 2][:, 0:HD], PTs[:, v % 2, c * 128:(c + 1) * 128], vrows[:, c, hcol:hcol + HD], start=(c == 0), stop=(c == v // 2))
                    x.then_inc(o_ps, 1)
                if (u - 3) % 2 == 1 and not (first and u < 4):
                    block_out(p if u >= 4 else p - 1, ((u - 3) % 8) // 2, first)

            def block_out(p, i, first=False):
                pe.wait_ge(a_ok, 8 * p + 2 * i + 2)
                if not (first and i < 2):
                    pe.wait_ge(at_ok, 4 * p + i - 1)
                nc.tensor.transpose(bank[6 + i % 2][:, 0:128], Arow[:, i % 2, :], ident).then_inc(at_ps, 1)
            for p in range(8):
                for u in range(8):
                    step(p, u, first=p == 0)
            for u in range(2):
                step(8, u, last=True)
            block_out(7, 3)

            pe.wait_ge(at_ok, 32)
            pe.wait_ge(z_init, 9)
            pe.wait_ge(Qs_ok, 4)

            def keys_T(b, ch, first):
                if ch >= 3:
                    if ch % 2:
                        pe.wait_ge(kt_a, 8 * b + (ch - 3) // 2 + 1)
                    else:
                        pe.wait_ge(kt_v, 7 * b + (ch - 3) // 2 + 1)
                elif not first:
                    pe.wait_ge(kt_v if ch == 1 else kt_a, (8 * b - 1, 7 * b, 8 * b)[ch])
                pe.wait_ge(k_in[key_slot(ch)], 16 * (NCH[0] // NKF * b + ch // NKF if ch < NCH[0] else b) + 16)
                for c in range(NPAIR):
                    x = nc.tensor.transpose(bank[TB[ch % 3]][:, c * 128:(c + 1) * 128], key_rows(ch)[:, c * 128:(c + 1) * 128], ident)
                x.then_inc(kt_ps, 1)

            def scores(b, ch):
                pe.wait_ge(kt_v if ch % 2 else kt_a, (7 if ch % 2 else 8) * b + ch // 2 + 1)
                k = 0 if ch < NCH[0] else 1
                for c in range(NPAIR):
                    x = mm(bank[2][:, ch * 32 + c * 8:ch * 32 + c * 8 + 8], KTs[:, ch % 3, c * 128:(c + 1) * 128],
                           Qs[:, k, ds(b, 1), c].rearrange("p a j q -> p (a j q)"), start=True, stop=True)
                return x

            def gate_wait(b, s, hf, first):
                if hf == 0:
                    pe.wait_ge(wl_ok, 2 * b + s + 1)
                if not (first and s == 0):
                    pe.wait_ge(g_ok, 4 * b + 2 * s + hf - 1)

            def gate(s, n):
                hf, p, k = n // 24, n // 8 % 3, n % 8
                a, b = PASSES[p]
                x = mm(bank[6 + hf][:, 0:HALF], WS[:, s, a, k * 128:(k + 1) * 128], X2[:, b, k, hf * HALF:(hf + 1) * HALF], start=(n % 24 == 0), stop=(n % 24 == 23))
                if n % 24 == 23:
                    x.then_inc(prod_ps, 1)

            def gates(b, n0, n1, first):
                for n in range(n0, n1):
                    if n % 24 == 0:
                        gate_wait(b, n // 48, n // 24 % 2, first)
                    gate(n // 48, n % 48)

            def sums_of_logf(b, first=False):
                pe.wait_ge(l_in, 16 * 9 * (b + 1))
                if not first:
                    pe.wait_ge(cc_ok, b)
                mm(bank[5][:, 128:200], ntri[:, 384:512], lfp.rearrange("p c h -> p (c h)"), start=True, stop=False)
                for c in range(NPG):
                    x = mm(bank[5][:, 128 + 8 * (c + 1):200].rearrange("p (c h) -> p c h", h=H), ntri[:, 768:896],
                           lfp[:, c:c + 1, :].to_broadcast([128, NPG - c, H]), start=False, stop=(c == NPG - 1))
                x.then_inc(cc_ps, 1)

            def outputs(b, first):
                pe.wait_ge(sum_ok, 2 * b + 2)
                if not first:
                    pe.wait_ge(sat_ok, 4 * b)
                mm(bank[5][0:64, 0:1], ps_, ones[:, 0:1], start=True, stop=True)
                for k in range(2):
                    pe.wait_ge((vf_in, vd_in)[k], 16 * NCH[k] * (b + 1))
                    for ch in range(NCH[k]):
                        x = mm(bank[4][32 * k:32 * k + 32, :], S1[:, ch + k * NCH[0]], (Vf, Vd)[k][:, ch, :], start=(ch == 0), stop=(ch == NCH[k] - 1))
                    x.then_inc(so_ps, 1)

            def batch(b, first=False, last=False):
                if not last:
                    sums_of_logf(b + 1)
                    keys_T(b + 1, 0, False)
                    keys_T(b + 1, 1, False)
                gates(b, 0, 16, first)
                pe.wait_ge(mp_ok, 2 * b + 2)
                nc.tensor.transpose(bank[5][:, 0:128], mp, ident).then_inc(mt_ps, 1)
                gates(b, 16, 24, first)
                pe.wait_ge(dg_ok, b + 1)
                mm(bank[5][:, 0:64], ones[0:64], dg[0:64], start=True, stop=True).then_inc(mb_ps, 1)
                for ch in range(NALL):
                    if not last and ch + 2 < NALL:
                        keys_T(b + 1, ch + 2, False)
                    if ch < 7:
                        gates(b, 24 + 2 * ch, 26 + 2 * ch, first)
                    else:
                        gates(b, 64 + 4 * (ch - 7), 68 + 4 * (ch - 7), first)
                    if not last:
                        x = scores(b + 1, ch)
                    if ch == 6:
                        outputs(b, first)
                        gates(b, 38, 52, first)
                        pe.wait_ge(on_ok, b + 1)
                        for c in range(NPAIR):
                            x = nc.tensor.transpose(bank[4][:, c * 120:c * 120 + 128], onr[:, c * 128:(c + 1) * 128], ident)
                        x.then_inc(ot_ps, 1)
                        gates(b, 52, 64, first)
                if not last:
                    x.then_inc(sc_ps, 1)
            sums_of_logf(0, True)
            keys_T(0, 0, True)
            keys_T(0, 1, True)
            for ch in range(NALL):
                if ch + 2 < NALL:
                    keys_T(0, ch + 2, True)
                x = scores(0, ch)
            x.then_inc(sc_ps, 1)
            batch(0, first=True)
            with pe.Fori(1, DB - 1) as b:
                batch(b)
            batch(DB - 1, last=True)

            pe.wait_ge(sat_ok, 4 * DB)
            pe.wait_ge(g_ok, 4 * DB)
            pe.wait_ge(al_ok, 2 * NPAIR)

            def merged(m, s, first):
                pe.wait_ge(wl_ok, 16 + m + 1)
                if not first:
                    pe.wait_ge(tg_ok, 4 * m - 4)
                for hf in range(2):
                    for k in range(2):
                        for n, (a, b) in enumerate(PASSES):
                            for e in range(NPAIR):
                                x = mm(bank[4 * s + 2 * k + hf][:, 0:HALF], WS[:, s, a, (4 * k + e) * 128:(4 * k + e + 1) * 128],
                                       Ahl[:, b, 4 * k + e, hf * HALF:(hf + 1) * HALF], start=(n == 0 and e == 0), stop=(n == 2 and e == NPAIR - 1))
                    x.then_inc(prod_ps, 1)
            for m in range(2):
                merged(m, m, True)
            with pe.Fori(1, 4) as i:
                for s in range(2):
                    merged(2 * i + s, s, False)
            pe.wait_ge(m_ok, 8)
            ring_w = lambda s: (lambda a, k: WS[:, s, a, k * 128:(k + 1) * 128])

            def out_proj(m, s, first):
                pe.wait_ge(wl_ok, 24 + m + 1)
                if not first:
                    pe.wait_ge(h_ok, m - 1)
                halves(bank[2 * s:2 * s + 2], ring_w(s), X2, range(KT), prod_ps)
            for m in range(2):
                out_proj(m, m, True)
            with pe.Fori(1, 4) as i:
                for s in range(2):
                    out_proj(2 * i + s, s, False)
            mean_square(sq2_ok, sq2_used, sq2)

            pe.wait_ge(u_ok, KT)
            def up(m, s, first):
                if not first:
                    pe.wait_ge(ht_ok, m - 1)
                for k in range(2):
                    pe.wait_ge(wl_ok, 32 + 2 * m + k + 1)
                    halves(bank[4 * s + 2 * k:4 * s + 2 * k + 2], ring_w(k), X2, range(KT), prod_ps)
            for m in range(2):
                up(m, m, True)
            with pe.Fori(1, KF // 2) as i:
                for s in range(2):
                    up(2 * i + s, s, False)
            pe.wait_ge(hid_ok, KF)

            def y_out(m):
                pe.wait_ge(y_ok, m + 1)
                if m >= 2:
                    pe.wait_ge(yst_ok, m - 1)
                b0 = 4 + 2 * (m % 2)
                for t in range(4):
                    nc.tensor.transpose(bank[b0][:, t * 128:(t + 1) * 128], yT[:, m % 2, t * 128:(t + 1) * 128], ident)
                nc.tensor.transpose(bank[b0 + 1][0:TS, 0:128], yT[:, m % 2, TP:T], ident).then_inc(yt_ps, 1)
            for m in range(8):
                if m >= 2:
                    pe.wait_ge(y_ok, m - 1)
                for kh in range(2):
                    pe.wait_ge(dl_ok, 2 * m + kh + 1)
                    halves(bank[2 * (m % 2):2 * (m % 2) + 2], lambda a, k: WSD[:, kh, a, k * 128:(k + 1) * 128], Hhl,
                           range(KD * kh, KD * kh + KD), None, first=(kh == 0), last=(kh == 1)).then_inc(d_ps, 1)
                if m >= 1:
                    y_out(m - 1)
            y_out(7)


_INS = ["x_prompt", "x_sample", "cache_k_fox", "cache_v_fox", "cache_logf_fox", "state_k_dsw", "state_v_dsw", "page_table",
        "norm1_g", "w_in", "b_f", "q_norm_fox", "k_norm_fox", "q_norm_dsw", "k_norm_dsw", "w_o_fox", "w_o_dsw", "w_out",
        "norm2_g", "w_gate", "w_up", "w_down"]


def constants():
    import numpy as np
    p = np.arange(128)
    c = np.zeros((128, C_END), np.float32)
    c[:, C_ID:C_ID + 128] = np.eye(128)
    c[:, C_MEAN:C_MEAN + 128] = 1.0 / D
    c[:, C_ONE:C_ONE + 128] = 1.0
    c[:, C_TRI:C_TRI + 128] = np.where(p[None, :] <= p[:, None], 0.0, NEG)
    c[:, C_NTRI:C_NTRI + 896] = np.where(np.arange(896)[None, :] - 384 >= p[:, None], -1.0, 0.0)

    def log_count(dist):
        n = ((dist >= 0) & (dist <= 128)) * 1 + ((dist >= 0) & (dist <= 512) & (dist % 4 == 0)) + ((dist >= 0) & (dist <= 2048) & (dist % 16 == 0))
        return np.where(n > 0, np.log(np.maximum(n, 1)), NEG)
    for s in range(4):
        c[:, C_LC + 128 * s:C_LC + 128 * (s + 1)] = log_count(128 * (3 - s) + p[:, None] - p[None, :])
    half = HD // 2
    inv = np.float32(10000.0) ** (-np.arange(half, dtype=np.float32) / np.float32(half))
    for t in range(5):
        pos = (128 * t + p) if t < 4 else PAST + p % DS
        ang = pos.astype(np.float32)[:, None] * inv.astype(np.float32)[None, :]
        co, si = np.cos(ang), np.sin(ang)
        c[:, C_COS + 64 * t:C_COS + 64 * t + 64] = np.concatenate([co, co], 1)
        c[:, C_SIN + 64 * t:C_SIN + 64 * t + 64] = np.concatenate([-si, si], 1)
    for ch in range(6):
        key = 512 + 128 * ch + p if ch < 4 else 16 * (p // 4) + p % 4 if ch == 4 else PAST + p
        for q in range(DS):
            v = log_count(PAST + q - key)
            c[:, C_DM + 4 * ch + q] = np.where(p < DS, v, NEG) if ch == 5 else v
    for q in range(DS):
        c[:, C_FM + q] = np.where((p < DS) & (p <= q), 0.0, NEG)
    s = np.zeros((8, 8, 128), np.float32)
    for h in range(8):
        s[h, h, :] = 1.0
    return c, s.reshape(8, 1024)


def kernel(**inputs):
    import numpy as np
    import concourse.bacc as bacc
    from concourse.bass_utils import run_bass_kernel_spmd
    nc = bacc.Bacc("TRN2", target_bir_lowering=False, num_devices=1)
    arrays, args = {}, []
    cpack, selin = constants()
    for name, a in [(n, inputs[n]) for n in _INS] + [("cpack", cpack), ("selin", selin)]:
        a = np.ascontiguousarray(a)
        arrays["in_" + name] = a
        args.append(nc.dram_tensor("in_" + name, a.shape, mybir.dt.from_np(a.dtype), kind="ExternalInput").ap())
    L = 1
    outs = [(1, TP, D), (DB, DS, D), (L, 1, TP, H, HD), (L, 1, TP, H, HD), (L, 1, TP, H), (L, 1, TP, H, HD), (L, 1, TP, H, HD),
            (L, DB, DS, H, HD), (L, DB, DS, H, HD), (L, DB, DS, H), (L, DB, PAST, H, HD), (L, DB, PAST, H, HD)]
    for i, shape in enumerate(outs):
        args.append(nc.dram_tensor(f"out_{i}", shape, mybir.dt.float32, kind="ExternalOutput").ap())
    program(nc, *args)
    r = run_bass_kernel_spmd(nc, [arrays], core_ids=[0])
    return tuple(r.results[0][f"out_{i}"] for i in range(len(outs)))
```
